# Optimizing a Trainium2 kernel written in Bass

```python
import math
import jax, jax.numpy as jnp
from jax import lax
import numpy as np

D_MODEL = 1024
BATCH = 1
SEQ = 1024
DEPTH = 2

GRID_W = 64
CTX_LEN = 256
D_MIX = 2 * D_MODEL

SSD_HEADS = 16
SSD_HEAD_DIM = 64
SSD_WIDTH = SSD_HEADS * SSD_HEAD_DIM
SSD_GROUPS = 4
SSD_HPG = SSD_HEADS // SSD_GROUPS
SSD_STATE = 128
SSD_GN = SSD_GROUPS * SSD_STATE
SSD_XBC = SSD_WIDTH + 2 * SSD_GN
SSD_DT = 2 * SSD_HEADS
SSD_CHUNK = 128
SHORT_CONV = 3

DIFF_HEADS = 4
DIFF_DIM = 64
DIFF_WIDTH = DIFF_HEADS * 2 * DIFF_DIM
DIFF_SCALE = DIFF_DIM ** -0.5
Q_BLOCK = 128
ROPE_BASE = 10000.0
ROPE_FREQS = DIFF_DIM // 4

HY_WIDTH = D_MIX - SSD_WIDTH - DIFF_WIDTH
HY_ORDER = 2
HY_BANDS = 16
HY_EMB = 1 + 2 * HY_BANDS
HY_HIDDEN = 64
HY_DECAY_FAST = 0.3
HY_DECAY_SLOW = 1.5
HY_DECAY_TARGET = 1e-2
HY_MIN_DECAY = math.log(HY_DECAY_TARGET) / HY_DECAY_SLOW
HY_MAX_DECAY = math.log(HY_DECAY_TARGET) / HY_DECAY_FAST

IN_SIZES = (SSD_WIDTH, SSD_XBC, SSD_DT, DIFF_WIDTH, DIFF_WIDTH, DIFF_WIDTH, DIFF_WIDTH, 3 * HY_WIDTH, HY_WIDTH)
IN_SPLITS = tuple(int(s) for s in np.cumsum(IN_SIZES)[:-1])
N_IN = sum(IN_SIZES)

ALPHA = (2 * DEPTH) ** 0.25
BETA = (8 * DEPTH) ** -0.25
LN_EPS = 1e-5
RMS_EPS = 1e-6
F32 = jnp.float32

kernel_name = "hybrid_ssd_diffattn_hyena_dit"

def _layer_norm(x):
    xf = x.astype(F32)
    xc = xf - jnp.mean(xf, -1, keepdims=True)
    var = jnp.mean(xc * xc, -1, keepdims=True)
    return (xc * lax.rsqrt(var + LN_EPS)).astype(x.dtype)

def _rms_norm(x):
    xf = x.astype(F32)
    return (xf * lax.rsqrt(jnp.mean(xf * xf, -1, keepdims=True) + RMS_EPS)).astype(x.dtype)

def _centred_dwconv(u, w, b):
    pad = w.shape[0] // 2
    y = lax.conv_general_dilated(u, w[:, None, :].astype(u.dtype), (1,), [(pad, pad)],
                                 dimension_numbers=('NWC', 'WIO', 'NWC'),
                                 feature_group_count=u.shape[-1])
    return y + b

def _axial_rope_tables(L, dtype):
    rows = L // GRID_W
    row = jnp.repeat(jnp.arange(rows), GRID_W).astype(F32)
    col = jnp.tile(jnp.arange(GRID_W), rows).astype(F32)
    inv = ROPE_BASE ** (-jnp.arange(ROPE_FREQS, dtype=F32) / ROPE_FREQS)
    ar = row[:, None] * inv
    ac = col[:, None] * inv
    shp = (L, 1, 1, ROPE_FREQS)
    return (jnp.cos(ar).reshape(shp).astype(dtype), jnp.sin(ar).reshape(shp).astype(dtype),
            jnp.cos(ac).reshape(shp).astype(dtype), jnp.sin(ac).reshape(shp).astype(dtype))

def _rot_half(x, cos, sin):
    x1, x2 = jnp.split(x, 2, axis=-1)
    return jnp.concatenate([x1 * cos - x2 * sin, x2 * cos + x1 * sin], -1)

def _apply_axial_rope(x, rope):
    cr, sr, cc, sc = rope
    x_row, x_col = jnp.split(x, 2, axis=-1)
    return jnp.concatenate([_rot_half(x_row, cr, sr), _rot_half(x_col, cc, sc)], -1)

def _ssd_chunked(x, dt, a, bm, cm, h0):
    b, L, g, r, p = x.shape
    n = bm.shape[-1]
    q = SSD_CHUNK
    nc = L // q
    xc = x.reshape(b, nc, q, g, r, p)
    dtc = dt.reshape(b, nc, q, g, r).astype(F32)
    bc = bm.reshape(b, nc, q, g, n)
    cc = cm.reshape(b, nc, q, g, n)
    la = jnp.cumsum(dtc * a, axis=2)
    seg = la[:, :, :, None] - la[:, :, None, :]
    tri = jnp.tril(jnp.ones((q, q), bool))[:, :, None, None]
    decay = jnp.exp(jnp.where(tri, seg, -jnp.inf))
    cb = jnp.einsum('bclgn,bcsgn->bclsg', cc, bc).astype(F32)
    w = cb[..., None] * decay * dtc[:, :, None]
    y_diag = jnp.einsum('bclsgr,bcsgrp->bclgrp', w.astype(x.dtype), xc)
    to_end = jnp.exp(la[:, :, -1:] - la) * dtc
    states = jnp.einsum('bcsgn,bcsgr,bcsgrp->bcgrpn', bc, to_end.astype(x.dtype), xc)
    chunk_decay = jnp.exp(la[:, :, -1])

    def step(h, inp):
        dec, st = inp
        return h * dec[..., None, None] + st, h

    h_final, h_start = lax.scan(step, h0.astype(F32),
                                (jnp.moveaxis(chunk_decay, 1, 0), jnp.moveaxis(states, 1, 0).astype(F32)))
    h_start = jnp.moveaxis(h_start, 0, 1)
    y_off = jnp.einsum('bclgn,bcgrpn->bclgrp', cc, h_start.astype(x.dtype)) * jnp.exp(la)[..., None].astype(x.dtype)
    return (y_diag + y_off).reshape(b, L, g, r, p), h_final

def _ssd_prepare(xbc, dt_raw, conv_w, conv_b, dt_bias):
    B, L = xbc.shape[:2]
    xbc = jax.nn.silu(_centred_dwconv(xbc, conv_w, conv_b))
    xs, bm, cm = jnp.split(xbc, [SSD_WIDTH, SSD_WIDTH + SSD_GN], axis=-1)
    xs = xs.reshape(B, L, SSD_GROUPS, SSD_HPG, SSD_HEAD_DIM)
    bm = bm.reshape(B, L, SSD_GROUPS, SSD_STATE)
    cm = cm.reshape(B, L, SSD_GROUPS, SSD_STATE)
    dt = jax.nn.softplus(dt_raw.reshape(B, L, 2, SSD_HEADS).astype(F32) + dt_bias.astype(F32))
    dt = dt.reshape(B, L, 2, SSD_GROUPS, SSD_HPG)
    return xs, bm, cm, dt

def _ssd_bidir(lat, ctx, a_log, d_skip, need_ctx):
    xs, bm, cm, dt = lat
    xsc, bmc, cmc, dtc = ctx
    B = xs.shape[0]
    a = -jnp.exp(a_log.astype(F32)).reshape(2, SSD_GROUPS, SSD_HPG)
    h0 = jnp.zeros((B, SSD_GROUPS, SSD_HPG, SSD_HEAD_DIM, SSD_STATE), F32)
    flip = lambda t: jnp.flip(t, 1)
    yc_f, hc_f = _ssd_chunked(xsc, dtc[:, :, 0], a[0], bmc, cmc, h0)
    y_f, _ = _ssd_chunked(xs, dt[:, :, 0], a[0], bm, cm, hc_f)
    yc_b, hc_b = _ssd_chunked(flip(xsc), flip(dtc[:, :, 1]), a[1], flip(bmc), flip(cmc), h0)
    y_b, _ = _ssd_chunked(flip(xs), flip(dt[:, :, 1]), a[1], flip(bm), flip(cm), hc_b)
    dsk = d_skip.reshape(SSD_GROUPS, SSD_HPG, 1)
    y = y_f + flip(y_b) + dsk * xs
    yc = (yc_f + flip(yc_b) + dsk * xsc) if need_ctx else None
    return y, yc

def _diff_scores(q, k, v, lam):
    s = jnp.einsum('bqhmd,bkhmd->bhmqk', q, k).astype(F32) * DIFF_SCALE
    p = jax.nn.softmax(s, axis=-1)
    attn = p[:, :, 0] - lam * p[:, :, 1]
    return jnp.einsum('bhqk,bkhe->bqhe', attn.astype(v.dtype), v)

def _diff_attention(q, k, v, qc, kc, vc, lam_vecs, layer_idx, rope, need_ctx):
    B, L = q.shape[:2]
    Lc = qc.shape[1]
    shp = (DIFF_HEADS, 2, DIFF_DIM)
    q = _apply_axial_rope(q.reshape(B, L, *shp), rope)
    k = _apply_axial_rope(k.reshape(B, L, *shp), rope)
    v = v.reshape(B, L, DIFF_HEADS, 2 * DIFF_DIM)
    qc = qc.reshape(B, Lc, *shp)
    kc = kc.reshape(B, Lc, *shp)
    vc = vc.reshape(B, Lc, DIFF_HEADS, 2 * DIFF_DIM)
    lv = lam_vecs.astype(F32)
    lam_init = 0.8 - 0.6 * math.exp(-0.3 * layer_idx)
    lam = jnp.exp(jnp.sum(lv[0] * lv[1])) - jnp.exp(jnp.sum(lv[2] * lv[3])) + lam_init
    k_all = jnp.concatenate([kc, k], axis=1)
    v_all = jnp.concatenate([vc, v], axis=1)
    nb = L // Q_BLOCK
    q_blocks = jnp.moveaxis(q.reshape(B, nb, Q_BLOCK, *shp), 1, 0)
    o = lax.map(lambda qb: _diff_scores(qb, k_all, v_all, lam), q_blocks)
    o = jnp.moveaxis(o, 0, 1).reshape(B, L, DIFF_HEADS, 2 * DIFF_DIM)
    out = (_rms_norm(o) * (1.0 - lam_init)).reshape(B, L, DIFF_WIDTH)
    out_c = None
    if need_ctx:
        oc = _diff_scores(qc, kc, vc, lam)
        out_c = (_rms_norm(oc) * (1.0 - lam_init)).reshape(B, Lc, DIFF_WIDTH)
    return out, out_c

def _hyena_kernels_fft(L, filt):
    w1, b1, w2, b2, w3, b3, freq = [t.astype(F32) for t in filt]
    t = jnp.linspace(0.0, 1.0, L, dtype=F32)[:, None]
    wpos = (2.0 * math.pi / L) * jnp.arange(L, dtype=F32)[:, None]
    bands = jnp.linspace(1e-4, HY_BANDS - 1, HY_BANDS, dtype=F32)
    feats = jnp.concatenate([t, jnp.cos(wpos * bands), -jnp.sin(wpos * bands)], -1)
    hdn = jnp.sin(freq * (feats @ w1 + b1))
    hdn = jnp.sin(freq * (hdn @ w2 + b2))
    hf = (hdn @ w3 + b3).reshape(L, 2, HY_ORDER, HY_WIDTH)
    deltas = jnp.abs(jnp.linspace(HY_MIN_DECAY, HY_MAX_DECAY, HY_WIDTH, dtype=F32))
    hf = hf * jnp.exp(-t * deltas)[:, None, None, :]
    kern = jnp.concatenate([hf[:, 0], jnp.zeros((1, HY_ORDER, HY_WIDTH), F32), jnp.flip(hf[1:, 1], 0)], 0)
    kern = kern * lax.rsqrt(jnp.sum(kern * kern, 0, keepdims=True) + RMS_EPS)
    return jnp.fft.rfft(kern, axis=0)

def _fft_long_conv(u, kf, bias):
    L = u.shape[1]
    uf = jnp.fft.rfft(u.astype(F32), n=2 * L, axis=1)
    y = jnp.fft.irfft(uf * kf, n=2 * L, axis=1)[:, :L]
    return (y + bias.astype(F32) * u.astype(F32)).astype(u.dtype)

def _hyena(proj, conv_w, conv_b, filt, bias):
    L = proj.shape[1]
    v, x1, x2 = jnp.split(_centred_dwconv(proj, conv_w, conv_b), 3, axis=-1)
    kf = _hyena_kernels_fft(L, filt)
    z = x1 * _fft_long_conv(v, kf[:, 0], bias[0])
    return x2 * _fft_long_conv(z, kf[:, 1], bias[1])

def _trunk_layer(h, hc, mod, mod_c, w_in, ssd_conv_w, ssd_conv_b, dt_bias, a_log, d_skip, ssd_norm_w,
                 lam_vecs, hy_conv_w, hy_conv_b, hy_filt, hy_bias, w_out, ln_g, ln_b,
                 layer_idx, rope, need_ctx):
    B, L = h.shape[:2]
    Lc = hc.shape[1]
    shift, scale, gate = jnp.split(mod[:, None, :], 3, axis=-1)
    shift_c, scale_c, gate_c = jnp.split(mod_c, 3, axis=-1)
    u = _layer_norm(h) * (1.0 + scale) + shift
    uc = _layer_norm(hc) * (1.0 + scale_c) + shift_c
    z, xbc, dtr, q, k, v, gd, hp, gh = jnp.split(u @ w_in, IN_SPLITS, axis=-1)
    zc, xbcc, dtrc, qc, kc, vc, gdc, hpc, ghc = jnp.split(uc @ w_in, IN_SPLITS, axis=-1)

    ssd_lat = _ssd_prepare(xbc, dtr, ssd_conv_w, ssd_conv_b, dt_bias)
    ssd_ctx = _ssd_prepare(xbcc, dtrc, ssd_conv_w, ssd_conv_b, dt_bias)
    y_ssd, yc_ssd = _ssd_bidir(ssd_lat, ssd_ctx, a_log, d_skip, need_ctx)
    o_ssd = _rms_norm(y_ssd.reshape(B, L, SSD_WIDTH) * jax.nn.silu(z)) * ssd_norm_w
    o_diff, oc_diff = _diff_attention(q, k, v, qc, kc, vc, lam_vecs, layer_idx, rope, need_ctx)
    o_diff = o_diff * jax.nn.silu(gd)
    o_hy = _hyena(hp, hy_conv_w, hy_conv_b, hy_filt, hy_bias) * jax.nn.silu(gh)
    o = jnp.concatenate([o_ssd, o_diff, o_hy], axis=-1) @ w_out
    h_new = _layer_norm(ALPHA * h + gate * o) * ln_g + ln_b
    if not need_ctx:
        return h_new, None
    oc_ssd = _rms_norm(yc_ssd.reshape(B, Lc, SSD_WIDTH) * jax.nn.silu(zc)) * ssd_norm_w
    oc_diff = oc_diff * jax.nn.silu(gdc)
    oc_hy = _hyena(hpc, hy_conv_w, hy_conv_b, hy_filt, hy_bias) * jax.nn.silu(ghc)
    oc = jnp.concatenate([oc_ssd, oc_diff, oc_hy], axis=-1) @ w_out
    hc_new = _layer_norm(ALPHA * hc + gate_c * oc) * ln_g + ln_b
    return h_new, hc_new

def setup_inputs(seed: int = 0) -> dict:
    key = jax.random.key(seed)
    ks = jax.random.split(key, 32)
    nrm = lambda kk, shape, s: jax.random.normal(kk, shape, F32) * s
    dt0 = jnp.exp(jax.random.uniform(ks[9], (DEPTH, 2, SSD_HEADS), F32, math.log(1e-3), math.log(1e-1)))
    return {
        "x": nrm(ks[0], (BATCH, SEQ, D_MODEL), 1.0),
        "c": nrm(ks[1], (BATCH, D_MODEL), 1.0),
        "ctx": nrm(ks[2], (BATCH, CTX_LEN, D_MODEL), 1.0),
        "c_ctx": nrm(ks[3], (D_MODEL,), 1.0),
        "w_ada": nrm(ks[4], (DEPTH, D_MODEL, 3 * D_MODEL), 0.5 * D_MODEL ** -0.5),
        "b_ada": nrm(ks[5], (DEPTH, 3 * D_MODEL), 0.02),
        "w_in": nrm(ks[6], (DEPTH, D_MODEL, N_IN), D_MODEL ** -0.5),
        "ssd_conv_w": nrm(ks[7], (DEPTH, SHORT_CONV, SSD_XBC), SHORT_CONV ** -0.5),
        "ssd_conv_b": nrm(ks[8], (DEPTH, SSD_XBC), 0.02),
        "ssd_dt_bias": dt0 + jnp.log(-jnp.expm1(-dt0)),
        "ssd_a_log": jnp.log(jax.random.uniform(ks[10], (DEPTH, 2, SSD_HEADS), F32, 1.0, 16.0)),
        "ssd_d": 1.0 + nrm(ks[11], (DEPTH, SSD_HEADS), 0.1),
        "ssd_norm_w": 1.0 + nrm(ks[12], (DEPTH, SSD_WIDTH), 0.02),
        "diff_lambda": nrm(ks[13], (DEPTH, 4, DIFF_DIM), 0.1),
        "hy_conv_w": nrm(ks[14], (DEPTH, SHORT_CONV, 3 * HY_WIDTH), SHORT_CONV ** -0.5),
        "hy_conv_b": nrm(ks[15], (DEPTH, 3 * HY_WIDTH), 0.02),
        "hy_w1": nrm(ks[16], (DEPTH, HY_EMB, HY_HIDDEN), HY_EMB ** -0.5),
        "hy_b1": nrm(ks[17], (DEPTH, HY_HIDDEN), 0.1),
        "hy_w2": nrm(ks[18], (DEPTH, HY_HIDDEN, HY_HIDDEN), HY_HIDDEN ** -0.5),
        "hy_b2": nrm(ks[19], (DEPTH, HY_HIDDEN), 0.1),
        "hy_w3": nrm(ks[20], (DEPTH, HY_HIDDEN, 2 * HY_ORDER * HY_WIDTH), HY_HIDDEN ** -0.5),
        "hy_b3": nrm(ks[21], (DEPTH, 2 * HY_ORDER * HY_WIDTH), 0.02),
        "hy_freq": 1.0 + nrm(ks[22], (DEPTH, HY_HIDDEN), 0.1),
        "hy_bias": nrm(ks[23], (DEPTH, HY_ORDER, HY_WIDTH), 0.5),
        "w_out": nrm(ks[24], (DEPTH, D_MIX, D_MODEL), BETA * D_MIX ** -0.5),
        "ln_g": 1.0 + nrm(ks[25], (DEPTH, D_MODEL), 0.02),
        "ln_b": nrm(ks[26], (DEPTH, D_MODEL), 0.02),
    }

def reference(x, c, ctx, c_ctx, w_ada, b_ada, w_in, ssd_conv_w, ssd_conv_b, ssd_dt_bias, ssd_a_log, ssd_d,
              ssd_norm_w, diff_lambda, hy_conv_w, hy_conv_b, hy_w1, hy_b1, hy_w2, hy_b2, hy_w3, hy_b3,
              hy_freq, hy_bias, w_out, ln_g, ln_b):
    h, hc = x, ctx
    rope = _axial_rope_tables(x.shape[1], x.dtype)
    sc = jax.nn.silu(c)
    scc = jax.nn.silu(c_ctx)
    for l in range(DEPTH):
        mod = sc @ w_ada[l] + b_ada[l]
        mod_c = scc @ w_ada[l] + b_ada[l]
        hy_filt = (hy_w1[l], hy_b1[l], hy_w2[l], hy_b2[l], hy_w3[l], hy_b3[l], hy_freq[l])
        h, hc = _trunk_layer(h, hc, mod, mod_c, w_in[l], ssd_conv_w[l], ssd_conv_b[l], ssd_dt_bias[l],
                             ssd_a_log[l], ssd_d[l], ssd_norm_w[l], diff_lambda[l], hy_conv_w[l],
                             hy_conv_b[l], hy_filt, hy_bias[l], w_out[l], ln_g[l], ln_b[l],
                             l, rope, l < DEPTH - 1)
    return h


_drawn_inputs = setup_inputs


def setup_inputs(seed=0):
    import zlib

    import numpy as np

    out = dict(_drawn_inputs(seed))
    spreads = {}
    factors = {'ctx': 8.0,
     'c_ctx': 5.565,
     'ssd_conv_b': 8.0,
     'ssd_d': 8.0,
     'ssd_norm_w': 8.0,
     'diff_lambda': 8.0,
     'hy_conv_b': 2.674}
    for name, (base, spread) in spreads.items():
        noise = np.random.default_rng([zlib.crc32(name.encode()), seed]).standard_normal(out[name].shape)
        drawn = base * np.exp(spread * noise) if base else spread * noise
        out[name] = __import__('jax').numpy.asarray(drawn.astype(out[name].dtype))
    for name, factor in factors.items():
        out[name] = (out[name] * factor).astype(out[name].dtype)
    return out
```

```python
import math
from contextlib import ExitStack, contextmanager

import numpy as np

import concourse.bass as bass
from concourse import mybir

F32 = mybir.dt.float32
ACT = mybir.ActivationFunctionType
ALU = mybir.AluOpType
AX = mybir.AxisListType

P = 128
D = 1024
KD = D // P
LAT, CTX = 1024, 256
T = CTX + LAT
TT = T // P
CT = CTX // P
DEPTH = 2
GRID_W = 64
HEADS, HD = 16, 64
GROUPS, HPG, NS = 4, 4, 128
AH, AD = 4, 64
HYW = 512
ORDER = 2
BANDS, EMB, HID = 16, 33, 64
D_MIX = 2048
KM = D_MIX // P
SSD_TILES = HEADS * HD // P
SCALE = AD ** -0.5
ALPHA = (2 * DEPTH) ** 0.25
LN_EPS, RMS_EPS = 1e-5, 1e-6
BANK = 512
GW = 512
SIN_RANGE = 1.5 * 2.0 ** 23

Z0, XBC0, DT0, Q0, K0, V0, GD0, HP0, GH0, N_IN = 0, 1024, 3072, 3104, 3616, 4128, 4640, 5152, 6688, 7200


def lam_init(layer):
    return 0.8 - 0.6 * math.exp(-0.3 * layer)


def rope_tables():
    freqs = AD // 4
    inv = 10000.0 ** (-np.arange(freqs) / freqs)
    tok = np.arange(LAT)
    row, col = tok // GRID_W, tok % GRID_W
    f = np.arange(P)
    pos = np.where((f % AD < AD // 2)[:, None], row[None], col[None])
    ang = pos * inv[f % freqs][:, None]
    sign = np.where(f % 32 < 16, -1.0, 1.0)[:, None]
    return np.cos(ang).astype(np.float32), (sign * np.sin(ang)).astype(np.float32)


def swap_matrix():
    f = np.arange(P)
    return (f[:, None] == (f[None] ^ 16)).astype(np.float32)


def triangles():
    s, l = np.arange(P)[:, None], np.arange(P)[None]
    return np.stack([s <= l, s >= l, s >= 0 * l], 1).astype(np.float32)


def filter_features(n):
    t = np.linspace(0.0, 1.0, n)[:, None]
    w = (2.0 * math.pi / n) * np.arange(n)[:, None]
    bands = np.linspace(1e-4, BANDS - 1, BANDS)
    return np.concatenate([t, np.cos(w * bands), -np.sin(w * bands)], -1).T.astype(np.float32)


def filter_decay(n):
    deltas = np.abs(np.linspace(math.log(1e-2) / 1.5, math.log(1e-2) / 0.3, HYW))
    t = np.linspace(0.0, 1.0, n)[:, None]
    return np.exp(-t * deltas).reshape(n // P, P, HYW).transpose(1, 0, 2).astype(np.float32)


def spectra_matrices(J):
    n = 2 * J * P
    p = np.arange(P)[:, None]
    fwd = np.zeros((P, 4 * J + 2, P))
    inv = np.zeros((P, 4 * J, P))
    for k in range(J):
        m = np.arange(P)[None]
        f = 2 * J * m + k if k else np.where(m < 64, 2 * J * m, 2 * J * (m - 64) + J)
        ang = 2 * math.pi * ((f * p) % n) / n
        c, s = np.cos(ang), np.sin(ang)
        if k:
            mats = [c, -s, -s, -c]
            back = [c.T, -s.T, -s.T, -c.T]
            back = [2.0 / n * b for b in back]
        else:
            lo = (m < 64) * 1.0
            alt = (-1.0) ** p
            third = -s * lo
            third[:, 0:1] = alt
            mats = [c * lo, c * (1 - lo), third, -s * (1 - lo)]
            weight = np.full((1, P), 2.0 / n)
            weight[0, 0] = 1.0 / n
            i1, i2 = (c * lo * weight).T, (-s * lo * weight).T
            i2[0:1] = alt.T / n
            back = [i1, i2, (c * (1 - lo) * 2 / n).T, (-s * (1 - lo) * 2 / n).T]
            without, only = third.copy(), np.zeros_like(third)
            without[:, 0] = 0
            only[:, 0:1] = alt
            fwd[:, 4 * J], fwd[:, 4 * J + 1] = without, only
        for i in range(4):
            fwd[:, 4 * k + i] = mats[i]
            inv[:, 4 * k + i] = back[i]
    return fwd.astype(np.float32), inv.astype(np.float32)


def constants():
    cos, sin = rope_tables()
    fl, il = spectra_matrices(LAT // P)
    fc, ic = spectra_matrices(CT)
    return {
        "c_ident": np.eye(P, dtype=np.float32),
        "c_cos": cos, "c_sin": sin, "c_swap": swap_matrix(), "c_tri": triangles(),
        "c_feat": np.concatenate([filter_features(CTX), filter_features(LAT)], 1),
        "c_decay": np.concatenate([filter_decay(CTX), filter_decay(LAT)], 1),
        "c_fwd_lat": fl, "c_inv_lat": il, "c_fwd_ctx": fc, "c_inv_ctx": ic,
    }


@contextmanager
def stage(nc, *names):
    with ExitStack() as ctx:
        sems = [ctx.enter_context(nc.semaphore(n)) for n in names]
        yield ctx, sems
        nums = sorted(s.num for s in sems)
        starts = [n for n in nums if n - 1 not in nums]
        for first in starts:
            last = first
            while last + 1 in nums:
                last += 1
            nc.all_engine_barrier(sems_to_clear=range(first, last + 1))


def sb(nc, ctx, name, shape):
    return ctx.enter_context(nc.sbuf_tensor(name, list(shape), F32))


def ps(nc, ctx, name, cols):
    return ctx.enter_context(nc.psum_tensor(name, [P, cols], F32))


def halves(lo, n):
    return [(c, min(BANK, n - c)) for c in range(lo, n, BANK)]


def norm_stage(nc, tag, uT, ident, src_lat, src_ctx, c, c_ctx, w_ada, b_ada, mod_dram):
    NCH = 3 * D // GW
    with stage(nc, tag + "c_in", tag + "wada0", tag + "wada1", tag + "bada", tag + "cond_ready",
               tag + "mod_mm", tag + "mod_ready", tag + "modT_mm", tag + "modT_ready",
               tag + "h_in_ctx", tag + "h_in_lat0", tag + "h_in_lat1", tag + "var_ready", tag + "std_ready", tag + "xn_ready",
               tag + "xT_ready", tag + "u_ready", tag + "dve_step", tag + "stored") as (ctx, sems):
        (c_in, wada0, wada1, bada, cond_ready, mod_mm, mod_ready, modT_mm, modT_ready, h_in_ctx, h_in_lat0, h_in_lat1, var_ready,
         std_ready, xn_ready, xT_ready, u_ready, dve_step, stored) = sems
        wada = (wada0, wada1)
        cond = sb(nc, ctx, tag + "cond", [P, KD, 2])
        wa = sb(nc, ctx, tag + "wa", [P, 2, KD, GW])
        ba = sb(nc, ctx, tag + "ba", [2, 3 * D])
        mod = sb(nc, ctx, tag + "mod", [2, 3 * D])
        modT = sb(nc, ctx, tag + "modT", [P, 2 * KD, 2])
        xn = sb(nc, ctx, tag + "xn", [P, TT, D])
        st = sb(nc, ctx, tag + "st", [P, TT, 2, 6])
        mv = sb(nc, ctx, tag + "mv", [P, TT, 4])
        pm = ps(nc, ctx, tag + "pm", 2 * BANK)
        pT = ps(nc, ctx, tag + "pT", BANK)
        px = ps(nc, ctx, tag + "px", 4 * BANK)
        batches = [list(range(CT)), list(range(CT, CT + 4)), list(range(CT + 4, TT))]

        with nc.Block() as block:
            @block.sync
            def _(sp):
                with nc.allow_non_contiguous_dma(reason="two vectors onto the partitions"):
                    sp.dma_start(cond[:, :, 0], c_ctx.rearrange("(k p) -> p k", p=P)).then_inc(c_in, 16)
                    sp.dma_start(cond[:, :, 1], c[0].rearrange("(k p) -> p k", p=P)).then_inc(c_in, 16)
                sp.dma_start(xn[:, 0:CT], src_ctx.rearrange("(t p) n -> p t n", p=P)).then_inc(h_in_ctx, 16)
                for half, h_in in enumerate((h_in_lat0, h_in_lat1)):
                    t = 4 * half
                    sp.dma_start(xn[:, CT + t:CT + t + 4], src_lat[t * P:(t + 4) * P].rearrange("(t p) n -> p t n", p=P)).then_inc(h_in, 16)
                sp.dma_start(ba[:, :], b_ada.partition_broadcast(2)).then_inc(bada, 16)

                for j in range(NCH):
                    if j >= 2:
                        sp.wait_ge(mod_mm, j - 1)
                    sp.dma_start(wa[:, j % 2], w_ada[:, j * GW:(j + 1) * GW].rearrange("(k p) n -> p k n", p=P)).then_inc(wada[j % 2], 16)
                sp.wait_ge(mod_ready, NCH)
                sp.dma_start(mod_dram, mod[:, 2 * D:3 * D]).then_inc(stored, 16)
                sp.wait_ge(stored, 16)

            @block.scalar
            def _(act):
                act.wait_ge(c_in, 32)
                act.activation(cond[:], cond[:], ACT.Silu).then_inc(cond_ready, 1)
                for t in range(TT):
                    act.wait_ge(var_ready, t + 1)
                    act.activation(mv[:, t, 2:3], mv[:, t, 1:2], ACT.Sqrt).then_inc(std_ready, 1)
                act.wait_ge(modT_ready, 1)
                n = 0
                for b in batches:
                    for k in range(KD):
                        act.wait_ge(xT_ready, n + 1)
                        w = len(b) * P
                        act.activation(uT[:, k, b[0] * P:b[0] * P + w], px[:, (n % 4) * BANK:(n % 4) * BANK + w], ACT.Identity,
                                       scale=modT[:, KD + k, (b[0] >= CT):(b[0] >= CT) + 1],
                                       bias=modT[:, k, (b[0] >= CT):(b[0] >= CT) + 1]).then_inc(u_ready, 1)
                        n += 1

            @block.vector
            def _(dve):
                step = 0

                def normalise(t):
                    nonlocal step
                    dve.wait_ge(h_in_ctx if t < CT else (h_in_lat0, h_in_lat1)[(t - CT) // 4], 16)
                    for i in range(2):
                        dve.bn_stats(st[:, t, i], xn[:, t, i * BANK:(i + 1) * BANK]).then_inc(dve_step, 1)
                    step += 2
                    dve.wait_ge(dve_step, step)
                    dve.bn_aggr(mv[:, t, 0:2], st[:, t]).then_inc(dve_step, 1)
                    step += 1
                    dve.wait_ge(dve_step, step)
                    dve.tensor_scalar(mv[:, t, 1:2], mv[:, t, 1:2], LN_EPS, None, ALU.add).then_inc(var_ready, 1)
                    dve.wait_ge(std_ready, t + 1)
                    dve.reciprocal(mv[:, t, 3:4], mv[:, t, 2:3]).then_inc(dve_step, 1)
                    step += 1
                    dve.wait_ge(dve_step, step)
                    dve.tensor_scalar(xn[:, t], xn[:, t], mv[:, t, 0:1], mv[:, t, 3:4], ALU.subtract, ALU.mult).then_inc(xn_ready, 1)

                for t in range(CT + 4):
                    normalise(t)
                dve.wait_ge(bada, 16)
                for j in range(NCH):
                    dve.wait_ge(mod_mm, j + 1)
                    dve.scalar_tensor_tensor(mod[:, j * GW:(j + 1) * GW], pm[0:2, (j % 2) * BANK:(j % 2 + 1) * BANK],
                                             1.0 if 2 <= j < 4 else 0.0, ba[:, j * GW:(j + 1) * GW], ALU.add, ALU.add).then_inc(mod_ready, 1)
                dve.wait_ge(modT_mm, 1)
                dve.tensor_copy(modT[:].rearrange("p a b -> p (a b)"), pT[:, 0:4 * KD]).then_inc(modT_ready, 1)
                for t in range(CT + 4, TT):
                    normalise(t)

            @block.tensor
            def _(pe):
                pe.wait_ge(cond_ready, 1)
                for j in range(NCH):
                    pe.wait_ge(wada[j % 2], 16 * (j // 2 + 1))
                    if j >= 2:
                        pe.wait_ge(mod_ready, j - 1)
                    for k in range(KD):
                        mm = pe.matmul(pm[0:2, (j % 2) * BANK:(j % 2 + 1) * BANK], cond[:, k], wa[:, j % 2, k], start=(k == 0), stop=(k == KD - 1))
                    mm.then_inc(mod_mm, 1)
                pe.wait_ge(mod_ready, NCH)
                for k in range(2 * KD):
                    mm = pe.transpose(pT[:, 2 * k:2 * k + 2], mod[:, k * P:(k + 1) * P], ident[0:2, 0:2])
                mm.then_inc(modT_mm, 1)
                n = 0
                for b in batches:
                    pe.wait_ge(xn_ready, b[-1] + 1)
                    for k in range(KD):
                        if n >= 4:
                            pe.wait_ge(u_ready, n - 3)
                        for i, t in enumerate(b):
                            mm = pe.transpose(px[:, (n % 4) * BANK + i * P:(n % 4) * BANK + (i + 1) * P], xn[:, t, k * P:(k + 1) * P], ident[:, :])
                        mm.then_inc(xT_ready, 1)
                        n += 1



def repeat(engine, times, body):
    if times == 1:
        body(0)
    else:
        with engine.Fori(0, times) as turn:
            body(turn)


def project_stage(nc, tag, uT, w_in, runs, conv_w=None, conv_b=None, swap=None, cos_d=None, sin_d=None):
    HW = GW // 2
    n_taps = conv_b.shape[0] // P if conv_b is not None else 0
    with_rope = any(r[0] == "rope" for r in runs)
    with stage(nc, tag + "w0_in", tag + "w1_in", tag + "tables_in", tag + "pad_ready", tag + "acc_ready", tag + "acc_free",
               tag + "swapped", tag + "conv_step", tag + "finished", tag + "silu_done", tag + "ctx_copied",
               tag + "stored0", tag + "stored1") as (ctx, sems):
        w0_in, w1_in, tables_in, pad_ready, acc_ready, acc_free, swapped, conv_step, finished, silu_done, ctx_copied, stored0, stored1 = sems
        w_in_sem, stored = (w0_in, w1_in), (stored0, stored1)
        wt = sb(nc, ctx, tag + "wt", [P, 2, KD, HW])
        fin = sb(nc, ctx, tag + "fin", [P, 2, T])
        stg = sb(nc, ctx, tag + "stg", [P, T + 3])
        cv = sb(nc, ctx, tag + "cv", [P, T + 1])
        if n_taps:
            taps = sb(nc, ctx, tag + "taps", [P, 4, n_taps])
        if with_rope:
            cos = sb(nc, ctx, tag + "cos", [P, LAT])
            sin = sb(nc, ctx, tag + "sin", [P, LAT])
        acc = ps(nc, ctx, tag + "acc", 6 * BANK)
        sw = ps(nc, ctx, tag + "sw", 2 * BANK)
        STG_LAT = CTX + 2
        plan, base, shaped, silus = [], 0, 0, 0
        for kind, col, groups, t0, dst, crow in runs:
            plan.append((kind, col, groups, t0, dst, crow, base, shaped, silus))
            base += 4 * groups
            shaped += 4 * groups if kind != "gate" else 0
            silus += 4 * groups if kind == "conv_silu" else 0
        n_tiles = base

        with nc.Block() as block:
            @block.sync
            def _(sp):
                sp.sem_inc(stored0, 16)
                sp.sem_inc(stored1, 16)
                sp.sem_inc(acc_free, 2)
                if n_taps:
                    with nc.allow_non_contiguous_dma(reason="conv taps onto the partitions"):
                        for j in range(3):
                            sp.dma_start(taps[:, j], conv_w[j].rearrange("(n p) -> p n", p=P)).then_inc(tables_in, 16)
                        sp.dma_start(taps[:, 3], conv_b.rearrange("(n p) -> p n", p=P)).then_inc(tables_in, 16)
                if with_rope:
                    sp.dma_start(cos[:], cos_d).then_inc(tables_in, 16)
                    sp.dma_start(sin[:], sin_d).then_inc(tables_in, 16)
                for kind, col, groups, t0, dst, crow, base, shaped, silus in plan:
                    def load_group(g):
                        for half in range(2):
                            sp.wait_ge(acc_ready, base + 4 * g + (2 * half or 1))
                            sp.dma_start(wt[:, half], w_in[:, bass.ds(col + GW * g + HW * half, HW)].rearrange("(k p) n -> p k n", p=P)).then_inc(w_in_sem[half], 16)
                    repeat(sp, groups, load_group)

            @block.tensor
            def _(pe):
                pe.sem_inc(acc_ready, 2)
                for kind, col, groups, t0, dst, crow, base, shaped, silus in plan:
                    def group(g):
                        for i in range(4):
                            if i % 2 == 0:
                                pe.wait_ge(w_in_sem[i // 2], 16 * (base // 4 + g + 1))
                            pe.wait_ge(acc_free, base + 4 * g + i + 1)
                            for k in range(KD):
                                for c, w in halves(0, T - t0):
                                    a = (i % 2) * 3 * BANK + c
                                    mm = pe.matmul(acc[:, a:a + w], wt[:, i // 2, k, (i % 2) * P:(i % 2 + 1) * P], uT[:, k, t0 + c:t0 + c + w],
                                                   start=(k == 0), stop=(k == KD - 1))
                            mm.then_inc(acc_ready, 1)
                            if kind == "rope":
                                pe.wait_ge(acc_free, base + 4 * g + i + 3)
                                if shaped or i:
                                    pe.wait_ge(finished, shaped + 4 * g + i)
                                for c, w in halves(0, LAT):
                                    mm = pe.matmul(sw[:, c:c + w], swap[:, :], stg[:, STG_LAT + c:STG_LAT + c + w], start=True, stop=True)
                                mm.then_inc(swapped, 1)
                    repeat(pe, groups, group)

            @block.scalar
            def _(act):
                act.wait_ge(pad_ready, 1)
                for kind, col, groups, t0, dst, crow, base, shaped, silus in plan:
                    gain = SCALE if col == Q0 else 1.0

                    def group(g):
                        for i in range(4):
                            s, a = i % 2, (i % 2) * 3 * BANK
                            act.wait_ge(acc_ready, base + 4 * g + i + 3)
                            act.wait_ge(stored[s], 16 * (base // 2 + 2 * g + i // 2 + 1))
                            if kind == "gate":
                                act.activation(fin[:, s, t0:T], acc[:, a:a + T - t0], ACT.Silu).then_inc(acc_free, 1)
                                act.wait_ge(acc_free, base + 4 * g + i + 3)
                            else:
                                if kind == "rope" and t0 == 0:
                                    act.activation(fin[:, s, 0:CTX], acc[:, a:a + CTX], ACT.Copy, scale=gain).then_inc(ctx_copied, 1)
                                elif t0 == 0:
                                    act.activation(stg[:, 1:1 + CTX], acc[:, a:a + CTX], ACT.Copy).then_inc(ctx_copied, 1)
                                act.activation(stg[:, STG_LAT:STG_LAT + LAT], acc[:, a + CTX - t0:a + T - t0], ACT.Copy, scale=gain).then_inc(acc_free, 1)
                                act.wait_ge(finished, shaped + 4 * g + i + 1)
                                if kind == "conv_silu":
                                    act.activation(fin[:, s, t0:T], fin[:, s, t0:T], ACT.Silu).then_inc(silu_done, 1)
                                    act.wait_ge(silu_done, silus + 4 * g + i + 1)
                            act.dma_start(dst[bass.ds(P * (4 * g + i), P), t0:T], fin[:, s, t0:T]).then_inc(stored[s], 16)
                    repeat(act, groups, group)
                for s in range(2):
                    act.wait_ge(stored[s], 16 * (n_tiles // 2 + 1))

            @block.vector
            def _(dve):
                dve.memset(stg[:], 0.0).then_inc(pad_ready, 1)
                dve.wait_ge(pad_ready, 1)
                if n_taps or with_rope:
                    dve.wait_ge(tables_in, 64 * (n_taps > 0) + 32 * with_rope)
                steps = 0
                for kind, col, groups, t0, dst, crow, base, shaped, silus in plan:
                    if kind == "gate":
                        continue

                    def group(g):
                        first = steps
                        for i in range(4):
                            s, n = i % 2, 2 * (4 * g + i)
                            dve.wait_ge(acc_free, base + 4 * g + i + 3)
                            if kind == "rope":
                                dve.tensor_tensor(fin[:, s, CTX:T], stg[:, STG_LAT:STG_LAT + LAT], cos[:], ALU.mult).then_inc(conv_step, 1)
                                dve.wait_ge(swapped, shaped + 4 * g + i + 1)
                                dve.tensor_tensor(cv[:, 0:LAT], sw[:, 0:LAT], sin[:], ALU.mult).then_inc(conv_step, 1)
                                dve.wait_ge(conv_step, first + n + 2)
                                dve.tensor_tensor(fin[:, s, CTX:T], fin[:, s, CTX:T], cv[:, 0:LAT], ALU.add).then_inc(finished, 1)
                                continue
                            lo = 0 if t0 == 0 else CTX + 1
                            tile = crow + 4 * g + i

                            def tap(j):
                                return taps[:, j, bass.ds(tile, 1)]
                            dve.tensor_scalar(cv[:, lo:], stg[:, lo + 1:T + 2], tap(1), tap(3), ALU.mult, ALU.add).then_inc(conv_step, 1)
                            dve.wait_ge(conv_step, first + n + 1)
                            dve.scalar_tensor_tensor(cv[:, lo:], stg[:, lo:T + 1], tap(0), cv[:, lo:], ALU.mult, ALU.add).then_inc(conv_step, 1)
                            dve.wait_ge(conv_step, first + n + 2)
                            if t0 == 0:
                                dve.scalar_tensor_tensor(fin[:, s, 0:CTX], stg[:, 2:2 + CTX], tap(2), cv[:, 0:CTX], ALU.mult, ALU.add)
                            dve.scalar_tensor_tensor(fin[:, s, CTX:T], stg[:, STG_LAT + 1:STG_LAT + 1 + LAT], tap(2), cv[:, CTX + 1:], ALU.mult, ALU.add).then_inc(finished, 1)
                    repeat(dve, groups, group)
                    steps += 8 * groups


def v_dt_stage(nc, tag, uT, w_in, tri, ident, dt_bias, a_log, v_d, la_d, small):
    la, dt, to_end, whole = (small[:, i] for i in range(4))
    H2 = 2 * HEADS
    with stage(nc, tag + "wv_in", tag + "wdt_in", tag + "vec_in", tag + "v_mm", tag + "v_copied", tag + "v_out", tag + "dt_mm",
               tag + "dve_step", tag + "act_step", tag + "la_mm", tag + "la_ready", tag + "laT_mm", tag + "laT_ready", tag + "la_out") as (ctx, sems):
        wv_in, wdt_in, vec_in, v_mm, v_copied, v_out, dt_mm, dve_step, act_step, la_mm, la_ready, laT_mm, laT_ready, la_out = sems
        wv = sb(nc, ctx, tag + "wv", [P, KD, HYW])
        wdt = sb(nc, ctx, tag + "wdt", [P, KD, H2])
        vb = sb(nc, ctx, tag + "vb", [P, TT, HYW])
        bias = sb(nc, ctx, tag + "bias", [P, H2])
        alog = sb(nc, ctx, tag + "alog", [P, H2])
        tmp = sb(nc, ctx, tag + "tmp", [P, 4, TT * H2])
        laT = sb(nc, ctx, tag + "laT", [H2, T])
        pv = ps(nc, ctx, tag + "pv", 2 * BANK)
        pd = ps(nc, ctx, tag + "pd", BANK)
        pl = ps(nc, ctx, tag + "pl", 2 * BANK)
        pt = ps(nc, ctx, tag + "pt", 3 * BANK)
        N = TT * H2
        flat = "p t h -> p (t h)"
        lam = pl[:, 0:N].rearrange("p (t h) -> p t h", h=H2)
        end = pl[:, BANK:BANK + N].rearrange("p (t h) -> p t h", h=H2)

        with nc.Block() as block:
            @block.sync
            def _(sp):
                with nc.allow_non_contiguous_dma(reason="32 columns of w_in"):
                    sp.dma_start(wdt[:], w_in[:, DT0:DT0 + H2].rearrange("(k p) n -> p k n", p=P)).then_inc(wdt_in, 16)
                sp.dma_start(bias[:], dt_bias.rearrange("a h -> (a h)").partition_broadcast(P)).then_inc(vec_in, 16)
                sp.dma_start(alog[:], a_log.rearrange("a h -> (a h)").partition_broadcast(P)).then_inc(vec_in, 16)
                sp.dma_start(wv[:], w_in[:, V0:V0 + HYW].rearrange("(k p) n -> p k n", p=P)).then_inc(wv_in, 16)
                sp.wait_ge(laT_ready, 1)
                sp.dma_start(la_d, laT[:]).then_inc(la_out, 16)
                sp.wait_ge(la_out, 16)

            @block.tensor
            def _(pe):
                pe.wait_ge(wdt_in, 16)
                for t in range(TT):
                    for k in range(KD):
                        mm = pe.matmul(pd[:, t * H2:(t + 1) * H2], uT[:, k, t * P:(t + 1) * P], wdt[:, k], start=(k == 0), stop=(k == KD - 1))
                mm.then_inc(dt_mm, 1)
                pe.wait_ge(wv_in, 16)
                for t in range(TT):
                    if t >= 2:
                        pe.wait_ge(v_copied, t - 1)
                    for k in range(KD):
                        mm = pe.matmul(pv[:, (t % 2) * BANK:(t % 2 + 1) * BANK], uT[:, k, t * P:(t + 1) * P], wv[:, k], start=(k == 0), stop=(k == KD - 1))
                    mm.then_inc(v_mm, 1)
                pe.wait_ge(dve_step, 7)
                da = tmp[:, 3].rearrange("p (t h) -> p t h", h=H2)
                pe.matmul(lam[:, :, 0:HEADS], tri[:, 0], da[:, :, 0:HEADS], start=True, stop=True)
                pe.matmul(lam[:, :, HEADS:H2], tri[:, 1], da[:, :, HEADS:H2], start=True, stop=True)
                pe.matmul(pl[:, BANK:BANK + N], tri[:, 2], tmp[:, 3], start=True, stop=True).then_inc(la_mm, 1)
                pe.wait_ge(la_ready, 1)
                for t in range(TT):
                    mm = pe.transpose(pt[0:H2, t * P:(t + 1) * P], la[:, t], ident[:, :])
                mm.then_inc(laT_mm, 1)

            @block.scalar
            def _(act):
                act.wait_ge(vec_in, 32)
                act.activation(alog[:], alog[:], ACT.Exp).then_inc(act_step, 1)
                act.wait_ge(dve_step, 2)
                act.activation(tmp[:, 1], tmp[:, 1], ACT.Exp, scale=-1.0).then_inc(act_step, 1)
                act.wait_ge(act_step, 2)
                act.activation(tmp[:, 1], tmp[:, 1], ACT.Ln, bias=1.0).then_inc(act_step, 1)
                for t in range(TT):
                    act.wait_ge(v_mm, t + 1)
                    act.activation(vb[:, t], pv[:, (t % 2) * BANK:(t % 2 + 1) * BANK], ACT.Copy).then_inc(v_copied, 1)
                    act.wait_ge(v_copied, t + 1)
                    act.dma_start(v_d[t * P:(t + 1) * P], vb[:, t]).then_inc(v_out, 16)
                act.wait_ge(dve_step, 8)
                act.activation(to_end.rearrange(flat), to_end.rearrange(flat), ACT.Exp).then_inc(act_step, 1)
                act.activation(whole.rearrange(flat), pl[:, BANK:BANK + N], ACT.Exp).then_inc(act_step, 1)
                act.wait_ge(v_out, 16 * TT)

            @block.vector
            def _(dve):
                def bc(v):
                    return v[:].unsqueeze(1).to_broadcast([P, TT, H2])
                x3 = tmp[:, 0].rearrange("p (t h) -> p t h", h=H2)
                dve.wait_ge(dt_mm, 1)
                dve.wait_ge(vec_in, 32)
                dve.tensor_tensor(x3, pd[:, 0:N].rearrange("p (t h) -> p t h", h=H2), bc(bias), ALU.add).then_inc(dve_step, 1)
                dve.wait_ge(dve_step, 1)
                dve.scalar_tensor_tensor(tmp[:, 1], tmp[:, 0], -1.0, tmp[:, 0], ALU.mult, ALU.max).then_inc(dve_step, 1)
                dve.tensor_scalar(tmp[:, 2], tmp[:, 0], 0.0, None, ALU.max).then_inc(dve_step, 1)
                dve.wait_ge(act_step, 3)
                dve.wait_ge(dve_step, 3)
                dve.tensor_tensor(dt.rearrange(flat), tmp[:, 1], tmp[:, 2], ALU.add).then_inc(dve_step, 1)
                dve.wait_ge(dve_step, 4)
                dve.tensor_tensor(x3, dt, bc(alog), ALU.mult).then_inc(dve_step, 1)
                dve.wait_ge(dve_step, 5)
                dve.tensor_scalar(tmp[:, 3], tmp[:, 0], -1.0, None, ALU.mult).then_inc(dve_step, 2)
                dve.wait_ge(la_mm, 1)
                dve.tensor_copy(la, lam).then_inc(la_ready, 1)
                dve.wait_ge(la_ready, 1)
                dve.tensor_tensor(to_end, end, la, ALU.subtract).then_inc(dve_step, 1)
                dve.wait_ge(laT_mm, 1)
                dve.tensor_copy(laT[:], pt[0:H2, 0:T]).then_inc(laT_ready, 1)
                dve.wait_ge(act_step, 5)
                dve.tensor_tensor(to_end.rearrange(flat), to_end.rearrange(flat), dt.rearrange(flat), ALU.mult).then_inc(dve_step, 1)


def attention_stage(nc, tag, layer, first_tile, ident, tri, lam_vecs, qk_d, v_d, gate_d, o_d):
    tiles = list(range(first_tile, TT))
    nq = len(tiles)
    BODY = 2
    units = [(hh, q) for hh in range(BODY) for q in tiles]
    NU = len(units)

    def keys(q):
        return CTX if q < CT else T

    batches = [-(-keys(q) // BANK) for _, q in units]
    before = [sum(batches[:n]) for n in range(NU + 1)]
    with stage(nc, tag + "lam_in", tag + "in0", tag + "in1", tag + "lam_step", tag + "lam_exp", tag + "scored", tag + "maxed", tag + "exped",
               tag + "mix_step", tag + "mixed", tag + "turned", tag + "turned_copied", tag + "pv_done", tag + "squared", tag + "sq_summed",
               tag + "log_done", tag + "rms_ready", tag + "scaled", tag + "gated", tag + "stored0", tag + "stored1") as (ctx, sems):
        (lam_in, in0, in1, lam_step, lam_exp, scored, maxed, exped, mix_step, mixed, turned, turned_copied, pv_done, squared, sq_summed,
         log_done, rms_ready, scaled, gated, stored0, stored1) = sems
        stored = (stored0, stored1)
        head_in = (in0, in1)
        q_s = sb(nc, ctx, tag + "q", [P, BODY, T])
        k_s = sb(nc, ctx, tag + "k", [P, BODY, T])
        g_s = sb(nc, ctx, tag + "g", [P, BODY, T])
        v_s = sb(nc, ctx, tag + "v", [P, BODY, TT, P])
        o_s = sb(nc, ctx, tag + "o", [P, BODY, T])
        prob = sb(nc, ctx, tag + "prob", [P, 2, 2, T])
        mix = sb(nc, ctx, tag + "mix", [P, 2, T])
        mixT = sb(nc, ctx, tag + "mixT", [P, TT, P])
        sq = sb(nc, ctx, tag + "sq", [P, 2, P])
        rms = sb(nc, ctx, tag + "rms", [P, 2, P])
        part = sb(nc, ctx, tag + "part", [P, P])
        nmax = sb(nc, ctx, tag + "nmax", [P, 2, 2])
        sums = sb(nc, ctx, tag + "sums", [P, 2, 2])
        recip = sb(nc, ctx, tag + "recip", [P, 2, 2])
        lv = sb(nc, ctx, tag + "lv", [P, 4, AD])
        lt = sb(nc, ctx, tag + "lt", [P, 2, AD])
        lam = sb(nc, ctx, tag + "lam", [P, 4])
        cst = sb(nc, ctx, tag + "cst", [P, 2])
        pS = ps(nc, ctx, tag + "pS", 6 * BANK)
        pT = ps(nc, ctx, tag + "pT", BANK)
        pO = ps(nc, ctx, tag + "pO", BANK)

        def turns(engine, body):
            with engine.Fori(0, AH // BODY) as turn:
                body(turn)

        with nc.Block() as block:
            @block.sync
            def _(sp):
                sp.dma_start(lv[:], lam_vecs.partition_broadcast(P)).then_inc(lam_in, 16)
                t0 = first_tile * P

                def store(h):
                    sp.wait_ge(gated, (h + 1) * nq + 1)
                    sp.dma_start(o_d[1024 + h * P:1024 + (h + 1) * P, t0:], o_s[:, h % BODY, t0:]).then_inc(stored[h % BODY], 16)

                for h in range(AH):
                    hh, row = h % BODY, P * h
                    if h >= BODY:
                        store(h - BODY)
                        sp.wait_ge(stored[hh], 16 * (h // BODY))
                    sp.dma_start(q_s[:, hh, t0:], qk_d[row:row + P, t0:]).then_inc(head_in[hh], 16)
                    sp.dma_start(k_s[:, hh], qk_d[row + HYW:row + HYW + P, :]).then_inc(head_in[hh], 16)
                    sp.dma_start(v_s[:, hh], v_d.rearrange("(t p) n -> p t n", p=P)[:, :, row:row + P]).then_inc(head_in[hh], 16)
                    sp.dma_start(g_s[:, hh, t0:], gate_d[row:row + P, t0:]).then_inc(head_in[hh], 16)
                for h in range(AH - BODY, AH):
                    store(h)
                for hh in range(BODY):
                    sp.wait_ge(stored[hh], 16 * (AH // BODY))

            @block.tensor
            def _(pe):
                pe.wait_ge(lam_exp, 1)

                def body(g):
                    def scores(n, m):
                        hh, q = units[n]
                        if q == tiles[0] and m == 0:
                            pe.wait_ge(head_in[hh], 64 * (g + 1))
                        pe.wait_ge(exped, 2 * (NU * g + n) + m + 1)
                        for c, w in halves(0, keys(q)):
                            mm = pe.matmul(pS[:, m * 3 * BANK + c:m * 3 * BANK + c + w], q_s[AD * m:AD * (m + 1), hh, q * P:(q + 1) * P],
                                           k_s[AD * m:AD * (m + 1), hh, c:c + w], start=True, stop=True)
                        mm.then_inc(scored, 1)

                    def values(n):
                        hh, q = units[n]
                        pe.wait_ge(mixed, NU * g + n + 3)
                        for b in range(batches[n]):
                            pe.wait_ge(turned_copied, before[NU] * g + before[n] + b + 1)
                            for kt in range(4 * b, min(4 * b + 4, keys(q) // P)):
                                mm = pe.transpose(pT[:, (kt % 4) * P:(kt % 4 + 1) * P], mix[:, n % 2, kt * P:(kt + 1) * P], ident[:, :])
                            mm.then_inc(turned, 1)
                        pe.wait_ge(turned_copied, before[NU] * g + before[n + 1] + 1)
                        pe.wait_ge(scaled, NU * g + n + 1)
                        for kt in range(keys(q) // P):
                            mm = pe.matmul(pO[:, 0:P], v_s[:, hh, kt], mixT[:, kt], start=(kt == 0), stop=(kt == keys(q) // P - 1))
                        mm.then_inc(pv_done, 1)

                    def squares(n):
                        pe.wait_ge(squared, NU * g + n + 1)
                        pe.matmul(pO[:, P:2 * P], tri[:, 2], sq[:, n % 2], start=True, stop=True).then_inc(sq_summed, 1)

                    for i in range(NU + 3):
                        if i < NU:
                            scores(i, 0)
                        if i >= 3:
                            squares(i - 3)
                        if i < NU:
                            scores(i, 1)
                        if 2 <= i < NU + 2:
                            values(i - 2)
                turns(pe, body)

            @block.scalar
            def _(act):
                act.preload_act_table_set("natural_log_exp_and_others")
                act.sem_inc(exped, 2)
                act.sem_inc(turned_copied, 1)
                act.wait_ge(lam_step, 3)
                act.activation(lam[:, 2:4], lam[:, 0:2], ACT.Exp).then_inc(lam_exp, 1)

                def body(g):
                    def exps(n):
                        hh, q = units[n]
                        for m in range(2):
                            act.wait_ge(maxed, 2 * (NU * g + n) + m + 1)
                            act.wait_ge(mixed, NU * g + n + 1)
                            act.activation(prob[:, n % 2, m, 0:keys(q)], pS[:, m * 3 * BANK:m * 3 * BANK + keys(q)], ACT.Exp,
                                           bias=nmax[:, n % 2, m:m + 1], accum_out=sums[:, n % 2, m:m + 1]).then_inc(exped, 1)

                    def turn(n):
                        hh, q = units[n]
                        for b in range(batches[n]):
                            act.wait_ge(turned, before[NU] * g + before[n] + b + 1)
                            w = min(BANK, keys(q) - b * BANK)
                            act.activation(mixT[:, 4 * b:4 * b + w // P].rearrange("p a b -> p (a b)"), pT[:, 0:w], ACT.Copy).then_inc(turned_copied, 1)
                        act.wait_ge(pv_done, NU * g + n + 1)
                        act.activation(sq[:, n % 2], pO[:, 0:P], ACT.Square).then_inc(squared, 1)

                    def norm(n):
                        act.wait_ge(sq_summed, NU * g + n + 1)
                        act.activation(rms[:, n % 2], pO[:, P:2 * P], ACT.Ln, scale=1.0 / P, bias=cst[:, 0:1]).then_inc(log_done, 1)
                        act.wait_ge(log_done, NU * g + n + 1)
                        act.activation(rms[:, n % 2], rms[:, n % 2], ACT.Exp, scale=-0.5, bias=cst[:, 1:2]).then_inc(rms_ready, 1)

                    for i in range(NU + 3):
                        if i >= 3:
                            norm(i - 3)
                        if i < NU:
                            exps(i)
                        if 2 <= i < NU + 2:
                            turn(i - 2)
                turns(act, body)

            @block.vector
            def _(dve):
                dve.sem_inc(scaled, 1)
                dve.sem_inc(mixed, 2)
                dve.memset(cst[:, 0:1], RMS_EPS)
                dve.memset(cst[:, 1:2], math.log(1.0 - lam_init(layer))).then_inc(lam_step, 1)
                dve.wait_ge(lam_in, 16)
                dve.tensor_tensor(lt[:], lv[:, 0:4:2], lv[:, 1:4:2], ALU.mult).then_inc(lam_step, 1)
                dve.wait_ge(lam_step, 2)
                dve.tensor_reduce(lam[:, 0:2], lt[:], AX.X, ALU.add).then_inc(lam_step, 1)
                dve.wait_ge(lam_exp, 1)
                dve.tensor_tensor(lam[:, 1:2], lam[:, 3:4], lam[:, 2:3], ALU.subtract).then_inc(lam_step, 1)
                dve.wait_ge(lam_step, 4)
                dve.tensor_scalar(lam[:, 0:1], lam[:, 1:2], -lam_init(layer), None, ALU.add).then_inc(lam_step, 1)
                dve.wait_ge(lam_step, 5)

                def body(g):
                    def maximum(n, m):
                        hh, q = units[n]
                        dve.wait_ge(scored, 2 * (NU * g + n) + m + 1)
                        dve.tensor_reduce(nmax[:, n % 2, m:m + 1], pS[:, m * 3 * BANK:m * 3 * BANK + keys(q)], AX.X, ALU.max, negate=True).then_inc(maxed, 1)

                    def combine(n):
                        hh, q = units[n]
                        s, steps = n % 2, 3 * (NU * g + n)
                        dve.wait_ge(exped, 2 * (NU * g + n) + 4)
                        dve.reciprocal(recip[:, s], sums[:, s]).then_inc(mix_step, 1)
                        dve.wait_ge(mix_step, steps + 1)
                        dve.tensor_scalar(recip[:, s, 1:2], recip[:, s, 1:2], lam[:, 0:1], None, ALU.mult).then_inc(mix_step, 1)
                        if n >= 2:
                            dve.wait_ge(turned, before[NU] * g + before[n - 1])
                        dve.tensor_scalar(mix[:, s, 0:keys(q)], prob[:, s, 0, 0:keys(q)], recip[:, s, 0:1], None, ALU.mult).then_inc(mix_step, 1)
                        dve.wait_ge(mix_step, steps + 3)
                        dve.scalar_tensor_tensor(mix[:, s, 0:keys(q)], prob[:, s, 1, 0:keys(q)], recip[:, s, 1:2], mix[:, s, 0:keys(q)], ALU.mult, ALU.add).then_inc(mixed, 1)

                    def gate(n):
                        hh, q = units[n]
                        dve.wait_ge(rms_ready, NU * g + n + 1)
                        dve.wait_ge(gated, NU * g + n + 1)
                        dve.tensor_tensor(part[:], pO[:, 0:P], rms[:, n % 2], ALU.mult).then_inc(scaled, 1)
                        dve.wait_ge(scaled, NU * g + n + 2)
                        dve.tensor_tensor(o_s[:, hh, q * P:(q + 1) * P], part[:], g_s[:, hh, q * P:(q + 1) * P], ALU.mult).then_inc(gated, 1)

                    for i in range(NU + 3):
                        if i < NU:
                            maximum(i, 0)
                        if i >= 3:
                            gate(i - 3)
                        if i < NU:
                            maximum(i, 1)
                        if 1 <= i < NU + 1:
                            combine(i - 1)
                dve.sem_inc(gated, 1)
                turns(dve, body)


def ssd_stage(nc, tag, first_tile, tri, ident, small, skip, xbc_d, la_d, gate_z, o_d):
    XG = HPG * HD
    XT = XG // P
    BODY = 2
    outs = list(range(first_tile, TT))
    NO = len(outs)
    order = [list(range(TT)), list(range(CT))[::-1] + list(range(CT, TT))[::-1]]
    NSTEP = TT - 1
    with stage(nc, tag + "in0", tag + "in1", tag + "la0_in", tag + "la1_in", tag + "skip_in", tag + "zeroed", tag + "picked", tag + "turned", tag + "x_copied",
               tag + "x_scaled", tag + "state_mm", tag + "decayed", tag + "state_ready", tag + "cb_mm", tag + "cb_masked", tag + "seg_ready",
               tag + "dec_ready", tag + "w_ready", tag + "c_scaled", tag + "y_mm", tag + "skipped", tag + "gated", tag + "stored0", tag + "stored1") as (ctx, sems):
        (in0, in1, la0_in, la1_in, skip_in, zeroed, picked, turned, x_copied, x_scaled, state_mm, decayed, state_ready, cb_mm, cb_masked, seg_ready,
         dec_ready, w_ready, c_scaled, y_mm, skipped, gated, stored0, stored1) = sems
        group_in, la_in, stored = (in0, in1), (la0_in, la1_in), (stored0, stored1)
        xT = sb(nc, ctx, tag + "xT", [P, BODY, XT, T])
        zT = sb(nc, ctx, tag + "zT", [P, BODY, XT, T])
        bT = sb(nc, ctx, tag + "bT", [P, BODY, T])
        cT = sb(nc, ctx, tag + "cT", [P, BODY, T])
        o_s = sb(nc, ctx, tag + "o", [P, BODY, XT, T])
        tok = sb(nc, ctx, tag + "tok", [P, TT, XG + P])
        xdt = sb(nc, ctx, tag + "xdt", [P, TT, 2, HPG, HD])
        xend = sb(nc, ctx, tag + "xend", [P, TT, 2, HPG, HD])
        state = sb(nc, ctx, tag + "state", [P, 2, TT, HPG, HD])
        fade = sb(nc, ctx, tag + "fade", [P, 2, HPG, HD])
        mine = sb(nc, ctx, tag + "mine", [P, BODY, 4, TT, 2, HPG])
        la_b = sb(nc, ctx, tag + "la_b", [P, 2, 2, HPG, P])
        seg = sb(nc, ctx, tag + "seg", [P, 2, 2, HPG, P])
        cs = sb(nc, ctx, tag + "cs", [P, 2, 2 * HPG, P])
        cbm = sb(nc, ctx, tag + "cbm", [P, 2, 2, P])
        d_s = sb(nc, ctx, tag + "d", [P, SSD_TILES])
        part = sb(nc, ctx, tag + "part", [P, XT, P])
        pT = ps(nc, ctx, tag + "pT", 2 * BANK)
        pS = ps(nc, ctx, tag + "pS", 2 * BANK)
        pC = ps(nc, ctx, tag + "pC", 2 * BANK)
        pY = ps(nc, ctx, tag + "pY", 2 * BANK)
        steps = [(d, order[d][n], order[d][n + 1]) for n in range(NSTEP) for d in range(2)]

        def turns(engine, body):
            with engine.Fori(0, GROUPS // BODY) as turn:
                def groups():
                    for hh in range(BODY):
                        body(hh, BODY * turn + hh, turn)
                groups()

        with nc.Block() as block:
            @block.sync
            def _(sp):
                for half in range(2):
                    with nc.allow_non_contiguous_dma(reason="one value per head"):
                        sp.dma_start(d_s[HD * half:HD * (half + 1), :], skip.rearrange("(n b) -> b n", b=2)[half].partition_broadcast(HD)).then_inc(skip_in, 16)

                def load_group(gr):
                    hh = gr % BODY
                    if gr >= BODY:
                        sp.wait_ge(stored[hh], 16 * (gr // BODY))
                    t0 = first_tile * P
                    sp.dma_start(xT[:, hh], xbc_d[gr * XG:(gr + 1) * XG].rearrange("(n p) t -> p n t", p=P)).then_inc(group_in[hh], 16)
                    sp.dma_start(bT[:, hh], xbc_d[1024 + gr * P:1024 + (gr + 1) * P]).then_inc(group_in[hh], 16)
                    sp.dma_start(cT[:, hh], xbc_d[1536 + gr * P:1536 + (gr + 1) * P]).then_inc(group_in[hh], 16)
                    sp.dma_start(zT[:, hh, :, t0:], gate_z[gr * XG:(gr + 1) * XG, t0:].rearrange("(n p) t -> p n t", p=P)).then_inc(group_in[hh], 16)

                def store_group(gr):
                    hh, t0 = gr % BODY, first_tile * P
                    sp.wait_ge(gated, NO * (gr + 1) + 2)
                    sp.dma_start(o_d[gr * XG:(gr + 1) * XG, t0:].rearrange("(n p) t -> p n t", p=P), o_s[:, hh, :, t0:]).then_inc(stored[hh], 16)

                load_group(0)
                for gr in range(GROUPS):
                    for i, c in enumerate(outs):
                        n = gr * NO + i
                        if n >= 2:
                            sp.wait_ge(c_scaled, n - 1)
                        for d in range(2):
                            rows = d * HEADS + gr * HPG
                            sp.dma_start(la_b[:, n % 2, d], la_d[rows:rows + HPG, c * P:(c + 1) * P].partition_broadcast(P)).then_inc(la_in[n % 2], 16)
                        if i == 1:
                            if gr:
                                store_group(gr - 1)
                            if gr + 1 < GROUPS:
                                load_group(gr + 1)
                store_group(GROUPS - 1)
                for hh in range(BODY):
                    sp.wait_ge(stored[hh], 16 * (GROUPS // BODY))

            @block.tensor
            def _(pe):
                pe.wait_ge(zeroed, 1)

                def body(hh, gr, turn):
                    pe.wait_ge(group_in[hh], 64 * (turn + 1))
                    for c in range(TT):
                        pe.wait_ge(x_copied, TT * gr + c + 1)
                        b = (c % 2) * BANK
                        cols = slice(c * P, (c + 1) * P)
                        for n in range(XT):
                            pe.transpose(pT[:, b + n * P:b + (n + 1) * P], xT[:, hh, n, cols], ident[:, :])
                        pe.transpose(pT[:, b + XG:b + XG + P], bT[:, hh, cols], ident[:, :]).then_inc(turned, 1)
                    pe.wait_ge(x_scaled, 2 * TT * (gr + 1))
                    for n, (d, c, nxt) in enumerate(steps):
                        pe.wait_ge(state_ready, 2 * NSTEP * gr + n + 1)
                        pe.matmul(pS[:, d * BANK:d * BANK + XG], tok[:, c, XG:XG + P], xend[:, c, d].rearrange("p h e -> p (h e)"),
                                  start=True, stop=True).then_inc(state_mm, 1)

                    def outputs(i):
                        c, b = outs[i], (i % 2) * BANK
                        if i == 0:
                            pe.wait_ge(state_ready, 2 * NSTEP * (gr + 1) + 2)
                        pe.wait_ge(w_ready, NO * gr + i + 1)
                        pe.wait_ge(c_scaled, NO * gr + i + 1)
                        pe.wait_ge(gated, NO * gr + i + 1)
                        for j in range(HPG):
                            out = pY[HD * (j % 2):HD * (j % 2 + 1), b + (j // 2) * P:b + (j // 2 + 1) * P]
                            for d in range(2):
                                pe.matmul(out, xdt[:, c, d, j], seg[:, i % 2, d, j], start=(d == 0), stop=False)
                                mm = pe.matmul(out, state[:, d, c, j], cs[:, i % 2, d * HPG + j], start=False, stop=(d == 1))
                        mm.then_inc(y_mm, 1)

                    for i in range(NO + 1):
                        if i < NO:
                            c = outs[i]
                            pe.wait_ge(cb_masked, NO * gr + i + 1)
                            pe.matmul(pC[:, (i % 2) * BANK:(i % 2) * BANK + P], bT[:, hh, c * P:(c + 1) * P], cT[:, hh, c * P:(c + 1) * P],
                                      start=True, stop=True).then_inc(cb_mm, 1)
                        if i >= 1:
                            outputs(i - 1)
                turns(pe, body)

            @block.scalar
            def _(act):
                act.preload_act_table_set("natural_log_exp_and_others")
                act.sem_inc(x_copied, 2)

                def body(hh, gr, turn):
                    for c in range(TT):
                        act.wait_ge(turned, TT * gr + c + 1)
                        act.activation(tok[:, c], pT[:, (c % 2) * BANK:(c % 2) * BANK + XG + P], ACT.Copy).then_inc(x_copied, 1)
                    for i in range(NO):
                        act.wait_ge(seg_ready, NO * gr + i + 1)
                        act.activation(seg[:, i % 2].rearrange("p d h l -> p (d h l)"), seg[:, i % 2].rearrange("p d h l -> p (d h l)"), ACT.Exp).then_inc(dec_ready, 1)
                        act.activation(la_b[:, i % 2].rearrange("p d h l -> p (d h l)"), la_b[:, i % 2].rearrange("p d h l -> p (d h l)"), ACT.Exp).then_inc(dec_ready, 1)
                turns(act, body)

            @block.gpsimd
            def _(pool):
                def body(hh, gr, turn):
                    pool.wait_ge(picked, gr + 1)
                    for c in range(TT):
                        pool.wait_ge(x_copied, TT * gr + c + 3)
                        x = tok[:, c, 0:XG].rearrange("p (h e) -> p h e", h=HPG).unsqueeze(1).to_broadcast([P, 2, HPG, HD])
                        for dst, kind in ((xdt, 1), (xend, 2)):
                            pool.tensor_tensor(dst[:, c], x, mine[:, hh, kind, c].unsqueeze(3).to_broadcast([P, 2, HPG, HD]), ALU.mult).then_inc(x_scaled, 1)
                    for i in range(NO):
                        c = outs[i]
                        pool.wait_ge(dec_ready, 2 * (NO * gr + i) + 2)
                        pool.wait_ge(y_mm, NO * gr + i + 1)
                        pool.tensor_tensor(cs[:, i % 2], la_b[:, i % 2].rearrange("p d h l -> p (d h) l"),
                                           cT[:, hh, c * P:(c + 1) * P].unsqueeze(1).to_broadcast([P, 2 * HPG, P]), ALU.mult).then_inc(c_scaled, 1)
                pool.sem_inc(y_mm, 2)
                turns(pool, body)

            @block.vector
            def _(dve):
                for d in range(2):
                    z = dve.memset(state[:, d, order[d][0]], 0.0)
                z.then_inc(zeroed, 1)
                dve.sem_inc(state_ready, 2)
                dve.sem_inc(cb_masked, 2)
                dve.sem_inc(gated, 2)
                dve.wait_ge(skip_in, 32)

                def body(hh, gr, turn):
                    cols = small[:].rearrange("p k t (d h) -> p (k t) d h", d=2)[:, :, :, bass.ds(HPG * gr, HPG)]
                    dve.tensor_copy(mine[:, hh].rearrange("p k t d h -> p (k t) d h"), cols).then_inc(picked, 1)
                    dve.wait_ge(picked, gr + 1)
                    for n, (d, c, nxt) in enumerate(steps):
                        at = 2 * NSTEP * gr + n
                        dve.wait_ge(state_ready, at + 1)
                        dve.tensor_tensor(fade[:, d], state[:, d, c], mine[:, hh, 3, c, d].unsqueeze(2).to_broadcast([P, HPG, HD]), ALU.mult).then_inc(decayed, 1)
                        dve.wait_ge(decayed, at + 1)
                        dve.wait_ge(state_mm, at + 1)
                        dve.tensor_tensor(state[:, d, nxt].rearrange("p h e -> p (h e)"), fade[:, d].rearrange("p h e -> p (h e)"),
                                          pS[:, d * BANK:d * BANK + XG], ALU.add).then_inc(state_ready, 1)

                    def differences(i):
                        c, at = outs[i], NO * gr + i
                        dve.wait_ge(la_in[i % 2], 32 * ((NO // 2) * gr + i // 2 + 1))
                        dve.wait_ge(y_mm, at + 1)
                        for d in range(2):
                            for j in range(HPG):
                                last = dve.tensor_scalar(seg[:, i % 2, d, j], la_b[:, i % 2, d, j], mine[:, hh, 0, c, d, j:j + 1], 0.0, ALU.subtract, ALU.min)
                        last.then_inc(seg_ready, 1)
                        dve.wait_ge(cb_mm, at + 1)
                        cb = pC[:, (i % 2) * BANK:(i % 2) * BANK + P].unsqueeze(1).to_broadcast([P, 2, P])
                        dve.tensor_tensor(cbm[:, i % 2], cb, tri[:, 0:2], ALU.mult).then_inc(cb_masked, 1)

                    def weights(i):
                        at = NO * gr + i
                        dve.wait_ge(dec_ready, 2 * at + 1)
                        dve.wait_ge(cb_masked, at + 3)
                        dve.tensor_tensor(seg[:, i % 2], seg[:, i % 2], cbm[:, i % 2].unsqueeze(2).to_broadcast([P, 2, HPG, P]), ALU.mult).then_inc(w_ready, 1)

                    def gate(i):
                        at, c = NO * gr + i, outs[i]
                        cols, b = slice(c * P, (c + 1) * P), (i % 2) * BANK
                        dve.wait_ge(y_mm, at + 3)
                        dve.wait_ge(gated, at + 2)
                        for n in range(XT):
                            last = dve.scalar_tensor_tensor(part[:, n], xT[:, hh, n, cols], d_s[:, bass.ds(XT * gr + n, 1)], pY[:, b + n * P:b + (n + 1) * P], ALU.mult, ALU.add)
                        last.then_inc(skipped, 1)
                        dve.wait_ge(skipped, at + 1)
                        dve.tensor_tensor(o_s[:, hh, :, cols], part[:], zT[:, hh, :, cols], ALU.mult).then_inc(gated, 1)

                    for i in range(NO + 2):
                        if i < NO:
                            differences(i)
                        if 1 <= i < NO + 1:
                            weights(i - 1)
                        if i >= 2:
                            gate(i - 2)
                turns(dve, body)


R2 = math.sqrt(0.5)
C1, C3 = math.cos(math.pi / 8), math.cos(3 * math.pi / 8)


class Steps:

    def __init__(self, engine, sem):
        self.engine, self.sem, self.n = engine, sem, 0

    def add(self, out, a, b):
        self.engine.tensor_tensor(out, a, b, ALU.add).then_inc(self.sem, 1)
        self.n += 1

    def sub(self, out, a, b):
        self.engine.tensor_tensor(out, a, b, ALU.subtract).then_inc(self.sem, 1)
        self.n += 1

    def scale(self, out, a, s):
        self.engine.tensor_scalar(out, a, s, None, ALU.mult).then_inc(self.sem, 1)
        self.n += 1

    def axpy(self, out, s, a, b, op=ALU.add):
        self.engine.scalar_tensor_tensor(out, a, s, b, ALU.mult, op).then_inc(self.sem, 1)
        self.n += 1

    def level(self):
        self.engine.wait_ge(self.sem, self.n)


def butterfly(do, J, u, R, Tm):
    def r(k):
        return R[:, k, 0]

    def w(k):
        return R[:, k, 1]
    if J == 2:
        do.add(r(0), u[:, 0], u[:, 1])
        do.sub(w(0), u[:, 0], u[:, 1])
        do.scale(R[:, 1], u[:, 0:2], 1.0)
        return
    s, d = Tm[:, 0:4], Tm[:, 4:8]
    do.add(s, u[:, 0:4], u[:, 4:8])
    do.sub(d, u[:, 0:4], u[:, 4:8])
    for j in (1, 2, 3):
        do.sub(Tm[:, 7 + j], u[:, j], u[:, 8 - j])
        do.add(Tm[:, 10 + j], u[:, j], u[:, 8 - j])
    do.level()
    a1, a2, a3, b1, b2, b3 = (Tm[:, i] for i in range(8, 14))
    do.sub(r(4), s[:, 0], s[:, 2])
    do.sub(w(4), s[:, 1], s[:, 3])
    do.add(Tm[:, 14:16], s[:, 0:2], s[:, 2:4])
    do.sub(r(2), d[:, 1], d[:, 3])
    do.add(w(2), d[:, 1], d[:, 3])
    do.axpy(r(1), R2, a2, u[:, 0])
    do.axpy(r(3), -R2, a2, u[:, 0])
    do.axpy(w(1), R2, b2, u[:, 4])
    do.axpy(w(3), R2, b2, u[:, 4], ALU.subtract)
    do.scale(r(5), a3, C3)
    do.scale(w(5), b3, C1)
    do.scale(r(7), a3, C1)
    do.scale(w(7), b3, C3)
    do.level()
    do.add(r(0), Tm[:, 14], Tm[:, 15])
    do.sub(w(0), Tm[:, 14], Tm[:, 15])
    do.axpy(r(6), -R2, r(2), d[:, 0])
    do.axpy(w(6), R2, w(2), d[:, 2], ALU.subtract)
    do.axpy(Tm[:, 9], C3, a1, r(7), ALU.subtract)
    do.axpy(Tm[:, 10], C1, a1, r(5))
    do.axpy(Tm[:, 12], C3, b1, w(5))
    do.axpy(Tm[:, 13], C1, b1, w(7), ALU.subtract)
    do.level()
    do.axpy(r(2), R2, r(2), d[:, 0])
    do.axpy(w(2), R2, w(2), d[:, 2])
    do.sub(r(7), r(1), Tm[:, 10])
    do.sub(r(5), r(3), Tm[:, 9])
    do.sub(w(7), Tm[:, 12], w(1))
    do.sub(w(5), Tm[:, 13], w(3))
    do.level()
    do.add(r(1), r(1), Tm[:, 10])
    do.add(r(3), r(3), Tm[:, 9])
    do.add(w(1), Tm[:, 12], w(1))
    do.add(w(3), Tm[:, 13], w(3))


def butterfly_back(do, J, Q, Tm, y):
    def q(k):
        return Q[:, k, 0]

    def v(k):
        return Q[:, k, 1]

    def t(i):
        return Tm[:, i]
    if J == 2:
        do.add(t(0), q(0), v(0))
        do.sub(t(1), q(0), v(0))
        do.level()
        do.add(y[:, 0:2], Tm[:, 0:2], Q[:, 1])
        do.level()
        return
    for at, k in ((0, 1), (4, 3), (10, 2)):
        do.add(Tm[:, at:at + 2], Q[:, k], Q[:, 8 - k])
        do.sub(Tm[:, at + 2:at + 4], Q[:, k], Q[:, 8 - k])
    do.add(t(8), q(0), v(0))
    do.sub(t(9), q(0), v(0))
    do.level()
    do.add(Q[:, 0], Tm[:, 8:10], Q[:, 4])
    do.sub(Q[:, 1], Tm[:, 8:10], Q[:, 4])
    do.scale(t(14), t(12), R2)
    do.add(q(2), t(0), t(4))
    do.sub(v(2), t(3), t(7))
    do.sub(q(3), t(0), t(4))
    do.add(v(3), t(3), t(7))
    do.scale(q(5), t(6), C3)
    do.scale(v(5), t(6), C1)
    do.scale(q(6), t(5), C1)
    do.scale(v(6), t(5), C3)
    do.level()
    do.axpy(q(7), C1, t(2), q(5))
    do.axpy(v(7), C3, t(2), v(5), ALU.subtract)
    do.axpy(t(15), C3, t(1), q(6))
    do.axpy(t(5), C1, t(1), v(6), ALU.subtract)
    do.axpy(t(8), R2, t(11), t(14))
    do.axpy(t(9), R2, t(11), t(14), ALU.subtract)
    do.add(y[:, 0], q(0), t(10))
    do.sub(y[:, 4], q(0), t(10))
    do.add(y[:, 2], q(1), t(13))
    do.sub(y[:, 6], q(1), t(13))
    do.add(t(0), q(3), v(3))
    do.sub(t(4), v(3), q(3))
    do.level()
    do.add(t(1), q(7), t(15))
    do.sub(t(2), t(15), q(7))
    do.add(t(3), v(7), t(5))
    do.sub(t(6), t(5), v(7))
    do.add(y[:, 1], v(0), t(8))
    do.sub(y[:, 5], v(0), t(8))
    do.add(y[:, 3], v(1), t(9))
    do.sub(y[:, 7], v(1), t(9))
    do.add(y[:, 0], y[:, 0], q(2))
    do.add(y[:, 4], y[:, 4], v(2))
    do.axpy(y[:, 2], R2, t(0), y[:, 2])
    do.axpy(y[:, 6], R2, t(4), y[:, 6])
    do.level()
    do.add(y[:, 1], y[:, 1], t(1))
    do.add(y[:, 7], y[:, 7], t(2))
    do.add(y[:, 3], y[:, 3], t(3))
    do.add(y[:, 5], y[:, 5], t(6))
    do.level()


def filter_stage(nc, tag, J, tri, feat_d, decay_d, fwd_d, w1_d, b1_d, w2_d, b2_d, w3_d, b3_d, freq_d, bias_d, kf_d):
    n = J * P
    with stage(nc, tag + "mlp_in", tag + "w3_in", tag + "mat_in", tag + "bias_in", tag + "dec0_in", tag + "dec1_in", tag + "mlp_mm", tag + "mlp_step", tag + "sin_done",
               tag + "w_step", tag + "eo_mm", tag + "eo_ready", tag + "fixed", tag + "squared", tag + "sq_added", tag + "norm_mm", tag + "norm_step",
               tag + "dft_step", tag + "r_ready", tag + "kept", tag + "k_mm", tag + "k_read", tag + "k_step", tag + "stored") as (ctx, sems):
        (mlp_in, w3_in, mat_in, bias_in, dec0_in, dec1_in, mlp_mm, mlp_step, sin_done, w_step, eo_mm, eo_ready, fixed, squared, sq_added, norm_mm, norm_step,
         dft_step, r_ready, kept, k_mm, k_read, k_step, stored) = sems
        dec_in = (dec0_in, dec1_in)
        feat = sb(nc, ctx, tag + "feat", [EMB, n])
        w1 = sb(nc, ctx, tag + "w1", [EMB, HID])
        w2 = sb(nc, ctx, tag + "w2", [HID, HID])
        vec = sb(nc, ctx, tag + "vec", [HID, 3])
        hid = sb(nc, ctx, tag + "hid", [HID + 1, 2, n])
        w3 = sb(nc, ctx, tag + "w3", [HID + 1, 2, ORDER, HYW])
        w3eo = sb(nc, ctx, tag + "w3eo", [HID + 1, 2, ORDER, HYW])
        mats = sb(nc, ctx, tag + "mats", [P, 4 * J + 2, P])
        dec = sb(nc, ctx, tag + "dec", [P, 2, HYW])
        eo = sb(nc, ctx, tag + "eo", [P, 2, J, HYW])
        sq = sb(nc, ctx, tag + "sq", [P, 2, 2, HYW])
        acc = sb(nc, ctx, tag + "acc", [P, HYW])
        rs = sb(nc, ctx, tag + "rs", [P, HYW])
        bias = sb(nc, ctx, tag + "bias", [P, ORDER, HYW])
        R = sb(nc, ctx, tag + "R", [P, J, 2, HYW])
        Tm = sb(nc, ctx, tag + "Tm", [P, 2 * J, HYW])
        pre = Tm[0:HID, 0:2 * n // HYW or 1].rearrange("p a b -> p (a b)")[:, 0:2 * n].rearrange("p (a b) -> p a b", a=2)
        keep = sb(nc, ctx, tag + "keep", [P, HYW])
        K = sb(nc, ctx, tag + "K", [P, 2 * J + 1, HYW])
        cst = sb(nc, ctx, tag + "cst", [P, 1])
        pE = ps(nc, ctx, tag + "pE", 4 * BANK)
        pN = ps(nc, ctx, tag + "pN", BANK)
        pK = ps(nc, ctx, tag + "pK", 2 * BANK)
        half = n // 2 if n > BANK else n

        with nc.Block() as block:
            @block.sync
            def _(sp):
                sp.dma_start(feat[:], feat_d).then_inc(mlp_in, 16)
                sp.dma_start(w1[:], w1_d).then_inc(mlp_in, 16)
                sp.dma_start(w2[:], w2_d).then_inc(mlp_in, 16)
                for i, v in enumerate((b1_d, b2_d, freq_d)):
                    sp.dma_start(vec[:, i:i + 1], v.rearrange("(p a) -> p a", a=1)).then_inc(mlp_in, 16)
                sp.dma_start(w3[0:HID].rearrange("p a o n -> p (a o n)"), w3_d).then_inc(w3_in, 16)
                sp.dma_start(w3[HID:HID + 1].rearrange("p a o n -> p (a o n)"), b3_d.rearrange("(a n) -> a n", a=1)).then_inc(w3_in, 16)
                sp.dma_start(mats[:], fwd_d).then_inc(mat_in, 16)
                sp.dma_start(bias[:], bias_d.partition_broadcast(P)).then_inc(bias_in, 16)
                for i in range(ORDER * J):
                    if i >= 2:
                        sp.wait_ge(eo_ready, i - 1)
                    sp.dma_start(dec[:, i % 2], decay_d[:, i % J]).then_inc(dec_in[i % 2], 16)
                for o in range(ORDER):
                    sp.wait_ge(k_step, 3 * (o + 1))
                    sp.dma_start(kf_d[o], K[:]).then_inc(stored, 16)
                sp.wait_ge(stored, 16 * ORDER)

            @block.tensor
            def _(pe):
                pe.wait_ge(mlp_in, 96)
                for c in range(0, n, half):
                    mm = pe.matmul(pE[0:HID, c:c + half], w1[:], feat[:, c:c + half], start=True, stop=True)
                mm.then_inc(mlp_mm, 1)
                pe.wait_ge(sin_done, 1)
                for c in range(0, n, half):
                    mm = pe.matmul(pE[0:HID, c:c + half], w2[:], hid[0:HID, 0, c:c + half], start=True, stop=True)
                mm.then_inc(mlp_mm, 1)
                pe.wait_ge(sin_done, 2)
                pe.wait_ge(w_step, 3)
                pe.wait_ge(mat_in, 16)
                for o in range(ORDER):
                    for j in range(J):
                        i = o * J + j
                        if i >= 2:
                            pe.wait_ge(eo_ready, i - 1)
                        for e in range(2):
                            b = (2 * (i % 2) + e) * BANK
                            mm = pe.matmul(pE[:, b:b + HYW], hid[:, 1, j * P:(j + 1) * P], w3eo[:, e, o], start=True, stop=True)
                        mm.then_inc(eo_mm, 1)
                    pe.wait_ge(sq_added, 2 * J * (o + 1))
                    pe.matmul(pN[:, 0:HYW], tri[:, 2], acc[:], start=True, stop=True).then_inc(norm_mm, 1)
                    for e in range(2):
                        pe.wait_ge(r_ready, 2 * o + e + 1)
                        if e:
                            pe.wait_ge(kept, o + 1)
                        for k in range(J):
                            i = (2 * o + e) * J + k
                            if i >= 2:
                                pe.wait_ge(k_read, i - 1)
                            out = pK[:, (i % 2) * BANK:(i % 2) * BANK + HYW]
                            if e and k == 0:
                                pe.matmul(out, mats[:, 4 * J], R[:, 0, 0], start=True, stop=False)
                                pe.matmul(out, mats[:, 4 * J + 1], keep[:], start=False, stop=False)
                            else:
                                pe.matmul(out, mats[:, 4 * k + 2 * e], R[:, k, 0], start=True, stop=False)
                            pe.matmul(out, mats[:, 4 * k + 2 * e + 1], R[:, k, 1], start=False, stop=True).then_inc(k_mm, 1)

            @block.scalar
            def _(act):
                for i in range(2):
                    act.wait_ge(mlp_step, 6 * (i + 1))
                    act.activation(hid[0:HID, i], pre[:, 0], ACT.Sin).then_inc(sin_done, 1)
                for o in range(ORDER):
                    for j in range(J):
                        i = o * J + j
                        act.wait_ge(eo_ready, i + 1)
                        if j == 0:
                            act.wait_ge(fixed, 3 * (o + 1))
                        if i >= 2:
                            act.wait_ge(sq_added, 2 * (i - 1))
                        act.activation(sq[:, i % 2], eo[:, :, j], ACT.Square).then_inc(squared, 1)
                    act.wait_ge(norm_mm, o + 1)
                    act.activation(rs[:], pN[:, 0:HYW], ACT.Ln, scale=0.5, bias=cst[:, 0:1]).then_inc(norm_step, 1)
                    act.wait_ge(norm_step, 2 * o + 1)
                    act.activation(rs[:], rs[:], ACT.Exp, scale=-0.5).then_inc(norm_step, 1)
                    act.wait_ge(r_ready, 2 * o + 1)
                    act.activation(keep[:], R[:, 0, 0], ACT.Copy).then_inc(kept, 1)

            @block.gpsimd
            def _(pool):
                for i in range(ORDER * J):
                    pool.wait_ge(squared, i + 1)
                    if i % J == 0:
                        if i:
                            pool.wait_ge(norm_mm, i // J)
                        pool.tensor_tensor(acc[:], sq[:, i % 2, 0], sq[:, i % 2, 1], ALU.add).then_inc(sq_added, 2)
                    else:
                        for e in range(2):
                            pool.wait_ge(sq_added, 2 * i + e)
                            pool.tensor_tensor(acc[:], acc[:], sq[:, i % 2, e], ALU.add).then_inc(sq_added, 1)

            @block.vector
            def _(dve):
                dve.memset(cst[:], RMS_EPS)
                dve.memset(hid[HID:HID + 1, 1], 1.0).then_inc(w_step, 1)
                for i in range(2):
                    dve.wait_ge(mlp_in, 96)
                    dve.wait_ge(mlp_mm, i + 1)
                    m = 6 * i
                    dve.tensor_scalar(pre[:, 0], pE[0:HID, 0:n], vec[:, i:i + 1], vec[:, 2:3], ALU.add, ALU.mult).then_inc(mlp_step, 1)
                    dve.wait_ge(mlp_step, m + 1)
                    dve.tensor_scalar(pre[:, 1], pre[:, 0], 1.0 / (2 * math.pi), SIN_RANGE, ALU.mult, ALU.add).then_inc(mlp_step, 1)
                    dve.wait_ge(mlp_step, m + 2)
                    dve.tensor_scalar(pre[:, 1], pre[:, 1], SIN_RANGE, None, ALU.subtract).then_inc(mlp_step, 1)
                    dve.wait_ge(mlp_step, m + 3)
                    dve.scalar_tensor_tensor(pre[:, 0], pre[:, 1], -6.28125, pre[:, 0], ALU.mult, ALU.add).then_inc(mlp_step, 1)
                    dve.wait_ge(mlp_step, m + 4)
                    dve.scalar_tensor_tensor(pre[:, 0], pre[:, 1], -(2 * math.pi - 6.28125), pre[:, 0], ALU.mult, ALU.add).then_inc(mlp_step, 1)
                    dve.wait_ge(mlp_step, m + 5)
                    dve.tensor_scalar(pre[:, 0], pre[:, 0], 3.1415925, -3.1415925, ALU.min, ALU.max).then_inc(mlp_step, 1)
                    if i == 0:
                        dve.wait_ge(w3_in, 32)
                        dve.tensor_tensor(w3eo[:, 0], w3[:, 0], w3[:, 1], ALU.add).then_inc(w_step, 1)
                        dve.tensor_tensor(w3eo[:, 1], w3[:, 0], w3[:, 1], ALU.subtract).then_inc(w_step, 1)
                        dve.wait_ge(sin_done, 1)
                dve.wait_ge(bias_in, 16)
                do = Steps(dve, dft_step)
                for o in range(ORDER):
                    for j in range(J):
                        i = o * J + j
                        dve.wait_ge(dec_in[i % 2], 16 * (i // 2 + 1))
                        dve.wait_ge(eo_mm, i + 1)
                        if o:
                            dve.wait_ge(squared, o * J)
                            dve.wait_ge(r_ready, 2 * o)
                        out = eo[:, :, j]
                        b = 2 * (i % 2) * BANK
                        dve.tensor_tensor(out, pE[:, b:b + 2 * BANK].rearrange("p (e n) -> p e n", e=2),
                                          dec[:, i % 2].unsqueeze(1).to_broadcast([P, 2, HYW]), ALU.mult).then_inc(eo_ready, 1)
                        if j == 0:
                            dve.wait_ge(eo_ready, i + 1)
                            dve.tensor_tensor(eo[0:1, 0, 0], eo[0:1, 0, 0], eo[0:1, 1, 0], ALU.add).then_inc(fixed, 1)
                            dve.wait_ge(fixed, 3 * o + 1)
                            dve.tensor_scalar(eo[0:1, 1, 0], eo[0:1, 0, 0], 0.5, None, ALU.mult).then_inc(fixed, 1)
                            dve.wait_ge(fixed, 3 * o + 2)
                            dve.tensor_scalar(eo[0:1, 0, 0], eo[0:1, 0, 0], 0.5, None, ALU.mult).then_inc(fixed, 1)
                    dve.wait_ge(eo_ready, (o + 1) * J)
                    dve.wait_ge(fixed, 3 * (o + 1))
                    for e in range(2):
                        if o or e:
                            dve.wait_ge(k_mm, (2 * o + e) * J)
                            dve.wait_ge(kept, o + e)
                        butterfly(do, J, eo[:, e], R, Tm)
                        do.level()
                        dve.sem_inc(r_ready, 1)
                        if e == 0:
                            dve.wait_ge(norm_step, 2 * (o + 1))
                            if o:
                                dve.wait_ge(stored, 16 * o)
                        for k in range(J):
                            i = (2 * o + e) * J + k
                            dve.wait_ge(k_mm, i + 1)
                            dve.tensor_tensor(K[:, 2 * k + e], pK[:, (i % 2) * BANK:(i % 2) * BANK + HYW], rs[:], ALU.mult).then_inc(k_read, 1)
                            if e == 0:
                                dve.wait_ge(k_read, i + 1)
                                do.add(K[:, 2 * k], K[:, 2 * k], bias[:, o])
                    dve.wait_ge(k_read, (2 * o + 2) * J)
                    do.level()
                    dve.tensor_copy(K[:, 2 * J], K[:, 0]).then_inc(k_step, 1)
                    dve.wait_ge(k_step, 3 * o + 1)
                    dve.tensor_tensor(K[0:1, 2 * J], K[0:1, 1], bias[0:1, o], ALU.add).then_inc(k_step, 1)
                    dve.wait_ge(k_step, 3 * o + 2)
                    dve.memset(K[0:1, 1], 0.0).then_inc(k_step, 1)


def hyena_stage(nc, tag, J, tok0, ident, hp_d, gate_d, kf_d, fwd_d, inv_d, o_d):
    n = J * P
    CTS = HYW // P
    with stage(nc, tag + "v_in", tag + "x1_in", tag + "x2_in", tag + "g_in", tag + "mats_in", tag + "k0_in", tag + "k1_in", tag + "turned", tag + "tok_ready",
               tag + "dft_step", tag + "r_ready", tag + "x_mm", tag + "x_read", tag + "prod_step", tag + "y_ready", tag + "q_mm", tag + "q_ready",
               tag + "z_step", tag + "gate_ready", tag + "out_ready", tag + "stored") as (ctx, sems):
        (v_in, x1_in, x2_in, g_in, mats_in, k0_in, k1_in, turned, tok_ready, dft_step, r_ready, x_mm, x_read, prod_step, y_ready, q_mm, q_ready,
         z_step, gate_ready, out_ready, stored) = sems
        fwd = sb(nc, ctx, tag + "fwd", [P, 4 * J, P])
        inv = sb(nc, ctx, tag + "inv", [P, 4 * J, P])
        u = sb(nc, ctx, tag + "u", [P, J, HYW])
        x1 = sb(nc, ctx, tag + "x1", [P, J, HYW])
        xg = sb(nc, ctx, tag + "xg", [P, CTS, n])
        R = sb(nc, ctx, tag + "R", [P, J, 2, HYW])
        Tm = sb(nc, ctx, tag + "Tm", [P, 16, HYW])
        K = sb(nc, ctx, tag + "K", [P, 2 * J + 1, HYW])
        pX = ps(nc, ctx, tag + "pX", 4 * BANK)
        pQ = ps(nc, ctx, tag + "pQ", 4 * BANK)
        x1T = Tm[:, 0:J].rearrange("p j n -> p (j n)").rearrange("p (c t) -> p c t", c=CTS)
        gT = x1[:].rearrange("p j n -> p (j n)").rearrange("p (c t) -> p c t", c=CTS)
        k_in = (k0_in, k1_in)

        def rows(first):
            return hp_d[first:first + HYW, tok0:tok0 + n].rearrange("(c p) t -> p c t", p=P)

        with nc.Block() as block:
            @block.sync
            def _(sp):
                sp.dma_start(xg[:], rows(0)).then_inc(v_in, 16)
                sp.dma_start(x1T, rows(HYW)).then_inc(x1_in, 16)
                sp.dma_start(fwd[:], fwd_d[:, 0:4 * J]).then_inc(mats_in, 16)
                sp.dma_start(K[:], kf_d[0]).then_inc(k_in[0], 16)
                sp.dma_start(inv[:], inv_d).then_inc(mats_in, 16)
                sp.wait_ge(tok_ready, 2 * J)
                sp.dma_start(xg[:], rows(2 * HYW)).then_inc(x2_in, 16)
                sp.wait_ge(y_ready, J)
                sp.dma_start(K[:], kf_d[1]).then_inc(k_in[1], 16)
                sp.wait_ge(z_step, 1)
                sp.dma_start(gT, gate_d[:, tok0:tok0 + n].rearrange("(c p) t -> p c t", p=P)).then_inc(g_in, 16)
                sp.wait_ge(out_ready, 1)
                sp.dma_start(o_d[1536:1536 + HYW, tok0:tok0 + n].rearrange("(c p) t -> p c t", p=P), xg[:]).then_inc(stored, 16)
                sp.wait_ge(stored, 16)

            @block.tensor
            def _(pe):
                pe.wait_ge(v_in, 16)
                for src, first in ((xg, 0), (x1T, J)):
                    if first:
                        pe.wait_ge(x1_in, 16)
                    for j in range(J):
                        i = first + j
                        if i >= 2:
                            pe.wait_ge(tok_ready, i - 1)
                        for ct in range(CTS):
                            b = (i % 2) * BANK + ct * P
                            mm = pe.transpose(pX[:, b:b + P], src[:, ct, j * P:(j + 1) * P], ident[:, :])
                        mm.then_inc(turned, 1)
                pe.wait_ge(mats_in, 32)

                def forward(i):
                    o, k = divmod(i, J)
                    if k == 0:
                        pe.wait_ge(r_ready, o + 1)
                        pe.wait_ge(tok_ready, 2 * J)
                    if i >= 2:
                        pe.wait_ge(x_read, 2 * (i - 1))
                    b = 2 * (i % 2) * BANK
                    for part in range(2):
                        out = pX[:, b + part * BANK:b + part * BANK + HYW]
                        pe.matmul(out, fwd[:, 4 * k + 2 * part], R[:, k, 0], start=True, stop=False)
                        mm = pe.matmul(out, fwd[:, 4 * k + 2 * part + 1], R[:, k, 1], start=False, stop=True)
                    mm.then_inc(x_mm, 1)

                def backward(i):
                    o, k = divmod(i, J)
                    pe.wait_ge(y_ready, i + 1)
                    if i >= 2:
                        pe.wait_ge(q_ready, i - 1)
                    b = 2 * (i % 2) * BANK
                    for part in range(2):
                        at = b + part * BANK
                        m1, m2 = inv[:, 4 * k + 2 * part], inv[:, 4 * k + 2 * part + 1]
                        if o == 0:
                            pe.matmul(pQ[:, at:at + HYW], m1, R[:, k, 0], start=True, stop=False)
                            mm = pe.matmul(pQ[:, at:at + HYW], m2, R[:, k, 1], start=False, stop=True)
                        else:
                            for ct in range(CTS):
                                out = pQ[:, at + ct * P:at + (ct + 1) * P]
                                pe.matmul(out, R[:, k, 0, ct * P:(ct + 1) * P], m1, start=True, stop=False)
                                mm = pe.matmul(out, R[:, k, 1, ct * P:(ct + 1) * P], m2, start=False, stop=True)
                    mm.then_inc(q_mm, 1)

                for o in range(ORDER):
                    for k in range(J + 1):
                        if k < J:
                            forward(o * J + k)
                        if k >= 1:
                            backward(o * J + k - 1)

            @block.scalar
            def _(act):
                for i in range(2 * J):
                    act.wait_ge(turned, i + 1)
                    dst = u[:, i] if i < J else x1[:, i - J]
                    act.activation(dst, pX[:, (i % 2) * BANK:(i % 2) * BANK + HYW], ACT.Copy).then_inc(tok_ready, 1)
                for i in range(ORDER * J):
                    act.wait_ge(q_mm, i + 1)
                    b = 2 * (i % 2) * BANK
                    act.activation(R[:, i % J].rearrange("p a n -> p (a n)"), pQ[:, b:b + 2 * BANK], ACT.Copy).then_inc(q_ready, 1)

            @block.vector
            def _(dve):
                do = Steps(dve, dft_step)
                dve.wait_ge(tok_ready, 2 * J)
                for o in range(ORDER):
                    butterfly(do, J, u[:], R, Tm)
                    do.level()
                    dve.sem_inc(r_ready, 1)
                    dve.wait_ge(k_in[o], 16)
                    for k in range(J):
                        i = o * J + k
                        t = Tm[:, 4 * (i % 2):4 * (i % 2) + 4]
                        x = pX[:, 2 * (i % 2) * BANK:2 * (i % 2 + 1) * BANK].rearrange("p (a n) -> p a n", a=2)
                        kr, ki = K[:, 2 * k], K[:, 2 * k + 1]
                        dve.wait_ge(x_mm, i + 1)
                        if i >= 2:
                            dve.wait_ge(y_ready, i - 1)
                        if k == 0:
                            dve.tensor_tensor(t[:, 0], x[:, 0], kr, ALU.mult).then_inc(prod_step, 1)
                            dve.tensor_tensor(t[:, 1], x[:, 1], K[:, 2 * J], ALU.mult).then_inc(prod_step, 1)
                        else:
                            dve.tensor_tensor(t[:, 0:2], x, kr.unsqueeze(1).to_broadcast([P, 2, HYW]), ALU.mult).then_inc(prod_step, 2)
                        dve.tensor_tensor(t[:, 2:4], x, ki.unsqueeze(1).to_broadcast([P, 2, HYW]), ALU.mult).then_inc(x_read, 2)
                        dve.wait_ge(prod_step, 3 * i + 2)
                        dve.wait_ge(x_read, 2 * i + 2)
                        dve.tensor_tensor(R[:, k, 0], t[:, 0], t[:, 3], ALU.subtract).then_inc(prod_step, 1)
                        dve.tensor_tensor(R[:, k, 1], t[:, 1], t[:, 2], ALU.add).then_inc(y_ready, 1)
                    dve.wait_ge(prod_step, 3 * (o + 1) * J)
                    dve.wait_ge(y_ready, (o + 1) * J)
                    dve.wait_ge(q_ready, (o + 1) * J)
                    butterfly_back(do, J, R, Tm, u)
                    if o == 0:
                        dve.tensor_tensor(u[:], u[:], x1[:], ALU.mult).then_inc(z_step, 1)
                        dve.wait_ge(z_step, 1)
                    else:
                        dve.wait_ge(x2_in, 16)
                        dve.wait_ge(g_in, 16)
                        dve.tensor_tensor(xg[:], xg[:], gT, ALU.mult).then_inc(gate_ready, 1)
                        dve.wait_ge(gate_ready, 1)
                        x4 = xg[:].rearrange("p c (j q) -> p j c q", q=P)
                        dve.tensor_tensor(x4, x4, u[:].rearrange("p j (c q) -> p j c q", q=P), ALU.mult).then_inc(out_ready, 1)


def output_stage(nc, tag, first_tile, tri, o_d, w_out, norm_w, mod_d, ln_g, ln_b, h_lat, h_ctx, dst_lat, dst_ctx):
    tiles = list(range(first_tile, TT))
    NT = len(tiles)
    with stage(nc, tag + "w0_in", tag + "w1_in", tag + "vec_in", tag + "o0_in", tag + "o1_in", tag + "h0_in", tag + "h1_in", tag + "w_scaled", tag + "squared",
               tag + "sq_mm", tag + "out_mm", tag + "ms_ready", tag + "rms_ready", tag + "a_read", tag + "b_read", tag + "h_read", tag + "step",
               tag + "var_ready", tag + "std_ready", tag + "done", tag + "stored0", tag + "stored1") as (ctx, sems):
        (w0_in, w1_in, vec_in, o0_in, o1_in, h0_in, h1_in, w_scaled, squared, sq_mm, out_mm, ms_ready, rms_ready, a_read, b_read, h_read, step,
         var_ready, std_ready, done, stored0, stored1) = sems
        o_in, h_in, stored = (o0_in, o1_in), (h0_in, h1_in), (stored0, stored1)
        w = sb(nc, ctx, tag + "w", [P, KM, D])
        nw = sb(nc, ctx, tag + "nw", [P, SSD_TILES])
        oT = sb(nc, ctx, tag + "oT", [P, 2, KM, P])
        sq = sb(nc, ctx, tag + "sq", [P, 2, SSD_TILES, P])
        h = sb(nc, ctx, tag + "h", [P, 2, D])
        r = sb(nc, ctx, tag + "r", [P, 2, D])
        gate = sb(nc, ctx, tag + "gate", [P, 2, D])
        gb = sb(nc, ctx, tag + "gb", [P, 2, D])
        st = sb(nc, ctx, tag + "st", [P, 2, 6])
        mv = sb(nc, ctx, tag + "mv", [P, 8])
        pA = ps(nc, ctx, tag + "pA", 2 * BANK)
        pB = ps(nc, ctx, tag + "pB", 2 * BANK)
        pR = ps(nc, ctx, tag + "pR", BANK)

        with nc.Block() as block:
            @block.sync
            def _(sp):
                def load(i):
                    t = tiles[i]
                    src = h_ctx[t * P:(t + 1) * P] if t < CT else h_lat[(t - CT) * P:(t - CT + 1) * P]
                    sp.dma_start(h[:, i % 2], src).then_inc(h_in[i % 2], 16)
                    sp.dma_start(oT[:, i % 2], o_d[:, t * P:(t + 1) * P].rearrange("(k p) t -> p k t", p=P)).then_inc(o_in[i % 2], 16)

                with nc.allow_non_contiguous_dma(reason="a vector onto the partitions"):
                    sp.dma_start(nw[:], norm_w.rearrange("(k p) -> p k", p=P)).then_inc(vec_in, 16)
                sp.dma_start(w[:, 0:SSD_TILES], w_out[0:SSD_TILES * P].rearrange("(k p) n -> p k n", p=P)).then_inc(w0_in, 16)
                load(0)
                for i in range(2):
                    sp.dma_start(gate[:, i], mod_d[i].partition_broadcast(P)).then_inc(vec_in, 16)
                sp.dma_start(gb[:, 0], ln_g.partition_broadcast(P)).then_inc(vec_in, 16)
                sp.dma_start(gb[:, 1], ln_b.partition_broadcast(P)).then_inc(vec_in, 16)
                sp.dma_start(w[:, SSD_TILES:], w_out[SSD_TILES * P:].rearrange("(k p) n -> p k n", p=P)).then_inc(w1_in, 16)
                load(1)
                for i in range(2, NT):
                    sp.wait_ge(h_read, i - 1)
                    load(i)

            @block.tensor
            def _(pe):
                for i in range(NT):
                    s = i % 2
                    pe.wait_ge(squared, i + 1)
                    if i:
                        pe.wait_ge(ms_ready, i)
                    for k in range(SSD_TILES):
                        mm = pe.matmul(pR[:, 0:1], sq[:, s, k], tri[:, 2, 0:1], start=(k == 0), stop=(k == SSD_TILES - 1))
                    mm.then_inc(sq_mm, 1)
                    if i == 0:
                        pe.wait_ge(w_scaled, SSD_TILES)
                    else:
                        pe.wait_ge(a_read, i)
                    for acc, first, last in ((pA, 0, SSD_TILES), (pB, SSD_TILES, KM)):
                        if first:
                            if i == 0:
                                pe.wait_ge(w1_in, 16)
                            else:
                                pe.wait_ge(b_read, i)
                        for k in range(first, last):
                            for c in range(0, D, BANK):
                                mm = pe.matmul(acc[:, c:c + BANK], oT[:, s, k], w[:, k, c:c + BANK], start=(k == first), stop=(k == last - 1))
                        mm.then_inc(out_mm, 1)

            @block.scalar
            def _(act):
                def ln_std(i):
                    act.wait_ge(var_ready, i + 1)
                    act.activation(mv[:, 6:7], mv[:, 5:6], ACT.Sqrt).then_inc(std_ready, 1)

                def store(i):
                    t = tiles[i]
                    dst = dst_ctx[t * P:(t + 1) * P] if t < CT else dst_lat[(t - CT) * P:(t - CT + 1) * P]
                    act.wait_ge(done, i + 1)
                    act.dma_start(dst, r[:, i % 2]).then_inc(stored[i % 2], 16)

                def square(i):
                    act.wait_ge(o_in[i % 2], 16 * (i // 2 + 1))
                    if i >= 2:
                        act.wait_ge(sq_mm, i - 1)
                    act.activation(sq[:, i % 2], oT[:, i % 2, 0:SSD_TILES], ACT.Square).then_inc(squared, 1)

                square(0)
                for i in range(NT):
                    act.wait_ge(ms_ready, i + 1)
                    act.activation(mv[:, 1:2], mv[:, 0:1], ACT.Sqrt).then_inc(rms_ready, 1)
                    if i + 1 < NT:
                        square(i + 1)
                    ln_std(i)
                    store(i)
                for s in range(2):
                    act.wait_ge(stored[s], 16 * (NT // 2))

            @block.vector
            def _(dve):
                dve.wait_ge(vec_in, 80)
                dve.wait_ge(w0_in, 16)
                for k in range(SSD_TILES):
                    dve.tensor_scalar(w[:, k], w[:, k], nw[:, k:k + 1], None, ALU.mult).then_inc(w_scaled, 1)
                n = 0
                for i, t in enumerate(tiles):
                    s = i % 2
                    dve.wait_ge(sq_mm, i + 1)
                    dve.tensor_scalar(mv[:, 0:1], pR[:, 0:1], 1.0 / (SSD_TILES * P), RMS_EPS, ALU.mult, ALU.add).then_inc(ms_ready, 1)
                    dve.wait_ge(rms_ready, i + 1)
                    dve.reciprocal(mv[:, 2:3], mv[:, 1:2]).then_inc(step, 1)
                    dve.wait_ge(step, n + 1)
                    dve.wait_ge(out_mm, 2 * i + 1)
                    if i >= 2:
                        dve.wait_ge(stored[s], 16 * (i // 2))
                    dve.tensor_scalar(r[:, s], pA[:, :], mv[:, 2:3], None, ALU.mult).then_inc(a_read, 1)
                    dve.wait_ge(a_read, i + 1)
                    dve.wait_ge(out_mm, 2 * i + 2)
                    dve.tensor_tensor(r[:, s], r[:, s], pB[:, :], ALU.add).then_inc(b_read, 1)
                    dve.wait_ge(b_read, i + 1)
                    dve.tensor_tensor(r[:, s], r[:, s], gate[:, (t >= CT) * 1], ALU.mult).then_inc(step, 1)
                    dve.wait_ge(step, n + 2)
                    dve.wait_ge(h_in[s], 16 * (i // 2 + 1))
                    dve.scalar_tensor_tensor(r[:, s], h[:, s], ALPHA, r[:, s], ALU.mult, ALU.add).then_inc(h_read, 1)
                    dve.wait_ge(h_read, i + 1)
                    for c in range(2):
                        dve.bn_stats(st[:, c], r[:, s, c * BANK:(c + 1) * BANK]).then_inc(step, 1)
                    dve.wait_ge(step, n + 4)
                    dve.bn_aggr(mv[:, 3:5], st[:]).then_inc(step, 1)
                    dve.wait_ge(step, n + 5)
                    dve.tensor_scalar(mv[:, 5:6], mv[:, 4:5], LN_EPS, None, ALU.add).then_inc(var_ready, 1)
                    dve.wait_ge(std_ready, i + 1)
                    dve.reciprocal(mv[:, 7:8], mv[:, 6:7]).then_inc(step, 1)
                    dve.wait_ge(step, n + 6)
                    dve.tensor_scalar(r[:, s], r[:, s], mv[:, 3:4], mv[:, 7:8], ALU.subtract, ALU.mult).then_inc(step, 1)
                    dve.wait_ge(step, n + 7)
                    dve.tensor_tensor(r[:, s], r[:, s], gb[:, 0], ALU.mult).then_inc(step, 1)
                    dve.wait_ge(step, n + 8)
                    dve.tensor_tensor(r[:, s], r[:, s], gb[:, 1], ALU.add).then_inc(done, 1)
                    n += 8


def hybrid_backbone(nc, a, out):
    def dram(name, shape):
        return nc.dram_tensor(name, list(shape), F32, kind="Internal").ap()

    h_d = dram("h_d", [T, D])
    mod_d = dram("mod_d", [2, D])
    gate_z = dram("gate_z", [1024, T])
    xbc_d = dram("xbc_d", [2048, T])
    qk_d = dram("qk_d", [1024, T])
    v_d = dram("v_d", [T, HYW])
    gate_d = dram("gate_d", [512, T])
    hp_d = dram("hp_d", [1536, T])
    gate_h = dram("gate_h", [512, T])
    la_d = dram("la_d", [2 * HEADS, T])
    o_d = dram("o_d", [D_MIX, T])
    KF = {J: dram("kf%d_d" % J, [ORDER, P, 2 * J + 1, HYW]) for J in (CT, LAT // P)}

    with ExitStack() as ctx:
        ident = sb(nc, ctx, "ident", [P, P])
        swap = sb(nc, ctx, "swap", [P, P])
        tri = sb(nc, ctx, "tri", [P, 3, P])
        small = sb(nc, ctx, "small", [P, 4, TT, 2 * HEADS])
        with stage(nc, "const_in") as (_, (const_in,)):
            with nc.Block() as block:
                @block.sync
                def _(sp):
                    sp.dma_start(ident[:], a["c_ident"]).then_inc(const_in, 16)
                    sp.dma_start(swap[:], a["c_swap"]).then_inc(const_in, 16)
                    sp.dma_start(tri[:], a["c_tri"]).then_inc(const_in, 16)
                    sp.wait_ge(const_in, 48)

        for layer in range(DEPTH):
            need_ctx = layer < DEPTH - 1
            t0 = 0 if need_ctx else CTX
            g = "l%d_" % layer
            h_lat, h_ctx = (a["x"][0], a["ctx"][0]) if layer == 0 else (h_d[CTX:T], h_d[0:CTX])
            with ExitStack() as uctx:
                uT = sb(nc, uctx, g + "uT", [P, KD, T])
                norm_stage(nc, g + "n_", uT, ident, h_lat, h_ctx, a["c"], a["c_ctx"], a["w_ada"][layer], a["b_ada"][layer], mod_d)
                v_dt_stage(nc, g + "v_", uT, a["w_in"][layer], tri, ident, a["ssd_dt_bias"][layer], a["ssd_a_log"][layer], v_d, la_d, small)
                project_stage(nc, g + "pq_", uT, a["w_in"][layer],
                              [("rope", Q0, 1, t0, qk_d[0:512], None), ("rope", K0, 1, 0, qk_d[512:1024], None),
                               ("gate", GD0, 1, t0, gate_d, None), ("gate", Z0, 2, t0, gate_z, None), ("gate", GH0, 1, t0, gate_h, None)],
                              swap=swap, cos_d=a["c_cos"], sin_d=a["c_sin"])
                project_stage(nc, g + "px_", uT, a["w_in"][layer], [("conv_silu", XBC0, 4, 0, xbc_d, 0)],
                              a["ssd_conv_w"][layer], a["ssd_conv_b"][layer])
                project_stage(nc, g + "ph_", uT, a["w_in"][layer], [("conv", HP0, 3, t0, hp_d, 0)],
                              a["hy_conv_w"][layer], a["hy_conv_b"][layer])
            attention_stage(nc, g + "at_", layer, t0 // P, ident, tri, a["diff_lambda"][layer], qk_d, v_d, gate_d, o_d)
            ssd_stage(nc, g + "sd_", t0 // P, tri, ident, small, a["ssd_d"][layer], xbc_d, la_d, gate_z, o_d)
            for J, name, tok0, cols in ((LAT // P, "lat", CTX, slice(CTX, T)), (CT, "ctx", 0, slice(0, CTX))):
                if J == CT and not need_ctx:
                    continue
                first = tok0 // P
                filter_stage(nc, g + name + "f_", J, tri, a["c_feat"][:, cols], a["c_decay"][:, first:first + J], a["c_fwd_" + name],
                             a["hy_w1"][layer], a["hy_b1"][layer], a["hy_w2"][layer], a["hy_b2"][layer], a["hy_w3"][layer], a["hy_b3"][layer],
                             a["hy_freq"][layer], a["hy_bias"][layer], KF[J])
                hyena_stage(nc, g + name + "h_", J, tok0, ident, hp_d, gate_h, KF[J], a["c_fwd_" + name], a["c_inv_" + name], o_d)
            dst = h_d[CTX:T] if need_ctx else out[0]
            output_stage(nc, g + "o_", t0 // P, tri, o_d, a["w_out"][layer], a["ssd_norm_w"][layer], mod_d, a["ln_g"][layer], a["ln_b"][layer],
                         h_lat, h_ctx, dst, h_d[0:CTX])


INPUTS = ["x", "c", "ctx", "c_ctx", "w_ada", "b_ada", "w_in", "ssd_conv_w", "ssd_conv_b", "ssd_dt_bias", "ssd_a_log", "ssd_d",
          "ssd_norm_w", "diff_lambda", "hy_conv_w", "hy_conv_b", "hy_w1", "hy_b1", "hy_w2", "hy_b2", "hy_w3", "hy_b3",
          "hy_freq", "hy_bias", "w_out", "ln_g", "ln_b"]


def kernel(**inputs):
    import concourse.bacc as bacc
    from concourse.bass_utils import run_bass_kernel_spmd

    nc = bacc.Bacc("TRN2", target_bir_lowering=False, num_devices=1)
    arrays = {name: np.ascontiguousarray(inputs[name]) for name in INPUTS}
    arrays.update(constants())
    a = {name: nc.dram_tensor(name, list(v.shape), mybir.dt.from_np(v.dtype), kind="ExternalInput").ap() for name, v in arrays.items()}
    out = nc.dram_tensor("out", [1, LAT, D], F32, kind="ExternalOutput").ap()
    hybrid_backbone(nc, a, out)
    result = run_bass_kernel_spmd(nc, [arrays], core_ids=[0])
    return result.results[0]["out"]
```

```python
import math
from contextlib import ExitStack, contextmanager

import numpy as np

import concourse.bass as bass
from concourse import mybir

F32 = mybir.dt.float32
F32R = mybir.dt.float32r
ACT = mybir.ActivationFunctionType
ALU = mybir.AluOpType
AX = mybir.AxisListType

P = 128
D = 1024
KD = D // P
LAT, CTX = 1024, 256
T = CTX + LAT
TT = T // P
CT = CTX // P
DEPTH = 2
GRID_W = 64
HEADS, HD = 16, 64
GROUPS, HPG, NS = 4, 4, 128
AH, AD = 4, 64
HYW = 512
ORDER = 2
BANDS, EMB, HID = 16, 33, 64
D_MIX = 2048
KM = D_MIX // P
SSD_TILES = HEADS * HD // P
SCALE = AD ** -0.5
ALPHA = (2 * DEPTH) ** 0.25
LN_EPS, RMS_EPS = 1e-5, 1e-6
BANK = 512
GW = 512
SIN_RANGE = 1.5 * 2.0 ** 23

Z0, XBC0, DT0, Q0, K0, V0, GD0, HP0, GH0, N_IN = 0, 1024, 3072, 3104, 3616, 4128, 4640, 5152, 6688, 7200


def lam_init(layer):
    return 0.8 - 0.6 * math.exp(-0.3 * layer)


def rope_tables():
    freqs = AD // 4
    inv = 10000.0 ** (-np.arange(freqs) / freqs)
    tok = np.arange(LAT)
    row, col = tok // GRID_W, tok % GRID_W
    f = np.arange(P)
    pos = np.where((f % AD < AD // 2)[:, None], row[None], col[None])
    ang = pos * inv[f % freqs][:, None]
    sign = np.where(f % 32 < 16, -1.0, 1.0)[:, None]
    return np.cos(ang).astype(np.float32), (sign * np.sin(ang)).astype(np.float32)


def swap_matrix():
    f = np.arange(P)
    return (f[:, None] == (f[None] ^ 16)).astype(np.float32)


def triangles():
    s, l = np.arange(P)[:, None], np.arange(P)[None]
    return np.stack([s <= l, s >= l, s >= 0 * l], 1).astype(np.float32)


def filter_features(n):
    t = np.linspace(0.0, 1.0, n)[:, None]
    w = (2.0 * math.pi / n) * np.arange(n)[:, None]
    bands = np.linspace(1e-4, BANDS - 1, BANDS)
    return np.concatenate([t, np.cos(w * bands), -np.sin(w * bands)], -1).T.astype(np.float32)


def filter_decay(n):
    deltas = np.abs(np.linspace(math.log(1e-2) / 1.5, math.log(1e-2) / 0.3, HYW))
    t = np.linspace(0.0, 1.0, n)[:, None]
    return np.exp(-t * deltas).reshape(n // P, P, HYW).transpose(1, 0, 2).astype(np.float32)


def spectra_matrices(J):
    n = 2 * J * P
    p = np.arange(P)[:, None]
    fwd = np.zeros((P, 4 * J + 2, P))
    inv = np.zeros((P, 4 * J, P))
    for k in range(J):
        m = np.arange(P)[None]
        f = 2 * J * m + k if k else np.where(m < 64, 2 * J * m, 2 * J * (m - 64) + J)
        ang = 2 * math.pi * ((f * p) % n) / n
        c, s = np.cos(ang), np.sin(ang)
        if k:
            mats = [c, -s, -s, -c]
            back = [c.T, -s.T, -s.T, -c.T]
            back = [2.0 / n * b for b in back]
        else:
            lo = (m < 64) * 1.0
            alt = (-1.0) ** p
            third = -s * lo
            third[:, 0:1] = alt
            mats = [c * lo, c * (1 - lo), third, -s * (1 - lo)]
            weight = np.full((1, P), 2.0 / n)
            weight[0, 0] = 1.0 / n
            i1, i2 = (c * lo * weight).T, (-s * lo * weight).T
            i2[0:1] = alt.T / n
            back = [i1, i2, (c * (1 - lo) * 2 / n).T, (-s * (1 - lo) * 2 / n).T]
            without, only = third.copy(), np.zeros_like(third)
            without[:, 0] = 0
            only[:, 0:1] = alt
            fwd[:, 4 * J], fwd[:, 4 * J + 1] = without, only
        for i in range(4):
            fwd[:, 4 * k + i] = mats[i]
            inv[:, 4 * k + i] = back[i]
    return fwd.astype(np.float32), inv.astype(np.float32)


def constants():
    cos, sin = rope_tables()
    fl, il = spectra_matrices(LAT // P)
    fc, ic = spectra_matrices(CT)
    return {
        "c_ident": np.eye(P, dtype=np.float32),
        "c_cos": cos, "c_sin": sin, "c_swap": swap_matrix(), "c_tri": triangles(),
        "c_feat": np.concatenate([filter_features(CTX), filter_features(LAT)], 1),
        "c_decay": np.concatenate([filter_decay(CTX), filter_decay(LAT)], 1),
        "c_fwd_lat": fl, "c_inv_lat": il, "c_fwd_ctx": fc, "c_inv_ctx": ic,
    }


@contextmanager
def stage(nc, *names):
    with ExitStack() as ctx:
        sems = [ctx.enter_context(nc.semaphore(n)) for n in names]
        yield ctx, sems
        nums = sorted(s.num for s in sems)
        starts = [n for n in nums if n - 1 not in nums]
        for first in starts:
            last = first
            while last + 1 in nums:
                last += 1
            nc.all_engine_barrier(sems_to_clear=range(first, last + 1))


def sb(nc, ctx, name, shape, dtype=F32):
    return ctx.enter_context(nc.sbuf_tensor(name, list(shape), dtype))


def ps(nc, ctx, name, cols):
    return ctx.enter_context(nc.psum_tensor(name, [P, cols], F32))


PASSES = ((0, 0), (1, 0), (0, 1))


def halves(lo, n):
    return [(c, min(BANK, n - c)) for c in range(lo, n, BANK)]


def norm_stage(nc, tag, u_hi, u_lo, ident, src_lat, src_ctx, c, c_ctx, w_ada, b_ada, mod_dram):
    NCH = 3 * D // GW
    with stage(nc, tag + "c_in", tag + "wada0", tag + "wada1", tag + "bada", tag + "cond_ready",
               tag + "mod_mm", tag + "mod_ready", tag + "modT_mm", tag + "modT_ready",
               tag + "h_in_ctx", tag + "h_in_lat0", tag + "h_in_lat1", tag + "var_ready", tag + "std_ready", tag + "xn_ready",
               tag + "xT_ready", tag + "hi_ready", tag + "u_ready", tag + "lo_ready", tag + "dve_step", tag + "stored") as (ctx, sems):
        (c_in, wada0, wada1, bada, cond_ready, mod_mm, mod_ready, modT_mm, modT_ready, h_in_ctx, h_in_lat0, h_in_lat1, var_ready,
         std_ready, xn_ready, xT_ready, hi_ready, u_ready, lo_ready, dve_step, stored) = sems
        wada = (wada0, wada1)
        cond = sb(nc, ctx, tag + "cond", [P, KD, 2])
        wa = sb(nc, ctx, tag + "wa", [P, 2, KD, GW])
        ba = sb(nc, ctx, tag + "ba", [2, 3 * D])
        mod = sb(nc, ctx, tag + "mod", [2, 3 * D])
        modT = sb(nc, ctx, tag + "modT", [P, 2 * KD, 2])
        xn = sb(nc, ctx, tag + "xn", [P, TT, D])
        u = sb(nc, ctx, tag + "u", [P, 4, BANK])
        st = sb(nc, ctx, tag + "st", [P, TT, 2, 6])
        mv = sb(nc, ctx, tag + "mv", [P, TT, 4])
        pm = ps(nc, ctx, tag + "pm", 2 * BANK)
        pT = ps(nc, ctx, tag + "pT", BANK)
        px = ps(nc, ctx, tag + "px", 4 * BANK)
        batches = [list(range(CT)), list(range(CT, CT + 4)), list(range(CT + 4, TT))]

        with nc.Block() as block:
            @block.sync
            def _(sp):
                with nc.allow_non_contiguous_dma(reason="two vectors onto the partitions"):
                    sp.dma_start(cond[:, :, 0], c_ctx.rearrange("(k p) -> p k", p=P)).then_inc(c_in, 16)
                    sp.dma_start(cond[:, :, 1], c[0].rearrange("(k p) -> p k", p=P)).then_inc(c_in, 16)
                sp.dma_start(xn[:, 0:CT], src_ctx.rearrange("(t p) n -> p t n", p=P)).then_inc(h_in_ctx, 16)
                for half, h_in in enumerate((h_in_lat0, h_in_lat1)):
                    t = 4 * half
                    sp.dma_start(xn[:, CT + t:CT + t + 4], src_lat[t * P:(t + 4) * P].rearrange("(t p) n -> p t n", p=P)).then_inc(h_in, 16)
                sp.dma_start(ba[:, :], b_ada.partition_broadcast(2)).then_inc(bada, 16)

                for j in range(NCH):
                    if j >= 2:
                        sp.wait_ge(mod_mm, j - 1)
                    sp.dma_start(wa[:, j % 2], w_ada[:, j * GW:(j + 1) * GW].rearrange("(k p) n -> p k n", p=P)).then_inc(wada[j % 2], 16)
                sp.wait_ge(mod_ready, NCH)
                sp.dma_start(mod_dram, mod[:, 2 * D:3 * D]).then_inc(stored, 16)
                sp.wait_ge(stored, 16)

            @block.scalar
            def _(act):
                act.wait_ge(c_in, 32)
                act.activation(cond[:], cond[:], ACT.Silu).then_inc(cond_ready, 1)
                for t in range(TT):
                    act.wait_ge(var_ready, t + 1)
                    act.activation(mv[:, t, 2:3], mv[:, t, 1:2], ACT.Sqrt).then_inc(std_ready, 1)
                act.wait_ge(modT_ready, 1)
                n = 0
                for b in batches:
                    for k in range(KD):
                        act.wait_ge(xT_ready, n + 1)
                        w = len(b) * P
                        scale = modT[:, KD + k, (b[0] >= CT):(b[0] >= CT) + 1]
                        shift = modT[:, k, (b[0] >= CT):(b[0] >= CT) + 1]
                        x = px[:, (n % 4) * BANK:(n % 4) * BANK + w]
                        act.activation(u_hi[:, k, b[0] * P:b[0] * P + w], x, ACT.Identity, scale=scale, bias=shift).then_inc(hi_ready, 1)
                        if n >= 4:
                            act.wait_ge(lo_ready, n - 3)
                        act.activation(u[:, n % 4, 0:w], x, ACT.Identity, scale=scale, bias=shift).then_inc(u_ready, 1)
                        n += 1

            @block.vector
            def _(dve):
                step = 0

                def normalise(t):
                    nonlocal step
                    dve.wait_ge(h_in_ctx if t < CT else (h_in_lat0, h_in_lat1)[(t - CT) // 4], 16)
                    for i in range(2):
                        dve.bn_stats(st[:, t, i], xn[:, t, i * BANK:(i + 1) * BANK]).then_inc(dve_step, 1)
                    step += 2
                    dve.wait_ge(dve_step, step)
                    dve.bn_aggr(mv[:, t, 0:2], st[:, t]).then_inc(dve_step, 1)
                    step += 1
                    dve.wait_ge(dve_step, step)
                    dve.tensor_scalar(mv[:, t, 1:2], mv[:, t, 1:2], LN_EPS, None, ALU.add).then_inc(var_ready, 1)
                    dve.wait_ge(std_ready, t + 1)
                    dve.reciprocal(mv[:, t, 3:4], mv[:, t, 2:3]).then_inc(dve_step, 1)
                    step += 1
                    dve.wait_ge(dve_step, step)
                    dve.tensor_scalar(xn[:, t], xn[:, t], mv[:, t, 0:1], mv[:, t, 3:4], ALU.subtract, ALU.mult).then_inc(xn_ready, 1)

                for t in range(CT + 4):
                    normalise(t)
                dve.wait_ge(bada, 16)
                for j in range(NCH):
                    dve.wait_ge(mod_mm, j + 1)
                    dve.scalar_tensor_tensor(mod[:, j * GW:(j + 1) * GW], pm[0:2, (j % 2) * BANK:(j % 2 + 1) * BANK],
                                             1.0 if 2 <= j < 4 else 0.0, ba[:, j * GW:(j + 1) * GW], ALU.add, ALU.add).then_inc(mod_ready, 1)
                dve.wait_ge(modT_mm, 1)
                dve.tensor_copy(modT[:].rearrange("p a b -> p (a b)"), pT[:, 0:4 * KD]).then_inc(modT_ready, 1)
                for t in range(CT + 4, TT):
                    normalise(t)
                n = 0
                for b in batches:
                    w = len(b) * P
                    for k in range(KD):
                        dve.wait_ge(hi_ready, n + 1)
                        dve.wait_ge(u_ready, n + 1)
                        dve.tensor_tensor(u_lo[:, k, b[0] * P:b[0] * P + w], u[:, n % 4, 0:w], u_hi[:, k, b[0] * P:b[0] * P + w], ALU.subtract).then_inc(lo_ready, 1)
                        n += 1

            @block.tensor
            def _(pe):
                pe.wait_ge(cond_ready, 1)
                for j in range(NCH):
                    pe.wait_ge(wada[j % 2], 16 * (j // 2 + 1))
                    if j >= 2:
                        pe.wait_ge(mod_ready, j - 1)
                    for k in range(KD):
                        mm = pe.matmul(pm[0:2, (j % 2) * BANK:(j % 2 + 1) * BANK], cond[:, k], wa[:, j % 2, k], start=(k == 0), stop=(k == KD - 1))
                    mm.then_inc(mod_mm, 1)
                pe.wait_ge(mod_ready, NCH)
                for k in range(2 * KD):
                    mm = pe.transpose(pT[:, 2 * k:2 * k + 2], mod[:, k * P:(k + 1) * P], ident[0:2, 0:2])
                mm.then_inc(modT_mm, 1)
                n = 0
                for b in batches:
                    pe.wait_ge(xn_ready, b[-1] + 1)
                    for k in range(KD):
                        if n >= 4:
                            pe.wait_ge(u_ready, n - 3)
                        for i, t in enumerate(b):
                            mm = pe.transpose(px[:, (n % 4) * BANK + i * P:(n % 4) * BANK + (i + 1) * P], xn[:, t, k * P:(k + 1) * P], ident[:, :])
                        mm.then_inc(xT_ready, 1)
                        n += 1



def repeat(engine, times, body):
    if times == 1:
        body(0)
    else:
        with engine.Fori(0, times) as turn:
            body(turn)


def project_stage(nc, tag, u_hi, u_lo, w_in, runs, convs, swap, cos_d, sin_d):
    HW = GW // 2
    n_taps = sum(bias.shape[0] // P for _, bias in convs)
    with stage(nc, tag + "w0_in", tag + "w1_in", tag + "tables_in", tag + "w_rounded", tag + "w_split", tag + "pad_ready", tag + "acc_ready", tag + "acc_free",
               tag + "swapped", tag + "conv_step", tag + "finished", tag + "silu_done", tag + "ctx_copied",
               tag + "stored0", tag + "stored1") as (ctx, sems):
        w0_in, w1_in, tables_in, w_rounded, w_split, pad_ready, acc_ready, acc_free, swapped, conv_step, finished, silu_done, ctx_copied, stored0, stored1 = sems
        w_in_sem, stored = (w0_in, w1_in), (stored0, stored1)
        wt = sb(nc, ctx, tag + "wt", [P, 2, KD, HW])
        w_hi = sb(nc, ctx, tag + "w_hi", [P, 2, KD, HW], F32R)
        w_lo = sb(nc, ctx, tag + "w_lo", [P, 2, KD, HW], F32R)
        fin = sb(nc, ctx, tag + "fin", [P, 2, T])
        stg = sb(nc, ctx, tag + "stg", [P, T + 3])
        cv = sb(nc, ctx, tag + "cv", [P, T + 1])
        zero = sb(nc, ctx, tag + "zero", [P, 1])
        taps = sb(nc, ctx, tag + "taps", [P, 4, n_taps])
        cos = sb(nc, ctx, tag + "cos", [P, LAT])
        sin = sb(nc, ctx, tag + "sin", [P, LAT])
        acc = ps(nc, ctx, tag + "acc", 6 * BANK)
        sw = ps(nc, ctx, tag + "sw", 2 * BANK)
        STG_LAT = CTX + 2
        plan, base, shaped, silus = [], 0, 0, 0
        for kind, col, groups, t0, dst, crow in runs:
            plan.append((kind, col, groups, t0, dst, crow, base, shaped, silus))
            base += 4 * groups
            shaped += 4 * groups if kind != "gate" else 0
            silus += 4 * groups if kind == "conv_silu" else 0
        n_tiles = base

        with nc.Block() as block:
            @block.sync
            def _(sp):
                sp.sem_inc(stored0, 16)
                sp.sem_inc(stored1, 16)
                sp.sem_inc(acc_free, 2)
                sp.sem_inc(w_split, 2)
                def load_tables():
                    sp.dma_start(cos[:], cos_d).then_inc(tables_in, 16)
                    sp.dma_start(sin[:], sin_d).then_inc(tables_in, 16)
                    with nc.allow_non_contiguous_dma(reason="conv taps onto the partitions"):
                        at = 0
                        for weights, bias in convs:
                            nt = bias.shape[0] // P
                            for j in range(3):
                                sp.dma_start(taps[:, j, at:at + nt], weights[j].rearrange("(n p) -> p n", p=P)).then_inc(tables_in, 16)
                            sp.dma_start(taps[:, 3, at:at + nt], bias.rearrange("(n p) -> p n", p=P)).then_inc(tables_in, 16)
                            at += nt
                for kind, col, groups, t0, dst, crow, base, shaped, silus in plan:
                    def load_group(g):
                        for half in range(2):
                            sp.wait_ge(w_split, base // 2 + 2 * g + half + 1)
                            sp.dma_start(wt[:, half], w_in[:, bass.ds(col + GW * g + HW * half, HW)].rearrange("(k p) n -> p k n", p=P)).then_inc(w_in_sem[half], 16)
                    repeat(sp, groups, load_group)
                    if base == 0:
                        load_tables()

            @block.gpsimd
            def _(pool):
                pool.wait_ge(pad_ready, 1)
                for kind, col, groups, t0, dst, crow, base, shaped, silus in plan:
                    def split_group(g):
                        for half in range(2):
                            n = base // 2 + 2 * g + half
                            pool.wait_ge(w_in_sem[half], 16 * (base // 4 + g + 1))
                            pool.wait_ge(acc_ready, base + 4 * g + (2 * half or 1))
                            pool.tensor_tensor(w_hi[:, half], wt[:, half], zero[:].unsqueeze(2).to_broadcast([P, KD, HW]), ALU.add).then_inc(w_rounded, 1)
                            pool.wait_ge(w_rounded, n + 1)
                            pool.tensor_tensor(w_lo[:, half], wt[:, half], w_hi[:, half], ALU.subtract).then_inc(w_split, 1)
                    repeat(pool, groups, split_group)

            @block.tensor
            def _(pe):
                pe.sem_inc(acc_ready, 2)
                for kind, col, groups, t0, dst, crow, base, shaped, silus in plan:
                    def group(g):
                        for i in range(4):
                            if i % 2 == 0:
                                pe.wait_ge(w_split, base // 2 + 2 * g + i // 2 + 3)
                            pe.wait_ge(acc_free, base + 4 * g + i + 1)
                            for k in range(KD):
                                for n, (wp, up) in enumerate(PASSES):
                                    for c, w in halves(0, T - t0):
                                        a = (i % 2) * 3 * BANK + c
                                        mm = pe.matmul(acc[:, a:a + w], (w_hi, w_lo)[wp][:, i // 2, k, (i % 2) * P:(i % 2 + 1) * P],
                                                       (u_hi, u_lo)[up][:, k, t0 + c:t0 + c + w], start=(k == n == 0), stop=(k == KD - 1 and n == 2))
                            mm.then_inc(acc_ready, 1)
                            if kind == "rope":
                                pe.wait_ge(acc_free, base + 4 * g + i + 3)
                                if shaped or i:
                                    pe.wait_ge(finished, shaped + 4 * g + i)
                                for c, w in halves(0, LAT):
                                    mm = pe.matmul(sw[:, c:c + w], swap[:, :], stg[:, STG_LAT + c:STG_LAT + c + w], start=True, stop=True)
                                mm.then_inc(swapped, 1)
                    repeat(pe, groups, group)

            @block.scalar
            def _(act):
                act.wait_ge(pad_ready, 1)
                for kind, col, groups, t0, dst, crow, base, shaped, silus in plan:
                    gain = SCALE if col == Q0 else 1.0

                    def group(g):
                        for i in range(4):
                            s, a = i % 2, (i % 2) * 3 * BANK
                            act.wait_ge(acc_ready, base + 4 * g + i + 3)
                            act.wait_ge(stored[s], 16 * (base // 2 + 2 * g + i // 2 + 1))
                            if kind == "gate":
                                act.activation(fin[:, s, t0:T], acc[:, a:a + T - t0], ACT.Silu).then_inc(acc_free, 1)
                                act.wait_ge(acc_free, base + 4 * g + i + 3)
                            else:
                                if kind == "rope" and t0 == 0:
                                    act.activation(fin[:, s, 0:CTX], acc[:, a:a + CTX], ACT.Copy, scale=gain).then_inc(ctx_copied, 1)
                                elif t0 == 0:
                                    act.activation(stg[:, 1:1 + CTX], acc[:, a:a + CTX], ACT.Copy).then_inc(ctx_copied, 1)
                                act.activation(stg[:, STG_LAT:STG_LAT + LAT], acc[:, a + CTX - t0:a + T - t0], ACT.Copy, scale=gain).then_inc(acc_free, 1)
                                act.wait_ge(finished, shaped + 4 * g + i + 1)
                                if kind == "conv_silu":
                                    act.activation(fin[:, s, t0:T], fin[:, s, t0:T], ACT.Silu).then_inc(silu_done, 1)
                                    act.wait_ge(silu_done, silus + 4 * g + i + 1)
                            act.dma_start(dst[bass.ds(P * (4 * g + i), P), t0:T], fin[:, s, t0:T]).then_inc(stored[s], 16)
                    repeat(act, groups, group)
                for s in range(2):
                    act.wait_ge(stored[s], 16 * (n_tiles // 2 + 1))

            @block.vector
            def _(dve):
                dve.memset(zero[:], 0.0)
                dve.memset(stg[:], 0.0).then_inc(pad_ready, 1)
                dve.wait_ge(pad_ready, 1)
                dve.wait_ge(tables_in, 64 * len(convs) + 32)
                steps = 0
                for kind, col, groups, t0, dst, crow, base, shaped, silus in plan:
                    if kind == "gate":
                        continue

                    def group(g):
                        first = steps
                        for i in range(4):
                            s, n = i % 2, 2 * (4 * g + i)
                            dve.wait_ge(acc_free, base + 4 * g + i + 3)
                            if kind == "rope":
                                dve.tensor_tensor(fin[:, s, CTX:T], stg[:, STG_LAT:STG_LAT + LAT], cos[:], ALU.mult).then_inc(conv_step, 1)
                                dve.wait_ge(swapped, shaped + 4 * g + i + 1)
                                dve.tensor_tensor(cv[:, 0:LAT], sw[:, 0:LAT], sin[:], ALU.mult).then_inc(conv_step, 1)
                                dve.wait_ge(conv_step, first + n + 2)
                                dve.tensor_tensor(fin[:, s, CTX:T], fin[:, s, CTX:T], cv[:, 0:LAT], ALU.add).then_inc(finished, 1)
                                continue
                            lo = 0 if t0 == 0 else CTX + 1
                            tile = crow + 4 * g + i

                            def tap(j):
                                return taps[:, j, bass.ds(tile, 1)]
                            dve.tensor_scalar(cv[:, lo:], stg[:, lo + 1:T + 2], tap(1), tap(3), ALU.mult, ALU.add).then_inc(conv_step, 1)
                            dve.wait_ge(conv_step, first + n + 1)
                            dve.scalar_tensor_tensor(cv[:, lo:], stg[:, lo:T + 1], tap(0), cv[:, lo:], ALU.mult, ALU.add).then_inc(conv_step, 1)
                            dve.wait_ge(conv_step, first + n + 2)
                            if t0 == 0:
                                dve.scalar_tensor_tensor(fin[:, s, 0:CTX], stg[:, 2:2 + CTX], tap(2), cv[:, 0:CTX], ALU.mult, ALU.add)
                            dve.scalar_tensor_tensor(fin[:, s, CTX:T], stg[:, STG_LAT + 1:STG_LAT + 1 + LAT], tap(2), cv[:, CTX + 1:], ALU.mult, ALU.add).then_inc(finished, 1)
                    repeat(dve, groups, group)
                    steps += 8 * groups


def v_dt_stage(nc, tag, u_hi, u_lo, w_in, tri, ident, dt_bias, a_log, v_d, la_d, small):
    la, dt, to_end, whole = (small[:, i] for i in range(4))
    H2 = 2 * HEADS
    with stage(nc, tag + "wv_in", tag + "wdt_in", tag + "wdt_split", tag + "wv_rounded", tag + "wv_split", tag + "vec_in", tag + "v_mm", tag + "v_copied", tag + "v_out", tag + "dt_mm",
               tag + "dve_step", tag + "act_step", tag + "la_mm", tag + "la_ready", tag + "laT_mm", tag + "laT_ready", tag + "la_out") as (ctx, sems):
        wv_in, wdt_in, wdt_split, wv_rounded, wv_split, vec_in, v_mm, v_copied, v_out, dt_mm, dve_step, act_step, la_mm, la_ready, laT_mm, laT_ready, la_out = sems
        wv = sb(nc, ctx, tag + "wv", [P, KD, HYW])
        wv_s = [sb(nc, ctx, tag + "wv" + part, [P, KD, HYW], F32R) for part in ("_hi", "_lo")]
        wdt = sb(nc, ctx, tag + "wdt", [P, KD, H2])
        wdt_s = [sb(nc, ctx, tag + "wdt" + part, [P, KD, H2], F32R) for part in ("_hi", "_lo")]
        u = (u_hi, u_lo)
        vb = sb(nc, ctx, tag + "vb", [P, TT, HYW])
        bias = sb(nc, ctx, tag + "bias", [P, H2])
        alog = sb(nc, ctx, tag + "alog", [P, H2])
        tmp = sb(nc, ctx, tag + "tmp", [P, 4, TT * H2])
        laT = sb(nc, ctx, tag + "laT", [H2, T])
        pv = ps(nc, ctx, tag + "pv", 2 * BANK)
        pd = ps(nc, ctx, tag + "pd", BANK)
        pl = ps(nc, ctx, tag + "pl", 2 * BANK)
        pt = ps(nc, ctx, tag + "pt", 3 * BANK)
        N = TT * H2
        flat = "p t h -> p (t h)"
        lam = pl[:, 0:N].rearrange("p (t h) -> p t h", h=H2)
        end = pl[:, BANK:BANK + N].rearrange("p (t h) -> p t h", h=H2)

        with nc.Block() as block:
            @block.sync
            def _(sp):
                with nc.allow_non_contiguous_dma(reason="32 columns of w_in"):
                    sp.dma_start(wdt[:], w_in[:, DT0:DT0 + H2].rearrange("(k p) n -> p k n", p=P)).then_inc(wdt_in, 16)
                sp.dma_start(bias[:], dt_bias.rearrange("a h -> (a h)").partition_broadcast(P)).then_inc(vec_in, 16)
                sp.dma_start(alog[:], a_log.rearrange("a h -> (a h)").partition_broadcast(P)).then_inc(vec_in, 16)
                sp.dma_start(wv[:], w_in[:, V0:V0 + HYW].rearrange("(k p) n -> p k n", p=P)).then_inc(wv_in, 16)
                sp.wait_ge(laT_ready, 1)
                sp.dma_start(la_d, laT[:]).then_inc(la_out, 16)
                sp.wait_ge(la_out, 16)

            @block.tensor
            def _(pe):
                pe.wait_ge(wdt_split, 2)
                for t in range(TT):
                    for k in range(KD):
                        for n, (up, wp) in enumerate(PASSES):
                            mm = pe.matmul(pd[:, t * H2:(t + 1) * H2], u[up][:, k, t * P:(t + 1) * P], wdt_s[wp][:, k], start=(k == n == 0), stop=(k == KD - 1 and n == 2))
                mm.then_inc(dt_mm, 1)
                for t in range(TT):
                    if t >= 2:
                        pe.wait_ge(v_copied, t - 1)
                    for k in range(KD):
                        if t == 0:
                            pe.wait_ge(wv_split, k + 1)
                        for n, (up, wp) in enumerate(PASSES):
                            mm = pe.matmul(pv[:, (t % 2) * BANK:(t % 2 + 1) * BANK], u[up][:, k, t * P:(t + 1) * P], wv_s[wp][:, k],
                                           start=(k == n == 0), stop=(k == KD - 1 and n == 2))
                    mm.then_inc(v_mm, 1)
                pe.wait_ge(dve_step, 7)
                da = tmp[:, 3].rearrange("p (t h) -> p t h", h=H2)
                pe.matmul(lam[:, :, 0:HEADS], tri[:, 0], da[:, :, 0:HEADS], start=True, stop=True)
                pe.matmul(lam[:, :, HEADS:H2], tri[:, 1], da[:, :, HEADS:H2], start=True, stop=True)
                pe.matmul(pl[:, BANK:BANK + N], tri[:, 2], tmp[:, 3], start=True, stop=True).then_inc(la_mm, 1)
                pe.wait_ge(la_ready, 1)
                for t in range(TT):
                    mm = pe.transpose(pt[0:H2, t * P:(t + 1) * P], la[:, t], ident[:, :])
                mm.then_inc(laT_mm, 1)

            @block.gpsimd
            def _(pool):
                pool.wait_ge(wv_in, 16)
                for k in range(0, KD):
                    pool.tensor_copy(wv_s[0][:, k], wv[:, k]).then_inc(wv_rounded, 1)
                    pool.wait_ge(wv_rounded, k + 1)
                    pool.tensor_tensor(wv_s[1][:, k], wv[:, k], wv_s[0][:, k], ALU.subtract).then_inc(wv_split, 1)

            @block.scalar
            def _(act):
                act.wait_ge(vec_in, 32)
                act.activation(alog[:], alog[:], ACT.Exp).then_inc(act_step, 1)
                act.wait_ge(dve_step, 2)
                act.activation(tmp[:, 1], tmp[:, 1], ACT.Exp, scale=-1.0).then_inc(act_step, 1)
                act.wait_ge(act_step, 2)
                act.activation(tmp[:, 1], tmp[:, 1], ACT.Ln, bias=1.0).then_inc(act_step, 1)
                for t in range(TT):
                    act.wait_ge(v_mm, t + 1)
                    act.activation(vb[:, t], pv[:, (t % 2) * BANK:(t % 2 + 1) * BANK], ACT.Copy).then_inc(v_copied, 1)
                    act.wait_ge(v_copied, t + 1)
                    act.dma_start(v_d[t * P:(t + 1) * P], vb[:, t]).then_inc(v_out, 16)
                act.wait_ge(dve_step, 8)
                act.activation(to_end.rearrange(flat), to_end.rearrange(flat), ACT.Exp).then_inc(act_step, 1)
                act.activation(whole.rearrange(flat), pl[:, BANK:BANK + N], ACT.Exp).then_inc(act_step, 1)
                act.wait_ge(v_out, 16 * TT)

            @block.vector
            def _(dve):
                def bc(v):
                    return v[:].unsqueeze(1).to_broadcast([P, TT, H2])
                x3 = tmp[:, 0].rearrange("p (t h) -> p t h", h=H2)
                dve.wait_ge(wdt_in, 16)
                dve.tensor_copy(wdt_s[0][:], wdt[:]).then_inc(wdt_split, 1)
                dve.wait_ge(wdt_split, 1)
                dve.tensor_tensor(wdt_s[1][:], wdt[:], wdt_s[0][:], ALU.subtract).then_inc(wdt_split, 1)
                dve.wait_ge(dt_mm, 1)
                dve.wait_ge(vec_in, 32)
                dve.tensor_tensor(x3, pd[:, 0:N].rearrange("p (t h) -> p t h", h=H2), bc(bias), ALU.add).then_inc(dve_step, 1)
                dve.wait_ge(dve_step, 1)
                dve.scalar_tensor_tensor(tmp[:, 1], tmp[:, 0], -1.0, tmp[:, 0], ALU.mult, ALU.max).then_inc(dve_step, 1)
                dve.tensor_scalar(tmp[:, 2], tmp[:, 0], 0.0, None, ALU.max).then_inc(dve_step, 1)
                dve.wait_ge(act_step, 3)
                dve.wait_ge(dve_step, 3)
                dve.tensor_tensor(dt.rearrange(flat), tmp[:, 1], tmp[:, 2], ALU.add).then_inc(dve_step, 1)
                dve.wait_ge(dve_step, 4)
                dve.tensor_tensor(x3, dt, bc(alog), ALU.mult).then_inc(dve_step, 1)
                dve.wait_ge(dve_step, 5)
                dve.tensor_scalar(tmp[:, 3], tmp[:, 0], -1.0, None, ALU.mult).then_inc(dve_step, 2)
                dve.wait_ge(la_mm, 1)
                dve.tensor_copy(la, lam).then_inc(la_ready, 1)
                dve.wait_ge(la_ready, 1)
                dve.tensor_tensor(to_end, end, la, ALU.subtract).then_inc(dve_step, 1)
                dve.wait_ge(laT_mm, 1)
                dve.tensor_copy(laT[:], pt[0:H2, 0:T]).then_inc(laT_ready, 1)
                dve.wait_ge(act_step, 5)
                dve.tensor_tensor(to_end.rearrange(flat), to_end.rearrange(flat), dt.rearrange(flat), ALU.mult).then_inc(dve_step, 1)


def attention_stage(nc, tag, layer, first_tile, ident, tri, lam_vecs, qk_d, v_d, gate_d, o_d):
    tiles = list(range(first_tile, TT))
    nq = len(tiles)
    BODY = 2
    units = [(hh, q) for hh in range(BODY) for q in tiles]
    NU = len(units)

    def keys(q):
        return CTX if q < CT else T

    batches = [-(-keys(q) // BANK) for _, q in units]
    before = [sum(batches[:n]) for n in range(NU + 1)]
    with stage(nc, tag + "lam_in", tag + "in0", tag + "in1", tag + "lam_step", tag + "lam_exp", tag + "scored", tag + "maxed", tag + "exped",
               tag + "mix_step", tag + "mixed", tag + "turned", tag + "turned_copied", tag + "pv_done", tag + "squared", tag + "sq_summed",
               tag + "log_done", tag + "rms_ready", tag + "scaled", tag + "gated", tag + "stored0", tag + "stored1") as (ctx, sems):
        (lam_in, in0, in1, lam_step, lam_exp, scored, maxed, exped, mix_step, mixed, turned, turned_copied, pv_done, squared, sq_summed,
         log_done, rms_ready, scaled, gated, stored0, stored1) = sems
        stored = (stored0, stored1)
        head_in = (in0, in1)
        q_s = sb(nc, ctx, tag + "q", [P, BODY, T])
        k_s = sb(nc, ctx, tag + "k", [P, BODY, T])
        g_s = sb(nc, ctx, tag + "g", [P, BODY, T])
        v_s = sb(nc, ctx, tag + "v", [P, BODY, TT, P])
        o_s = sb(nc, ctx, tag + "o", [P, BODY, T])
        prob = sb(nc, ctx, tag + "prob", [P, 2, 2, T])
        mix = sb(nc, ctx, tag + "mix", [P, 2, T])
        mixT = sb(nc, ctx, tag + "mixT", [P, TT, P])
        sq = sb(nc, ctx, tag + "sq", [P, 2, P])
        rms = sb(nc, ctx, tag + "rms", [P, 2, P])
        part = sb(nc, ctx, tag + "part", [P, P])
        nmax = sb(nc, ctx, tag + "nmax", [P, 2, 2])
        sums = sb(nc, ctx, tag + "sums", [P, 2, 2])
        recip = sb(nc, ctx, tag + "recip", [P, 2, 2])
        lv = sb(nc, ctx, tag + "lv", [P, 4, AD])
        lt = sb(nc, ctx, tag + "lt", [P, 2, AD])
        lam = sb(nc, ctx, tag + "lam", [P, 4])
        cst = sb(nc, ctx, tag + "cst", [P, 2])
        pS = ps(nc, ctx, tag + "pS", 6 * BANK)
        pT = ps(nc, ctx, tag + "pT", BANK)
        pO = ps(nc, ctx, tag + "pO", BANK)

        def turns(engine, body):
            with engine.Fori(0, AH // BODY) as turn:
                body(turn)

        with nc.Block() as block:
            @block.sync
            def _(sp):
                sp.dma_start(lv[:], lam_vecs.partition_broadcast(P)).then_inc(lam_in, 16)
                t0 = first_tile * P

                def store(h):
                    sp.wait_ge(gated, (h + 1) * nq + 1)
                    sp.dma_start(o_d[1024 + h * P:1024 + (h + 1) * P, t0:], o_s[:, h % BODY, t0:]).then_inc(stored[h % BODY], 16)

                for h in range(AH):
                    hh, row = h % BODY, P * h
                    if h >= BODY:
                        store(h - BODY)
                        sp.wait_ge(stored[hh], 16 * (h // BODY))
                    sp.dma_start(q_s[:, hh, t0:], qk_d[row:row + P, t0:]).then_inc(head_in[hh], 16)
                    sp.dma_start(k_s[:, hh], qk_d[row + HYW:row + HYW + P, :]).then_inc(head_in[hh], 16)
                    sp.dma_start(v_s[:, hh], v_d.rearrange("(t p) n -> p t n", p=P)[:, :, row:row + P]).then_inc(head_in[hh], 16)
                    sp.dma_start(g_s[:, hh, t0:], gate_d[row:row + P, t0:]).then_inc(head_in[hh], 16)
                for h in range(AH - BODY, AH):
                    store(h)
                for hh in range(BODY):
                    sp.wait_ge(stored[hh], 16 * (AH // BODY))

            @block.tensor
            def _(pe):
                pe.wait_ge(lam_exp, 1)

                def body(g):
                    def scores(n, m):
                        hh, q = units[n]
                        if q == tiles[0] and m == 0:
                            pe.wait_ge(head_in[hh], 64 * (g + 1))
                        pe.wait_ge(exped, 2 * (NU * g + n) + m + 1)
                        for c, w in halves(0, keys(q)):
                            mm = pe.matmul(pS[:, m * 3 * BANK + c:m * 3 * BANK + c + w], q_s[AD * m:AD * (m + 1), hh, q * P:(q + 1) * P],
                                           k_s[AD * m:AD * (m + 1), hh, c:c + w], start=True, stop=True)
                        mm.then_inc(scored, 1)

                    def turn(n, b):
                        hh, q = units[n]
                        if b == 0:
                            pe.wait_ge(mixed, NU * g + n + 3)
                        pe.wait_ge(turned_copied, before[NU] * g + before[n] + b + 1)
                        for kt in range(4 * b, min(4 * b + 4, keys(q) // P)):
                            mm = pe.transpose(pT[:, (kt % 4) * P:(kt % 4 + 1) * P], mix[:, n % 2, kt * P:(kt + 1) * P], ident[:, :])
                        mm.then_inc(turned, 1)

                    def values(n):
                        hh, q = units[n]
                        pe.wait_ge(scaled, NU * g + n + 1)
                        for kt in range(keys(q) // P):
                            if kt % 4 == 0:
                                pe.wait_ge(turned_copied, before[NU] * g + before[n] + kt // 4 + 2)
                            mm = pe.matmul(pO[:, 0:P], v_s[:, hh, kt], mixT[:, kt], start=(kt == 0), stop=(kt == keys(q) // P - 1))
                        mm.then_inc(pv_done, 1)

                    def squares(n):
                        pe.wait_ge(squared, NU * g + n + 1)
                        pe.matmul(pO[:, P:2 * P], tri[:, 2], sq[:, n % 2], start=True, stop=True).then_inc(sq_summed, 1)

                    for i in range(NU + 3):
                        turning = batches[i - 2] if 2 <= i < NU + 2 else 0
                        if turning:
                            turn(i - 2, 0)
                        if i < NU:
                            scores(i, 0)
                        if i >= 3:
                            squares(i - 3)
                        if turning > 1:
                            turn(i - 2, 1)
                        if i < NU:
                            scores(i, 1)
                        if turning > 2:
                            turn(i - 2, 2)
                        if turning:
                            values(i - 2)
                turns(pe, body)

            @block.scalar
            def _(act):
                act.preload_act_table_set("natural_log_exp_and_others")
                act.sem_inc(exped, 2)
                act.sem_inc(turned_copied, 1)
                act.wait_ge(lam_step, 3)
                act.activation(lam[:, 2:4], lam[:, 0:2], ACT.Exp).then_inc(lam_exp, 1)

                def body(g):
                    def exp(n, m):
                        hh, q = units[n]
                        act.wait_ge(maxed, 2 * (NU * g + n) + m + 1)
                        act.wait_ge(mixed, NU * g + n + 1)
                        act.activation(prob[:, n % 2, m, 0:keys(q)], pS[:, m * 3 * BANK:m * 3 * BANK + keys(q)], ACT.Exp,
                                       bias=nmax[:, n % 2, m:m + 1], accum_out=sums[:, n % 2, m:m + 1]).then_inc(exped, 1)

                    def turn(n, b):
                        hh, q = units[n]
                        act.wait_ge(turned, before[NU] * g + before[n] + b + 1)
                        w = min(BANK, keys(q) - b * BANK)
                        act.activation(mixT[:, 4 * b:4 * b + w // P].rearrange("p a b -> p (a b)"), pT[:, 0:w], ACT.Copy).then_inc(turned_copied, 1)

                    def square(n):
                        act.wait_ge(pv_done, NU * g + n + 1)
                        act.activation(sq[:, n % 2], pO[:, 0:P], ACT.Square).then_inc(squared, 1)

                    def norm(n):
                        act.wait_ge(sq_summed, NU * g + n + 1)
                        act.activation(rms[:, n % 2], pO[:, P:2 * P], ACT.Ln, scale=1.0 / P, bias=cst[:, 0:1]).then_inc(log_done, 1)
                        act.wait_ge(log_done, NU * g + n + 1)
                        act.activation(rms[:, n % 2], rms[:, n % 2], ACT.Exp, scale=-0.5, bias=cst[:, 1:2]).then_inc(rms_ready, 1)

                    for i in range(NU + 3):
                        turning = batches[i - 2] if 2 <= i < NU + 2 else 0
                        for b in range(min(turning, 2)):
                            turn(i - 2, b)
                        if i >= 3:
                            norm(i - 3)
                        if i < NU:
                            exp(i, 0)
                        if turning > 2:
                            turn(i - 2, 2)
                        if i < NU:
                            exp(i, 1)
                        if turning:
                            square(i - 2)
                turns(act, body)

            @block.vector
            def _(dve):
                dve.sem_inc(scaled, 1)
                dve.sem_inc(mixed, 2)
                dve.memset(cst[:, 0:1], RMS_EPS)
                dve.memset(cst[:, 1:2], math.log(1.0 - lam_init(layer))).then_inc(lam_step, 1)
                dve.wait_ge(lam_in, 16)
                dve.tensor_tensor(lt[:], lv[:, 0:4:2], lv[:, 1:4:2], ALU.mult).then_inc(lam_step, 1)
                dve.wait_ge(lam_step, 2)
                dve.tensor_reduce(lam[:, 0:2], lt[:], AX.X, ALU.add).then_inc(lam_step, 1)
                dve.wait_ge(lam_exp, 1)
                dve.tensor_tensor(lam[:, 1:2], lam[:, 3:4], lam[:, 2:3], ALU.subtract).then_inc(lam_step, 1)
                dve.wait_ge(lam_step, 4)
                dve.tensor_scalar(lam[:, 0:1], lam[:, 1:2], -lam_init(layer), None, ALU.add).then_inc(lam_step, 1)
                dve.wait_ge(lam_step, 5)

                def body(g):
                    def maximum(n, m):
                        hh, q = units[n]
                        dve.wait_ge(scored, 2 * (NU * g + n) + m + 1)
                        dve.tensor_reduce(nmax[:, n % 2, m:m + 1], pS[:, m * 3 * BANK:m * 3 * BANK + keys(q)], AX.X, ALU.max, negate=True).then_inc(maxed, 1)

                    def combine(n):
                        hh, q = units[n]
                        s, steps = n % 2, 3 * (NU * g + n)
                        dve.wait_ge(exped, 2 * (NU * g + n) + 4)
                        dve.reciprocal(recip[:, s], sums[:, s]).then_inc(mix_step, 1)
                        dve.wait_ge(mix_step, steps + 1)
                        dve.tensor_scalar(recip[:, s, 1:2], recip[:, s, 1:2], lam[:, 0:1], None, ALU.mult).then_inc(mix_step, 1)
                        if n >= 2:
                            dve.wait_ge(turned, before[NU] * g + before[n - 1])
                        dve.tensor_scalar(mix[:, s, 0:keys(q)], prob[:, s, 0, 0:keys(q)], recip[:, s, 0:1], None, ALU.mult).then_inc(mix_step, 1)
                        dve.wait_ge(mix_step, steps + 3)
                        dve.scalar_tensor_tensor(mix[:, s, 0:keys(q)], prob[:, s, 1, 0:keys(q)], recip[:, s, 1:2], mix[:, s, 0:keys(q)], ALU.mult, ALU.add).then_inc(mixed, 1)

                    def gate(n):
                        hh, q = units[n]
                        dve.wait_ge(rms_ready, NU * g + n + 1)
                        dve.wait_ge(gated, NU * g + n + 1)
                        dve.tensor_tensor(part[:], pO[:, 0:P], rms[:, n % 2], ALU.mult).then_inc(scaled, 1)
                        dve.wait_ge(scaled, NU * g + n + 2)
                        dve.tensor_tensor(o_s[:, hh, q * P:(q + 1) * P], part[:], g_s[:, hh, q * P:(q + 1) * P], ALU.mult).then_inc(gated, 1)

                    for i in range(NU + 3):
                        if i < NU:
                            maximum(i, 0)
                        if 1 <= i < NU + 1:
                            combine(i - 1)
                        if i >= 3:
                            gate(i - 3)
                        if i < NU:
                            maximum(i, 1)
                dve.sem_inc(gated, 1)
                turns(dve, body)


def ssd_stage(nc, tag, first_tile, tri, ident, small, skip, xbc_d, la_d, gate_z, o_d):
    XG = HPG * HD
    XT = XG // P
    BODY = 2
    outs = list(range(first_tile, TT))
    NO = len(outs)
    order = [list(range(TT)), list(range(CT))[::-1] + list(range(CT, TT))[::-1]]
    NSTEP = TT - 1
    with stage(nc, tag + "in0", tag + "in1", tag + "z0_in", tag + "z1_in", tag + "la0_in", tag + "la1_in", tag + "skip_in", tag + "zeroed", tag + "picked", tag + "turned", tag + "x_copied",
               tag + "end_scaled", tag + "dt_scaled", tag + "state_mm", tag + "decayed", tag + "state_ready", tag + "cb_mm", tag + "cb_masked", tag + "seg_ready",
               tag + "dec_ready", tag + "w_ready", tag + "c_scaled", tag + "y_mm", tag + "skipped", tag + "gated", tag + "stored0", tag + "stored1") as (ctx, sems):
        (in0, in1, z0_in, z1_in, la0_in, la1_in, skip_in, zeroed, picked, turned, x_copied, end_scaled, dt_scaled, state_mm, decayed, state_ready, cb_mm, cb_masked, seg_ready,
         dec_ready, w_ready, c_scaled, y_mm, skipped, gated, stored0, stored1) = sems
        group_in, z_in, la_in, stored = (in0, in1), (z0_in, z1_in), (la0_in, la1_in), (stored0, stored1)
        xT = sb(nc, ctx, tag + "xT", [P, BODY, XT, T])
        zT = sb(nc, ctx, tag + "zT", [P, BODY, XT, T])
        bT = sb(nc, ctx, tag + "bT", [P, BODY, T])
        cT = sb(nc, ctx, tag + "cT", [P, BODY, T])
        o_s = sb(nc, ctx, tag + "o", [P, BODY, XT, T])
        tok = sb(nc, ctx, tag + "tok", [P, TT, XG + P])
        xdt = sb(nc, ctx, tag + "xdt", [P, TT, 2, HPG, HD])
        xend = sb(nc, ctx, tag + "xend", [P, TT, 2, HPG, HD])
        state = sb(nc, ctx, tag + "state", [P, 2, TT, HPG, HD])
        fade = sb(nc, ctx, tag + "fade", [P, 2, HPG, HD])
        mine = sb(nc, ctx, tag + "mine", [P, BODY, 4, TT, 2, HPG])
        la_b = sb(nc, ctx, tag + "la_b", [P, 2, 2, HPG, P])
        seg = sb(nc, ctx, tag + "seg", [P, 2, 2, HPG, P])
        cs = sb(nc, ctx, tag + "cs", [P, 2, 2 * HPG, P])
        cbm = sb(nc, ctx, tag + "cbm", [P, 2, 2, P])
        d_s = sb(nc, ctx, tag + "d", [P, SSD_TILES])
        part = sb(nc, ctx, tag + "part", [P, XT, P])
        pT = ps(nc, ctx, tag + "pT", 2 * BANK)
        pS = ps(nc, ctx, tag + "pS", 2 * BANK)
        pC = ps(nc, ctx, tag + "pC", 2 * BANK)
        pY = ps(nc, ctx, tag + "pY", 2 * BANK)
        steps = [(d, order[d][n], order[d][n + 1]) for n in range(NSTEP) for d in range(2)]
        needed = list(dict.fromkeys(c for _, c, _ in steps))

        def turns(engine, body):
            with engine.Fori(0, GROUPS // BODY) as turn:
                def groups():
                    for hh in range(BODY):
                        body(hh, BODY * turn + hh, turn)
                groups()

        with nc.Block() as block:
            @block.sync
            def _(sp):
                for half in range(2):
                    with nc.allow_non_contiguous_dma(reason="one value per head"):
                        sp.dma_start(d_s[HD * half:HD * (half + 1), :], skip.rearrange("(n b) -> b n", b=2)[half].partition_broadcast(HD)).then_inc(skip_in, 16)

                def load_group(gr):
                    hh = gr % BODY
                    if gr >= BODY:
                        sp.wait_ge(stored[hh], 16 * (gr // BODY))
                    t0 = first_tile * P
                    sp.dma_start(xT[:, hh], xbc_d[gr * XG:(gr + 1) * XG].rearrange("(n p) t -> p n t", p=P)).then_inc(group_in[hh], 16)
                    sp.dma_start(bT[:, hh], xbc_d[1024 + gr * P:1024 + (gr + 1) * P]).then_inc(group_in[hh], 16)
                    sp.dma_start(cT[:, hh], xbc_d[1536 + gr * P:1536 + (gr + 1) * P]).then_inc(group_in[hh], 16)
                    sp.dma_start(zT[:, hh, :, t0:], gate_z[gr * XG:(gr + 1) * XG, t0:].rearrange("(n p) t -> p n t", p=P)).then_inc(z_in[hh], 16)

                def store_group(gr):
                    hh, t0 = gr % BODY, first_tile * P
                    sp.wait_ge(gated, NO * (gr + 1) + 2)
                    sp.dma_start(o_d[gr * XG:(gr + 1) * XG, t0:].rearrange("(n p) t -> p n t", p=P), o_s[:, hh, :, t0:]).then_inc(stored[hh], 16)

                load_group(0)
                for gr in range(GROUPS):
                    for i, c in enumerate(outs):
                        n = gr * NO + i
                        if n >= 2:
                            sp.wait_ge(dec_ready, 2 * (n - 1))
                        for d in range(2):
                            rows = d * HEADS + gr * HPG
                            sp.dma_start(la_b[:, n % 2, d], la_d[rows:rows + HPG, c * P:(c + 1) * P].partition_broadcast(P)).then_inc(la_in[n % 2], 16)
                        if i == 1:
                            if gr:
                                store_group(gr - 1)
                            if gr + 1 < GROUPS:
                                load_group(gr + 1)
                store_group(GROUPS - 1)
                for hh in range(BODY):
                    sp.wait_ge(stored[hh], 16 * (GROUPS // BODY))

            @block.tensor
            def _(pe):
                pe.wait_ge(zeroed, 1)

                def body(hh, gr, turn):
                    pe.wait_ge(group_in[hh], 48 * (turn + 1))
                    for p, c in enumerate(needed):
                        pe.wait_ge(x_copied, TT * gr + p + 1)
                        b = (p % 2) * BANK
                        cols = slice(c * P, (c + 1) * P)
                        for n in range(XT):
                            pe.transpose(pT[:, b + n * P:b + (n + 1) * P], xT[:, hh, n, cols], ident[:, :])
                        pe.transpose(pT[:, b + XG:b + XG + P], bT[:, hh, cols], ident[:, :]).then_inc(turned, 1)
                    for n, (d, c, nxt) in enumerate(steps):
                        pe.wait_ge(end_scaled, TT * gr + needed.index(c) + 1)
                        pe.wait_ge(state_ready, 2 * NSTEP * gr + n + 1)
                        pe.matmul(pS[:, d * BANK:d * BANK + XG], tok[:, c, XG:XG + P], xend[:, c, d].rearrange("p h e -> p (h e)"),
                                  start=True, stop=True).then_inc(state_mm, 1)

                    def outputs(i):
                        c, b = outs[i], (i % 2) * BANK
                        if i == 0:
                            pe.wait_ge(state_ready, 2 * NSTEP * (gr + 1) + 2)
                        pe.wait_ge(dt_scaled, NO * gr + i + 1)
                        pe.wait_ge(w_ready, NO * gr + i + 1)
                        pe.wait_ge(c_scaled, NO * gr + i + 1)
                        pe.wait_ge(gated, NO * gr + i + 1)
                        for j in range(HPG):
                            out = pY[HD * (j % 2):HD * (j % 2 + 1), b + (j // 2) * P:b + (j // 2 + 1) * P]
                            for d in range(2):
                                pe.matmul(out, xdt[:, c, d, j], seg[:, i % 2, d, j], start=(d == 0), stop=False)
                                mm = pe.matmul(out, state[:, d, c, j], cs[:, i % 2, d * HPG + j], start=False, stop=(d == 1))
                        mm.then_inc(y_mm, 1)

                    for i in range(NO + 1):
                        if i < NO:
                            c = outs[i]
                            pe.wait_ge(cb_masked, NO * gr + i + 1)
                            pe.matmul(pC[:, (i % 2) * BANK:(i % 2) * BANK + P], bT[:, hh, c * P:(c + 1) * P], cT[:, hh, c * P:(c + 1) * P],
                                      start=True, stop=True).then_inc(cb_mm, 1)
                        if i >= 1:
                            outputs(i - 1)
                turns(pe, body)

            @block.scalar
            def _(act):
                act.preload_act_table_set("natural_log_exp_and_others")
                act.sem_inc(x_copied, 2)

                def body(hh, gr, turn):
                    for p, c in enumerate(needed):
                        act.wait_ge(turned, TT * gr + p + 1)
                        act.activation(tok[:, c], pT[:, (p % 2) * BANK:(p % 2) * BANK + XG + P], ACT.Copy).then_inc(x_copied, 1)
                    for i in range(NO):
                        act.wait_ge(seg_ready, NO * gr + i + 1)
                        act.activation(seg[:, i % 2].rearrange("p d h l -> p (d h l)"), seg[:, i % 2].rearrange("p d h l -> p (d h l)"), ACT.Exp).then_inc(dec_ready, 1)
                        act.activation(cs[:, i % 2].rearrange("p h l -> p (h l)"), la_b[:, i % 2].rearrange("p d h l -> p (d h l)"), ACT.Exp).then_inc(dec_ready, 1)
                turns(act, body)

            @block.gpsimd
            def _(pool):
                def body(hh, gr, turn):
                    pool.wait_ge(picked, gr + 1)
                    def scale(dst, kind, c):
                        x = tok[:, c, 0:XG].rearrange("p (h e) -> p h e", h=HPG).unsqueeze(1).to_broadcast([P, 2, HPG, HD])
                        return pool.tensor_tensor(dst[:, c], x, mine[:, hh, kind, c].unsqueeze(3).to_broadcast([P, 2, HPG, HD]), ALU.mult)

                    for p, c in enumerate(needed):
                        pool.wait_ge(x_copied, TT * gr + p + 3)
                        scale(xend, 2, c).then_inc(end_scaled, 1)
                    for c in outs:
                        scale(xdt, 1, c).then_inc(dt_scaled, 1)
                    for i in range(NO):
                        c = outs[i]
                        pool.wait_ge(dec_ready, 2 * (NO * gr + i) + 2)
                        pool.tensor_tensor(cs[:, i % 2], cs[:, i % 2],
                                           cT[:, hh, c * P:(c + 1) * P].unsqueeze(1).to_broadcast([P, 2 * HPG, P]), ALU.mult).then_inc(c_scaled, 1)
                pool.sem_inc(y_mm, 2)
                turns(pool, body)

            @block.vector
            def _(dve):
                for d in range(2):
                    z = dve.memset(state[:, d, order[d][0]], 0.0)
                z.then_inc(zeroed, 1)
                dve.sem_inc(state_ready, 2)
                dve.sem_inc(cb_masked, 2)
                dve.sem_inc(gated, 2)
                dve.wait_ge(skip_in, 32)

                def body(hh, gr, turn):
                    cols = small[:].rearrange("p k t (d h) -> p (k t) d h", d=2)[:, :, :, bass.ds(HPG * gr, HPG)]
                    dve.tensor_copy(mine[:, hh].rearrange("p k t d h -> p (k t) d h"), cols).then_inc(picked, 1)
                    dve.wait_ge(picked, gr + 1)
                    for n, (d, c, nxt) in enumerate(steps):
                        at = 2 * NSTEP * gr + n
                        dve.wait_ge(state_ready, at + 1)
                        dve.tensor_tensor(fade[:, d], state[:, d, c], mine[:, hh, 3, c, d].unsqueeze(2).to_broadcast([P, HPG, HD]), ALU.mult).then_inc(decayed, 1)
                        dve.wait_ge(decayed, at + 1)
                        dve.wait_ge(state_mm, at + 1)
                        dve.tensor_tensor(state[:, d, nxt].rearrange("p h e -> p (h e)"), fade[:, d].rearrange("p h e -> p (h e)"),
                                          pS[:, d * BANK:d * BANK + XG], ALU.add).then_inc(state_ready, 1)

                    def differences(i):
                        c, at = outs[i], NO * gr + i
                        dve.wait_ge(la_in[i % 2], 32 * ((NO // 2) * gr + i // 2 + 1))
                        dve.wait_ge(y_mm, at + 1)
                        for d in range(2):
                            for j in range(HPG):
                                last = dve.tensor_scalar(seg[:, i % 2, d, j], la_b[:, i % 2, d, j], mine[:, hh, 0, c, d, j:j + 1], 0.0, ALU.subtract, ALU.min)
                        last.then_inc(seg_ready, 1)
                        dve.wait_ge(cb_mm, at + 1)
                        cb = pC[:, (i % 2) * BANK:(i % 2) * BANK + P].unsqueeze(1).to_broadcast([P, 2, P])
                        dve.tensor_tensor(cbm[:, i % 2], cb, tri[:, 0:2], ALU.mult).then_inc(cb_masked, 1)

                    def weights(i):
                        at = NO * gr + i
                        dve.wait_ge(dec_ready, 2 * at + 1)
                        dve.wait_ge(cb_masked, at + 3)
                        dve.tensor_tensor(seg[:, i % 2], seg[:, i % 2], cbm[:, i % 2].unsqueeze(2).to_broadcast([P, 2, HPG, P]), ALU.mult).then_inc(w_ready, 1)

                    def gate(i):
                        at, c = NO * gr + i, outs[i]
                        cols, b = slice(c * P, (c + 1) * P), (i % 2) * BANK
                        dve.wait_ge(y_mm, at + 3)
                        dve.wait_ge(gated, at + 2)
                        if i == 0:
                            dve.wait_ge(z_in[hh], 16 * (turn + 1))
                        for n in range(XT):
                            last = dve.scalar_tensor_tensor(part[:, n], xT[:, hh, n, cols], d_s[:, bass.ds(XT * gr + n, 1)], pY[:, b + n * P:b + (n + 1) * P], ALU.mult, ALU.add)
                        last.then_inc(skipped, 1)
                        dve.wait_ge(skipped, at + 1)
                        dve.tensor_tensor(o_s[:, hh, :, cols], part[:], zT[:, hh, :, cols], ALU.mult).then_inc(gated, 1)

                    for i in range(NO + 2):
                        if 1 <= i < NO + 1:
                            weights(i - 1)
                        if i < NO:
                            differences(i)
                        if i >= 2:
                            gate(i - 2)
                turns(dve, body)


R2 = math.sqrt(0.5)
C1, C3 = math.cos(math.pi / 8), math.cos(3 * math.pi / 8)


class Steps:

    def __init__(self, engine, sem):
        self.engine, self.sem, self.n = engine, sem, 0

    def add(self, out, a, b):
        self.engine.tensor_tensor(out, a, b, ALU.add).then_inc(self.sem, 1)
        self.n += 1

    def sub(self, out, a, b):
        self.engine.tensor_tensor(out, a, b, ALU.subtract).then_inc(self.sem, 1)
        self.n += 1

    def scale(self, out, a, s):
        self.engine.tensor_scalar(out, a, s, None, ALU.mult).then_inc(self.sem, 1)
        self.n += 1

    def axpy(self, out, s, a, b, op=ALU.add):
        self.engine.scalar_tensor_tensor(out, a, s, b, ALU.mult, op).then_inc(self.sem, 1)
        self.n += 1

    def level(self):
        self.engine.wait_ge(self.sem, self.n)


def butterfly(do, J, u, R, Tm):
    def r(k):
        return R[:, k, 0]

    def w(k):
        return R[:, k, 1]
    if J == 2:
        do.add(r(0), u[:, 0], u[:, 1])
        do.sub(w(0), u[:, 0], u[:, 1])
        do.scale(R[:, 1], u[:, 0:2], 1.0)
        return
    s, d = Tm[:, 0:4], Tm[:, 4:8]
    do.add(s, u[:, 0:4], u[:, 4:8])
    do.sub(d, u[:, 0:4], u[:, 4:8])
    for j in (1, 2, 3):
        do.sub(Tm[:, 7 + j], u[:, j], u[:, 8 - j])
        do.add(Tm[:, 10 + j], u[:, j], u[:, 8 - j])
    do.level()
    a1, a2, a3, b1, b2, b3 = (Tm[:, i] for i in range(8, 14))
    do.sub(r(4), s[:, 0], s[:, 2])
    do.sub(w(4), s[:, 1], s[:, 3])
    do.add(Tm[:, 14:16], s[:, 0:2], s[:, 2:4])
    do.sub(r(2), d[:, 1], d[:, 3])
    do.add(w(2), d[:, 1], d[:, 3])
    do.axpy(r(1), R2, a2, u[:, 0])
    do.axpy(r(3), -R2, a2, u[:, 0])
    do.axpy(w(1), R2, b2, u[:, 4])
    do.axpy(w(3), R2, b2, u[:, 4], ALU.subtract)
    do.scale(r(5), a3, C3)
    do.scale(w(5), b3, C1)
    do.scale(r(7), a3, C1)
    do.scale(w(7), b3, C3)
    do.level()
    do.add(r(0), Tm[:, 14], Tm[:, 15])
    do.sub(w(0), Tm[:, 14], Tm[:, 15])
    do.axpy(r(6), -R2, r(2), d[:, 0])
    do.axpy(w(6), R2, w(2), d[:, 2], ALU.subtract)
    do.axpy(Tm[:, 9], C3, a1, r(7), ALU.subtract)
    do.axpy(Tm[:, 10], C1, a1, r(5))
    do.axpy(Tm[:, 12], C3, b1, w(5))
    do.axpy(Tm[:, 13], C1, b1, w(7), ALU.subtract)
    do.level()
    do.axpy(r(2), R2, r(2), d[:, 0])
    do.axpy(w(2), R2, w(2), d[:, 2])
    do.sub(r(7), r(1), Tm[:, 10])
    do.sub(r(5), r(3), Tm[:, 9])
    do.sub(w(7), Tm[:, 12], w(1))
    do.sub(w(5), Tm[:, 13], w(3))
    do.level()
    do.add(r(1), r(1), Tm[:, 10])
    do.add(r(3), r(3), Tm[:, 9])
    do.add(w(1), Tm[:, 12], w(1))
    do.add(w(3), Tm[:, 13], w(3))


def butterfly_back(do, J, Q, Tm, y):
    def q(k):
        return Q[:, k, 0]

    def v(k):
        return Q[:, k, 1]

    def t(i):
        return Tm[:, i]
    if J == 2:
        do.add(t(0), q(0), v(0))
        do.sub(t(1), q(0), v(0))
        do.level()
        do.add(y[:, 0:2], Tm[:, 0:2], Q[:, 1])
        do.level()
        return
    for at, k in ((0, 1), (4, 3), (10, 2)):
        do.add(Tm[:, at:at + 2], Q[:, k], Q[:, 8 - k])
        do.sub(Tm[:, at + 2:at + 4], Q[:, k], Q[:, 8 - k])
    do.add(t(8), q(0), v(0))
    do.sub(t(9), q(0), v(0))
    do.level()
    do.add(Q[:, 0], Tm[:, 8:10], Q[:, 4])
    do.sub(Q[:, 1], Tm[:, 8:10], Q[:, 4])
    do.scale(t(14), t(12), R2)
    do.add(q(2), t(0), t(4))
    do.sub(v(2), t(3), t(7))
    do.sub(q(3), t(0), t(4))
    do.add(v(3), t(3), t(7))
    do.scale(q(5), t(6), C3)
    do.scale(v(5), t(6), C1)
    do.scale(q(6), t(5), C1)
    do.scale(v(6), t(5), C3)
    do.level()
    do.axpy(q(7), C1, t(2), q(5))
    do.axpy(v(7), C3, t(2), v(5), ALU.subtract)
    do.axpy(t(15), C3, t(1), q(6))
    do.axpy(t(5), C1, t(1), v(6), ALU.subtract)
    do.axpy(t(8), R2, t(11), t(14))
    do.axpy(t(9), R2, t(11), t(14), ALU.subtract)
    do.add(y[:, 0], q(0), t(10))
    do.sub(y[:, 4], q(0), t(10))
    do.add(y[:, 2], q(1), t(13))
    do.sub(y[:, 6], q(1), t(13))
    do.add(t(0), q(3), v(3))
    do.sub(t(4), v(3), q(3))
    do.level()
    do.add(t(1), q(7), t(15))
    do.sub(t(2), t(15), q(7))
    do.add(t(3), v(7), t(5))
    do.sub(t(6), t(5), v(7))
    do.add(y[:, 1], v(0), t(8))
    do.sub(y[:, 5], v(0), t(8))
    do.add(y[:, 3], v(1), t(9))
    do.sub(y[:, 7], v(1), t(9))
    do.add(y[:, 0], y[:, 0], q(2))
    do.add(y[:, 4], y[:, 4], v(2))
    do.axpy(y[:, 2], R2, t(0), y[:, 2])
    do.axpy(y[:, 6], R2, t(4), y[:, 6])
    do.level()
    do.add(y[:, 1], y[:, 1], t(1))
    do.add(y[:, 7], y[:, 7], t(2))
    do.add(y[:, 3], y[:, 3], t(3))
    do.add(y[:, 5], y[:, 5], t(6))
    do.level()


def filter_stage(nc, tag, J, tri, feat_d, decay_d, fwd_d, w1_d, b1_d, w2_d, b2_d, w3_d, b3_d, freq_d, bias_d, kf_d):
    n = J * P
    with stage(nc, tag + "mlp_in", tag + "w3_in", tag + "mat_in", tag + "bias_in", tag + "dec0_in", tag + "dec1_in", tag + "mlp_mm", tag + "mlp_step", tag + "sin_done",
               tag + "w_step", tag + "eo_mm", tag + "eo_ready", tag + "fixed", tag + "squared", tag + "sq_added", tag + "norm_mm", tag + "norm_step",
               tag + "dft_step", tag + "r_ready", tag + "kept", tag + "k_mm", tag + "k_read", tag + "skip_added", tag + "k_step", tag + "stored") as (ctx, sems):
        (mlp_in, w3_in, mat_in, bias_in, dec0_in, dec1_in, mlp_mm, mlp_step, sin_done, w_step, eo_mm, eo_ready, fixed, squared, sq_added, norm_mm, norm_step,
         dft_step, r_ready, kept, k_mm, k_read, skip_added, k_step, stored) = sems
        dec_in = (dec0_in, dec1_in)
        feat = sb(nc, ctx, tag + "feat", [EMB, n])
        w1 = sb(nc, ctx, tag + "w1", [EMB, HID])
        w2 = sb(nc, ctx, tag + "w2", [HID, HID])
        vec = sb(nc, ctx, tag + "vec", [HID, 3])
        hid = sb(nc, ctx, tag + "hid", [HID + 1, 2, n])
        w3 = sb(nc, ctx, tag + "w3", [HID + 1, 2, ORDER, HYW])
        w3eo = sb(nc, ctx, tag + "w3eo", [HID + 1, 2, ORDER, HYW])
        mats = sb(nc, ctx, tag + "mats", [P, 4 * J + 2, P])
        dec = sb(nc, ctx, tag + "dec", [P, 2, HYW])
        eo = sb(nc, ctx, tag + "eo", [P, 2, J, HYW])
        sq = sb(nc, ctx, tag + "sq", [P, 2, 2, HYW])
        acc = sb(nc, ctx, tag + "acc", [P, HYW])
        rs = sb(nc, ctx, tag + "rs", [P, HYW])
        bias = sb(nc, ctx, tag + "bias", [P, ORDER, HYW])
        R = sb(nc, ctx, tag + "R", [P, J, 2, HYW])
        Tm = sb(nc, ctx, tag + "Tm", [P, 2 * J, HYW])
        pre = Tm[0:HID, 0:2 * n // HYW or 1].rearrange("p a b -> p (a b)")[:, 0:2 * n].rearrange("p (a b) -> p a b", a=2)
        keep = sb(nc, ctx, tag + "keep", [P, HYW])
        K = sb(nc, ctx, tag + "K", [P, 2 * J + 1, HYW])
        cst = sb(nc, ctx, tag + "cst", [P, 1])
        pE = ps(nc, ctx, tag + "pE", 4 * BANK)
        pN = ps(nc, ctx, tag + "pN", BANK)
        pK = ps(nc, ctx, tag + "pK", 2 * BANK)
        half = n // 2 if n > BANK else n

        with nc.Block() as block:
            @block.sync
            def _(sp):
                sp.dma_start(feat[:], feat_d).then_inc(mlp_in, 16)
                sp.dma_start(w1[:], w1_d).then_inc(mlp_in, 16)
                sp.dma_start(w2[:], w2_d).then_inc(mlp_in, 16)
                for i, v in enumerate((b1_d, b2_d, freq_d)):
                    sp.dma_start(vec[:, i:i + 1], v.rearrange("(p a) -> p a", a=1)).then_inc(mlp_in, 16)
                sp.dma_start(w3[0:HID].rearrange("p a o n -> p (a o n)"), w3_d).then_inc(w3_in, 16)
                sp.dma_start(w3[HID:HID + 1].rearrange("p a o n -> p (a o n)"), b3_d.rearrange("(a n) -> a n", a=1)).then_inc(w3_in, 16)
                sp.dma_start(mats[:], fwd_d).then_inc(mat_in, 16)
                sp.dma_start(bias[:], bias_d.partition_broadcast(P)).then_inc(bias_in, 16)
                for i in range(ORDER * J):
                    if i >= 2:
                        sp.wait_ge(eo_ready, i - 1)
                    sp.dma_start(dec[:, i % 2], decay_d[:, i % J]).then_inc(dec_in[i % 2], 16)
                for o in range(ORDER):
                    sp.wait_ge(k_step, 3 * (o + 1))
                    sp.dma_start(kf_d[o], K[:]).then_inc(stored, 16)
                sp.wait_ge(stored, 16 * ORDER)

            @block.tensor
            def _(pe):
                pe.wait_ge(mlp_in, 96)
                for c in range(0, n, half):
                    mm = pe.matmul(pE[0:HID, c:c + half], w1[:], feat[:, c:c + half], start=True, stop=True)
                mm.then_inc(mlp_mm, 1)
                pe.wait_ge(sin_done, 1)
                for c in range(0, n, half):
                    mm = pe.matmul(pE[0:HID, c:c + half], w2[:], hid[0:HID, 0, c:c + half], start=True, stop=True)
                mm.then_inc(mlp_mm, 1)
                pe.wait_ge(sin_done, 2)
                pe.wait_ge(w_step, 3)
                pe.wait_ge(mat_in, 16)
                for o in range(ORDER):
                    for j in range(J):
                        i = o * J + j
                        if i >= 2:
                            pe.wait_ge(eo_ready, i - 1)
                        for e in range(2):
                            b = (2 * (i % 2) + e) * BANK
                            mm = pe.matmul(pE[:, b:b + HYW], hid[:, 1, j * P:(j + 1) * P], w3eo[:, e, o], start=True, stop=True)
                        mm.then_inc(eo_mm, 1)
                    pe.wait_ge(sq_added, 2 * J * (o + 1))
                    pe.matmul(pN[:, 0:HYW], tri[:, 2], acc[:], start=True, stop=True).then_inc(norm_mm, 1)
                    for e in range(2):
                        pe.wait_ge(r_ready, 2 * o + e + 1)
                        if e:
                            pe.wait_ge(kept, o + 1)
                        for k in range(J):
                            i = (2 * o + e) * J + k
                            if i >= 2:
                                pe.wait_ge(k_read, i - 1)
                            out = pK[:, (i % 2) * BANK:(i % 2) * BANK + HYW]
                            if e and k == 0:
                                pe.matmul(out, mats[:, 4 * J], R[:, 0, 0], start=True, stop=False)
                                pe.matmul(out, mats[:, 4 * J + 1], keep[:], start=False, stop=False)
                            else:
                                pe.matmul(out, mats[:, 4 * k + 2 * e], R[:, k, 0], start=True, stop=False)
                            pe.matmul(out, mats[:, 4 * k + 2 * e + 1], R[:, k, 1], start=False, stop=True).then_inc(k_mm, 1)

            @block.scalar
            def _(act):
                for i in range(2):
                    act.wait_ge(mlp_step, 6 * (i + 1))
                    act.activation(hid[0:HID, i], pre[:, 0], ACT.Sin).then_inc(sin_done, 1)
                for o in range(ORDER):
                    for j in range(J):
                        i = o * J + j
                        act.wait_ge(eo_ready, i + 1)
                        if j == 0:
                            act.wait_ge(fixed, 3 * (o + 1))
                        if i >= 2:
                            act.wait_ge(sq_added, 2 * (i - 1))
                        act.activation(sq[:, i % 2], eo[:, :, j], ACT.Square).then_inc(squared, 1)
                    act.wait_ge(norm_mm, o + 1)
                    act.activation(rs[:], pN[:, 0:HYW], ACT.Ln, scale=0.5, bias=cst[:, 0:1]).then_inc(norm_step, 1)
                    act.wait_ge(norm_step, 2 * o + 1)
                    act.activation(rs[:], rs[:], ACT.Exp, scale=-0.5).then_inc(norm_step, 1)
                    act.wait_ge(r_ready, 2 * o + 1)
                    act.activation(keep[:], R[:, 0, 0], ACT.Copy).then_inc(kept, 1)

            @block.gpsimd
            def _(pool):
                def add_skip(o):
                    for k in range(J):
                        pool.wait_ge(k_read, 2 * o * J + k + 1)
                        pool.tensor_tensor(K[:, 2 * k], K[:, 2 * k], bias[:, o], ALU.add).then_inc(skip_added, 1)

                pool.wait_ge(bias_in, 16)
                for i in range(ORDER * J):
                    if i and i % J == 0:
                        add_skip(i // J - 1)
                    pool.wait_ge(squared, i + 1)
                    if i % J == 0:
                        if i:
                            pool.wait_ge(norm_mm, i // J)
                        pool.tensor_tensor(acc[:], sq[:, i % 2, 0], sq[:, i % 2, 1], ALU.add).then_inc(sq_added, 2)
                    else:
                        for e in range(2):
                            pool.wait_ge(sq_added, 2 * i + e)
                            pool.tensor_tensor(acc[:], acc[:], sq[:, i % 2, e], ALU.add).then_inc(sq_added, 1)
                add_skip(ORDER - 1)

            @block.vector
            def _(dve):
                dve.memset(cst[:], RMS_EPS)
                dve.memset(hid[HID:HID + 1, 1], 1.0).then_inc(w_step, 1)
                for i in range(2):
                    dve.wait_ge(mlp_in, 96)
                    dve.wait_ge(mlp_mm, i + 1)
                    m = 6 * i
                    dve.tensor_scalar(pre[:, 0], pE[0:HID, 0:n], vec[:, i:i + 1], vec[:, 2:3], ALU.add, ALU.mult).then_inc(mlp_step, 1)
                    dve.wait_ge(mlp_step, m + 1)
                    dve.tensor_scalar(pre[:, 1], pre[:, 0], 1.0 / (2 * math.pi), SIN_RANGE, ALU.mult, ALU.add).then_inc(mlp_step, 1)
                    dve.wait_ge(mlp_step, m + 2)
                    dve.tensor_scalar(pre[:, 1], pre[:, 1], SIN_RANGE, None, ALU.subtract).then_inc(mlp_step, 1)
                    dve.wait_ge(mlp_step, m + 3)
                    dve.scalar_tensor_tensor(pre[:, 0], pre[:, 1], -6.28125, pre[:, 0], ALU.mult, ALU.add).then_inc(mlp_step, 1)
                    dve.wait_ge(mlp_step, m + 4)
                    dve.scalar_tensor_tensor(pre[:, 0], pre[:, 1], -(2 * math.pi - 6.28125), pre[:, 0], ALU.mult, ALU.add).then_inc(mlp_step, 1)
                    dve.wait_ge(mlp_step, m + 5)
                    dve.tensor_scalar(pre[:, 0], pre[:, 0], 3.1415925, -3.1415925, ALU.min, ALU.max).then_inc(mlp_step, 1)
                    if i == 0:
                        dve.wait_ge(w3_in, 32)
                        dve.tensor_tensor(w3eo[:, 0], w3[:, 0], w3[:, 1], ALU.add).then_inc(w_step, 1)
                        dve.tensor_tensor(w3eo[:, 1], w3[:, 0], w3[:, 1], ALU.subtract).then_inc(w_step, 1)
                        dve.wait_ge(sin_done, 1)
                dve.wait_ge(bias_in, 16)
                do = Steps(dve, dft_step)
                for o in range(ORDER):
                    for j in range(J):
                        i = o * J + j
                        dve.wait_ge(dec_in[i % 2], 16 * (i // 2 + 1))
                        dve.wait_ge(eo_mm, i + 1)
                        if o:
                            dve.wait_ge(squared, o * J)
                            dve.wait_ge(r_ready, 2 * o)
                        out = eo[:, :, j]
                        b = 2 * (i % 2) * BANK
                        dve.tensor_tensor(out, pE[:, b:b + 2 * BANK].rearrange("p (e n) -> p e n", e=2),
                                          dec[:, i % 2].unsqueeze(1).to_broadcast([P, 2, HYW]), ALU.mult).then_inc(eo_ready, 1)
                        if j == 0:
                            dve.wait_ge(eo_ready, i + 1)
                            dve.tensor_tensor(eo[0:1, 0, 0], eo[0:1, 0, 0], eo[0:1, 1, 0], ALU.add).then_inc(fixed, 1)
                            dve.wait_ge(fixed, 3 * o + 1)
                            dve.tensor_scalar(eo[0:1, 1, 0], eo[0:1, 0, 0], 0.5, None, ALU.mult).then_inc(fixed, 1)
                            dve.wait_ge(fixed, 3 * o + 2)
                            dve.tensor_scalar(eo[0:1, 0, 0], eo[0:1, 0, 0], 0.5, None, ALU.mult).then_inc(fixed, 1)
                    dve.wait_ge(eo_ready, (o + 1) * J)
                    dve.wait_ge(fixed, 3 * (o + 1))
                    for e in range(2):
                        if o or e:
                            dve.wait_ge(k_mm, (2 * o + e) * J)
                            dve.wait_ge(kept, o + e)
                        butterfly(do, J, eo[:, e], R, Tm)
                        do.level()
                        dve.sem_inc(r_ready, 1)
                        if e == 0:
                            dve.wait_ge(norm_step, 2 * (o + 1))
                            if o:
                                dve.wait_ge(stored, 16 * o)
                        for k in range(J):
                            i = (2 * o + e) * J + k
                            dve.wait_ge(k_mm, i + 1)
                            dve.tensor_tensor(K[:, 2 * k + e], pK[:, (i % 2) * BANK:(i % 2) * BANK + HYW], rs[:], ALU.mult).then_inc(k_read, 1)
                    dve.wait_ge(k_read, (2 * o + 2) * J)
                    dve.wait_ge(skip_added, (o + 1) * J)
                    dve.tensor_copy(K[:, 2 * J], K[:, 0]).then_inc(k_step, 1)
                    dve.wait_ge(k_step, 3 * o + 1)
                    dve.tensor_tensor(K[0:1, 2 * J], K[0:1, 1], bias[0:1, o], ALU.add).then_inc(k_step, 1)
                    dve.wait_ge(k_step, 3 * o + 2)
                    dve.memset(K[0:1, 1], 0.0).then_inc(k_step, 1)


def hyena_stage(nc, tag, J, tok0, ident, hp_d, gate_d, kf_d, fwd_d, inv_d, o_d):
    n = J * P
    CTS = HYW // P
    with stage(nc, tag + "v_in", tag + "x1_in", tag + "x2_in", tag + "g_in", tag + "mats_in", tag + "k0_in", tag + "k1_in", tag + "turned", tag + "tok_ready",
               tag + "dft_step", tag + "r_ready", tag + "x_mm", tag + "x_read", tag + "prod_step", tag + "y_ready", tag + "q_mm", tag + "q_ready",
               tag + "z_step", tag + "gate_ready", tag + "out_ready", tag + "stored") as (ctx, sems):
        (v_in, x1_in, x2_in, g_in, mats_in, k0_in, k1_in, turned, tok_ready, dft_step, r_ready, x_mm, x_read, prod_step, y_ready, q_mm, q_ready,
         z_step, gate_ready, out_ready, stored) = sems
        fwd = sb(nc, ctx, tag + "fwd", [P, 4 * J, P])
        inv = sb(nc, ctx, tag + "inv", [P, 4 * J, P])
        u = sb(nc, ctx, tag + "u", [P, J, HYW])
        x1 = sb(nc, ctx, tag + "x1", [P, J, HYW])
        xg = sb(nc, ctx, tag + "xg", [P, CTS, n])
        R = sb(nc, ctx, tag + "R", [P, J, 2, HYW])
        Tm = sb(nc, ctx, tag + "Tm", [P, 16, HYW])
        K = sb(nc, ctx, tag + "K", [P, 2 * J + 1, HYW])
        pX = ps(nc, ctx, tag + "pX", 4 * BANK)
        pQ = ps(nc, ctx, tag + "pQ", 4 * BANK)
        x1T = Tm[:, 0:J].rearrange("p j n -> p (j n)").rearrange("p (c t) -> p c t", c=CTS)
        gT = x1[:].rearrange("p j n -> p (j n)").rearrange("p (c t) -> p c t", c=CTS)
        k_in = (k0_in, k1_in)

        def rows(first):
            return hp_d[first:first + HYW, tok0:tok0 + n].rearrange("(c p) t -> p c t", p=P)

        with nc.Block() as block:
            @block.sync
            def _(sp):
                sp.dma_start(xg[:], rows(0)).then_inc(v_in, 16)
                sp.dma_start(x1T, rows(HYW)).then_inc(x1_in, 16)
                sp.dma_start(fwd[:], fwd_d[:, 0:4 * J]).then_inc(mats_in, 16)
                sp.dma_start(K[:], kf_d[0]).then_inc(k_in[0], 16)
                sp.dma_start(inv[:], inv_d).then_inc(mats_in, 16)
                sp.wait_ge(tok_ready, 2 * J)
                sp.dma_start(xg[:], rows(2 * HYW)).then_inc(x2_in, 16)
                sp.wait_ge(y_ready, J)
                sp.dma_start(K[:], kf_d[1]).then_inc(k_in[1], 16)
                sp.wait_ge(z_step, 1)
                sp.dma_start(gT, gate_d[:, tok0:tok0 + n].rearrange("(c p) t -> p c t", p=P)).then_inc(g_in, 16)
                sp.wait_ge(out_ready, 1)
                sp.dma_start(o_d[1536:1536 + HYW, tok0:tok0 + n].rearrange("(c p) t -> p c t", p=P), xg[:]).then_inc(stored, 16)
                sp.wait_ge(stored, 16)

            @block.tensor
            def _(pe):
                pe.wait_ge(v_in, 16)
                for src, first in ((xg, 0), (x1T, J)):
                    if first:
                        pe.wait_ge(x1_in, 16)
                    for j in range(J):
                        i = first + j
                        if i >= 2:
                            pe.wait_ge(tok_ready, i - 1)
                        for ct in range(CTS):
                            b = (i % 2) * BANK + ct * P
                            mm = pe.transpose(pX[:, b:b + P], src[:, ct, j * P:(j + 1) * P], ident[:, :])
                        mm.then_inc(turned, 1)
                pe.wait_ge(mats_in, 32)

                def forward(i):
                    o, k = divmod(i, J)
                    if k == 0:
                        pe.wait_ge(r_ready, o + 1)
                        pe.wait_ge(tok_ready, 2 * J)
                    if i >= 2:
                        pe.wait_ge(x_read, 2 * (i - 1))
                    b = 2 * (i % 2) * BANK
                    for part in range(2):
                        out = pX[:, b + part * BANK:b + part * BANK + HYW]
                        pe.matmul(out, fwd[:, 4 * k + 2 * part], R[:, k, 0], start=True, stop=False)
                        mm = pe.matmul(out, fwd[:, 4 * k + 2 * part + 1], R[:, k, 1], start=False, stop=True)
                    mm.then_inc(x_mm, 1)

                def backward(i):
                    o, k = divmod(i, J)
                    pe.wait_ge(y_ready, i + 1)
                    if i >= 2:
                        pe.wait_ge(q_ready, i - 1)
                    b = 2 * (i % 2) * BANK
                    for part in range(2):
                        at = b + part * BANK
                        m1, m2 = inv[:, 4 * k + 2 * part], inv[:, 4 * k + 2 * part + 1]
                        if o == 0:
                            pe.matmul(pQ[:, at:at + HYW], m1, R[:, k, 0], start=True, stop=False)
                            mm = pe.matmul(pQ[:, at:at + HYW], m2, R[:, k, 1], start=False, stop=True)
                        else:
                            for ct in range(CTS):
                                out = pQ[:, at + ct * P:at + (ct + 1) * P]
                                pe.matmul(out, R[:, k, 0, ct * P:(ct + 1) * P], m1, start=True, stop=False)
                                mm = pe.matmul(out, R[:, k, 1, ct * P:(ct + 1) * P], m2, start=False, stop=True)
                    mm.then_inc(q_mm, 1)

                for o in range(ORDER):
                    for k in range(J + 1):
                        if k < J:
                            forward(o * J + k)
                        if k >= 1:
                            backward(o * J + k - 1)

            @block.scalar
            def _(act):
                for i in range(2 * J):
                    act.wait_ge(turned, i + 1)
                    dst = u[:, i] if i < J else x1[:, i - J]
                    act.activation(dst, pX[:, (i % 2) * BANK:(i % 2) * BANK + HYW], ACT.Copy).then_inc(tok_ready, 1)
                for i in range(ORDER * J):
                    act.wait_ge(q_mm, i + 1)
                    b = 2 * (i % 2) * BANK
                    act.activation(R[:, i % J].rearrange("p a n -> p (a n)"), pQ[:, b:b + 2 * BANK], ACT.Copy).then_inc(q_ready, 1)

            @block.gpsimd
            def _(pool):
                pool.wait_ge(x2_in, 16)
                pool.wait_ge(g_in, 16)
                pool.tensor_tensor(xg[:], xg[:], gT, ALU.mult).then_inc(gate_ready, 1)

            @block.vector
            def _(dve):
                do = Steps(dve, dft_step)
                dve.wait_ge(tok_ready, 2 * J)
                for o in range(ORDER):
                    butterfly(do, J, u[:], R, Tm)
                    do.level()
                    dve.sem_inc(r_ready, 1)
                    dve.wait_ge(k_in[o], 16)
                    for k in range(J):
                        i = o * J + k
                        t = Tm[:, 4 * (i % 2):4 * (i % 2) + 4]
                        x = pX[:, 2 * (i % 2) * BANK:2 * (i % 2 + 1) * BANK].rearrange("p (a n) -> p a n", a=2)
                        kr, ki = K[:, 2 * k], K[:, 2 * k + 1]
                        dve.wait_ge(x_mm, i + 1)
                        if i >= 2:
                            dve.wait_ge(y_ready, i - 1)
                        if k == 0:
                            dve.tensor_tensor(t[:, 0], x[:, 0], kr, ALU.mult).then_inc(prod_step, 1)
                            dve.tensor_tensor(t[:, 1], x[:, 1], K[:, 2 * J], ALU.mult).then_inc(prod_step, 1)
                        else:
                            dve.tensor_tensor(t[:, 0:2], x, kr.unsqueeze(1).to_broadcast([P, 2, HYW]), ALU.mult).then_inc(prod_step, 2)
                        dve.tensor_tensor(t[:, 2:4], x, ki.unsqueeze(1).to_broadcast([P, 2, HYW]), ALU.mult).then_inc(x_read, 2)
                        dve.wait_ge(prod_step, 3 * i + 2)
                        dve.wait_ge(x_read, 2 * i + 2)
                        dve.tensor_tensor(R[:, k, 0], t[:, 0], t[:, 3], ALU.subtract).then_inc(prod_step, 1)
                        dve.tensor_tensor(R[:, k, 1], t[:, 1], t[:, 2], ALU.add).then_inc(y_ready, 1)
                    dve.wait_ge(prod_step, 3 * (o + 1) * J)
                    dve.wait_ge(y_ready, (o + 1) * J)
                    dve.wait_ge(q_ready, (o + 1) * J)
                    butterfly_back(do, J, R, Tm, u)
                    if o == 0:
                        dve.tensor_tensor(u[:], u[:], x1[:], ALU.mult).then_inc(z_step, 1)
                        dve.wait_ge(z_step, 1)
                    else:
                        dve.wait_ge(gate_ready, 1)
                        x4 = xg[:].rearrange("p c (j q) -> p j c q", q=P)
                        dve.tensor_tensor(x4, x4, u[:].rearrange("p j (c q) -> p j c q", q=P), ALU.mult).then_inc(out_ready, 1)


def output_stage(nc, tag, first_tile, tri, o_d, w_out, norm_w, mod_d, ln_g, ln_b, h_lat, h_ctx, dst_lat, dst_ctx):
    tiles = list(range(first_tile, TT))
    NT = len(tiles)
    with stage(nc, tag + "w0_in", tag + "w1_in", tag + "w2_in", tag + "nw_in", tag + "vec_in", tag + "o_in", tag + "h_in", tag + "w_rounded", tag + "w_split", tag + "o_rounded", tag + "o_split", tag + "squared",
               tag + "sq_mm", tag + "out_mm", tag + "ms_ready", tag + "rms_ready", tag + "a_read", tag + "b_read", tag + "h_read", tag + "step",
               tag + "var_ready", tag + "std_ready", tag + "done", tag + "stored0", tag + "stored1") as (ctx, sems):
        (w0_in, w1_in, w2_in, nw_in, vec_in, o_in, h_in, w_rounded, w_split, o_rounded, o_split, squared, sq_mm, out_mm, ms_ready, rms_ready, a_read, b_read, h_read, step,
         var_ready, std_ready, done, stored0, stored1) = sems
        stored = (stored0, stored1)
        w_in = (w0_in, w1_in, w2_in)
        WS = len(w_in)
        w_hi = sb(nc, ctx, tag + "w_hi", [P, KM, D], F32R)
        w_lo = sb(nc, ctx, tag + "w_lo", [P, KM, D], F32R)
        rows = sb(nc, ctx, tag + "rows", [P, WS, D])
        r, h = rows[:, 0:2], rows[:, 2]
        nw = sb(nc, ctx, tag + "nw", [P, SSD_TILES])
        oT = sb(nc, ctx, tag + "oT", [P, KM, P])
        o_hi = sb(nc, ctx, tag + "o_hi", [P, 2, KM, P], F32R)
        o_lo = sb(nc, ctx, tag + "o_lo", [P, 2, KM, P], F32R)
        sq = sb(nc, ctx, tag + "sq", [P, SSD_TILES, P])
        gate = sb(nc, ctx, tag + "gate", [P, 2, D])
        gb = sb(nc, ctx, tag + "gb", [P, 2, D])
        st = sb(nc, ctx, tag + "st", [P, 2, 6])
        mv = sb(nc, ctx, tag + "mv", [P, 8])
        pA = ps(nc, ctx, tag + "pA", 2 * BANK)
        pB = ps(nc, ctx, tag + "pB", 2 * BANK)
        pR = ps(nc, ctx, tag + "pR", BANK)

        with nc.Block() as block:
            @block.sync
            def _(sp):
                def load_o(i):
                    t = tiles[i]
                    sp.dma_start(oT[:], o_d[:, t * P:(t + 1) * P].rearrange("(k p) t -> p k t", p=P)).then_inc(o_in, 16)

                def load_h(i):
                    t = tiles[i]
                    src = h_ctx[t * P:(t + 1) * P] if t < CT else h_lat[(t - CT) * P:(t - CT + 1) * P]
                    sp.dma_start(h, src).then_inc(h_in, 16)

                with nc.allow_non_contiguous_dma(reason="a vector onto the partitions"):
                    sp.dma_start(nw[:], norm_w.rearrange("(k p) -> p k", p=P)).then_inc(nw_in, 16)
                for k in range(KM):
                    if k >= WS:
                        sp.wait_ge(w_split, k - WS + 1)
                    sp.dma_start(rows[:, k % WS], w_out[k * P:(k + 1) * P]).then_inc(w_in[k % WS], 16)
                    if k == 0:
                        load_o(0)
                for i in range(2):
                    sp.dma_start(gate[:, i], mod_d[i].partition_broadcast(P)).then_inc(vec_in, 16)
                sp.dma_start(gb[:, 0], ln_g.partition_broadcast(P)).then_inc(vec_in, 16)
                sp.dma_start(gb[:, 1], ln_b.partition_broadcast(P)).then_inc(vec_in, 16)
                for i in range(NT):
                    if i:
                        sp.wait_ge(o_split, i)
                        load_o(i)
                        sp.wait_ge(h_read, i)
                    else:
                        sp.wait_ge(w_split, KM)
                    load_h(i)

            @block.tensor
            def _(pe):
                for i in range(NT):
                    s = i % 2
                    pe.wait_ge(squared, i + 1)
                    if i:
                        pe.wait_ge(ms_ready, i)
                    for k in range(SSD_TILES):
                        mm = pe.matmul(pR[:, 0:1], sq[:, k], tri[:, 2, 0:1], start=(k == 0), stop=(k == SSD_TILES - 1))
                    mm.then_inc(sq_mm, 1)
                    pe.wait_ge(o_split, i + 1)
                    if i:
                        pe.wait_ge(a_read, i)
                    for acc, first, last in ((pA, 0, SSD_TILES), (pB, SSD_TILES, KM)):
                        if first and i:
                            pe.wait_ge(b_read, i)
                        for k in range(first, last):
                            if i == 0:
                                pe.wait_ge(w_split, k + 1)
                            for n, (op, wp) in enumerate(PASSES):
                                for c in range(0, D, BANK):
                                    mm = pe.matmul(acc[:, c:c + BANK], (o_hi, o_lo)[op][:, s, k], (w_hi, w_lo)[wp][:, k, c:c + BANK],
                                                   start=(k == first and n == 0), stop=(k == last - 1 and n == 2))
                        mm.then_inc(out_mm, 1)

            @block.scalar
            def _(act):
                def ln_std(i):
                    act.wait_ge(var_ready, i + 1)
                    act.activation(mv[:, 6:7], mv[:, 5:6], ACT.Sqrt).then_inc(std_ready, 1)

                def store(i):
                    t = tiles[i]
                    dst = dst_ctx[t * P:(t + 1) * P] if t < CT else dst_lat[(t - CT) * P:(t - CT + 1) * P]
                    act.wait_ge(done, i + 1)
                    act.dma_start(dst, r[:, i % 2]).then_inc(stored[i % 2], 16)

                def square(i):
                    act.wait_ge(o_in, 16 * (i + 1))
                    if i:
                        act.wait_ge(sq_mm, i)
                    act.activation(sq[:], oT[:, 0:SSD_TILES], ACT.Square).then_inc(squared, 1)
                    if i >= 2:
                        act.wait_ge(out_mm, 2 * (i - 1))
                    act.activation(o_hi[:, i % 2], oT[:], ACT.Copy).then_inc(o_rounded, 1)

                act.wait_ge(nw_in, 16)
                for k in range(KM):
                    act.wait_ge(w_in[k % WS], 16 * (k // WS + 1))
                    act.activation(w_hi[:, k], rows[:, k % WS], ACT.Copy, scale=nw[:, k:k + 1] if k < SSD_TILES else 1.0).then_inc(w_rounded, 1)
                    if k == 1:
                        square(0)
                for i in range(NT):
                    act.wait_ge(ms_ready, i + 1)
                    act.activation(mv[:, 1:2], mv[:, 0:1], ACT.Sqrt).then_inc(rms_ready, 1)
                    if i + 1 < NT:
                        square(i + 1)
                    ln_std(i)
                    store(i)
                for s in range(2):
                    act.wait_ge(stored[s], 16 * (NT // 2))

            @block.vector
            def _(dve):
                def split(i):
                    dve.wait_ge(squared, i + 1)
                    dve.wait_ge(o_rounded, i + 1)
                    dve.tensor_tensor(o_lo[:, i % 2], oT[:], o_hi[:, i % 2], ALU.subtract).then_inc(o_split, 1)

                dve.wait_ge(nw_in, 16)
                for k in range(KM):
                    dve.wait_ge(w_rounded, k + 1)
                    raw = rows[:, k % WS]
                    if k < SSD_TILES:
                        dve.scalar_tensor_tensor(w_lo[:, k], raw, nw[:, k:k + 1], w_hi[:, k], ALU.mult, ALU.subtract).then_inc(w_split, 1)
                    else:
                        dve.tensor_tensor(w_lo[:, k], raw, w_hi[:, k], ALU.subtract).then_inc(w_split, 1)
                    if k == 1:
                        split(0)
                dve.wait_ge(vec_in, 64)
                n = 0
                for i, t in enumerate(tiles):
                    s = i % 2
                    dve.wait_ge(sq_mm, i + 1)
                    dve.tensor_scalar(mv[:, 0:1], pR[:, 0:1], 1.0 / (SSD_TILES * P), RMS_EPS, ALU.mult, ALU.add).then_inc(ms_ready, 1)
                    dve.wait_ge(rms_ready, i + 1)
                    dve.reciprocal(mv[:, 2:3], mv[:, 1:2]).then_inc(step, 1)
                    dve.wait_ge(step, n + 1)
                    dve.wait_ge(out_mm, 2 * i + 1)
                    if i >= 2:
                        dve.wait_ge(stored[s], 16 * (i // 2))
                    dve.tensor_scalar(r[:, s], pA[:, :], mv[:, 2:3], None, ALU.mult).then_inc(a_read, 1)
                    if i + 1 < NT:
                        split(i + 1)
                    dve.wait_ge(a_read, i + 1)
                    dve.wait_ge(out_mm, 2 * i + 2)
                    dve.tensor_tensor(r[:, s], r[:, s], pB[:, :], ALU.add).then_inc(b_read, 1)
                    dve.wait_ge(b_read, i + 1)
                    dve.tensor_tensor(r[:, s], r[:, s], gate[:, (t >= CT) * 1], ALU.mult).then_inc(step, 1)
                    dve.wait_ge(step, n + 2)
                    dve.wait_ge(h_in, 16 * (i + 1))
                    dve.scalar_tensor_tensor(r[:, s], h, ALPHA, r[:, s], ALU.mult, ALU.add).then_inc(h_read, 1)
                    dve.wait_ge(h_read, i + 1)
                    for c in range(2):
                        dve.bn_stats(st[:, c], r[:, s, c * BANK:(c + 1) * BANK]).then_inc(step, 1)
                    dve.wait_ge(step, n + 4)
                    dve.bn_aggr(mv[:, 3:5], st[:]).then_inc(step, 1)
                    dve.wait_ge(step, n + 5)
                    dve.tensor_scalar(mv[:, 5:6], mv[:, 4:5], LN_EPS, None, ALU.add).then_inc(var_ready, 1)
                    dve.wait_ge(std_ready, i + 1)
                    dve.reciprocal(mv[:, 7:8], mv[:, 6:7]).then_inc(step, 1)
                    dve.wait_ge(step, n + 6)
                    dve.tensor_scalar(r[:, s], r[:, s], mv[:, 3:4], mv[:, 7:8], ALU.subtract, ALU.mult).then_inc(step, 1)
                    dve.wait_ge(step, n + 7)
                    dve.tensor_tensor(r[:, s], r[:, s], gb[:, 0], ALU.mult).then_inc(step, 1)
                    dve.wait_ge(step, n + 8)
                    dve.tensor_tensor(r[:, s], r[:, s], gb[:, 1], ALU.add).then_inc(done, 1)
                    n += 8


def hybrid_backbone(nc, a, out):
    def dram(name, shape):
        return nc.dram_tensor(name, list(shape), F32, kind="Internal").ap()

    h_d = dram("h_d", [T, D])
    mod_d = dram("mod_d", [2, D])
    gate_z = dram("gate_z", [1024, T])
    xbc_d = dram("xbc_d", [2048, T])
    qk_d = dram("qk_d", [1024, T])
    v_d = dram("v_d", [T, HYW])
    gate_d = dram("gate_d", [512, T])
    hp_d = dram("hp_d", [1536, T])
    gate_h = dram("gate_h", [512, T])
    la_d = dram("la_d", [2 * HEADS, T])
    o_d = dram("o_d", [D_MIX, T])
    KF = {J: dram("kf%d_d" % J, [ORDER, P, 2 * J + 1, HYW]) for J in (CT, LAT // P)}

    with ExitStack() as ctx:
        ident = sb(nc, ctx, "ident", [P, P])
        swap = sb(nc, ctx, "swap", [P, P])
        tri = sb(nc, ctx, "tri", [P, 3, P])
        small = sb(nc, ctx, "small", [P, 4, TT, 2 * HEADS])
        with stage(nc, "const_in") as (_, (const_in,)):
            with nc.Block() as block:
                @block.sync
                def _(sp):
                    sp.dma_start(ident[:], a["c_ident"]).then_inc(const_in, 16)
                    sp.dma_start(swap[:], a["c_swap"]).then_inc(const_in, 16)
                    sp.dma_start(tri[:], a["c_tri"]).then_inc(const_in, 16)
                    sp.wait_ge(const_in, 48)

        for layer in range(DEPTH):
            need_ctx = layer < DEPTH - 1
            t0 = 0 if need_ctx else CTX
            g = "l%d_" % layer
            h_lat, h_ctx = (a["x"][0], a["ctx"][0]) if layer == 0 else (h_d[CTX:T], h_d[0:CTX])
            with ExitStack() as uctx:
                u_hi = sb(nc, uctx, g + "u_hi", [P, KD, T], F32R)
                u_lo = sb(nc, uctx, g + "u_lo", [P, KD, T], F32R)
                norm_stage(nc, g + "n_", u_hi, u_lo, ident, h_lat, h_ctx, a["c"], a["c_ctx"], a["w_ada"][layer], a["b_ada"][layer], mod_d)
                v_dt_stage(nc, g + "v_", u_hi, u_lo, a["w_in"][layer], tri, ident, a["ssd_dt_bias"][layer], a["ssd_a_log"][layer], v_d, la_d, small)
                project_stage(nc, g + "p_", u_hi, u_lo, a["w_in"][layer],
                              [("rope", Q0, 1, t0, qk_d[0:512], None), ("rope", K0, 1, 0, qk_d[512:1024], None),
                               ("gate", GD0, 1, t0, gate_d, None), ("gate", Z0, 2, t0, gate_z, None), ("gate", GH0, 1, t0, gate_h, None),
                               ("conv_silu", XBC0, 4, 0, xbc_d, 0), ("conv", HP0, 3, t0, hp_d, a["ssd_conv_b"].shape[1] // P)],
                              [(a["ssd_conv_w"][layer], a["ssd_conv_b"][layer]), (a["hy_conv_w"][layer], a["hy_conv_b"][layer])],
                              swap, a["c_cos"], a["c_sin"])
            attention_stage(nc, g + "at_", layer, t0 // P, ident, tri, a["diff_lambda"][layer], qk_d, v_d, gate_d, o_d)
            ssd_stage(nc, g + "sd_", t0 // P, tri, ident, small, a["ssd_d"][layer], xbc_d, la_d, gate_z, o_d)
            for J, name, tok0, cols in ((LAT // P, "lat", CTX, slice(CTX, T)), (CT, "ctx", 0, slice(0, CTX))):
                if J == CT and not need_ctx:
                    continue
                first = tok0 // P
                filter_stage(nc, g + name + "f_", J, tri, a["c_feat"][:, cols], a["c_decay"][:, first:first + J], a["c_fwd_" + name],
                             a["hy_w1"][layer], a["hy_b1"][layer], a["hy_w2"][layer], a["hy_b2"][layer], a["hy_w3"][layer], a["hy_b3"][layer],
                             a["hy_freq"][layer], a["hy_bias"][layer], KF[J])
                hyena_stage(nc, g + name + "h_", J, tok0, ident, hp_d, gate_h, KF[J], a["c_fwd_" + name], a["c_inv_" + name], o_d)
            dst = h_d[CTX:T] if need_ctx else out[0]
            output_stage(nc, g + "o_", t0 // P, tri, o_d, a["w_out"][layer], a["ssd_norm_w"][layer], mod_d, a["ln_g"][layer], a["ln_b"][layer],
                         h_lat, h_ctx, dst, h_d[0:CTX])


INPUTS = ["x", "c", "ctx", "c_ctx", "w_ada", "b_ada", "w_in", "ssd_conv_w", "ssd_conv_b", "ssd_dt_bias", "ssd_a_log", "ssd_d",
          "ssd_norm_w", "diff_lambda", "hy_conv_w", "hy_conv_b", "hy_w1", "hy_b1", "hy_w2", "hy_b2", "hy_w3", "hy_b3",
          "hy_freq", "hy_bias", "w_out", "ln_g", "ln_b"]


def kernel(**inputs):
    import concourse.bacc as bacc
    from concourse.bass_utils import run_bass_kernel_spmd

    nc = bacc.Bacc("TRN2", target_bir_lowering=False, num_devices=1)
    arrays = {name: np.ascontiguousarray(inputs[name]) for name in INPUTS}
    arrays.update(constants())
    a = {name: nc.dram_tensor(name, list(v.shape), mybir.dt.from_np(v.dtype), kind="ExternalInput").ap() for name, v in arrays.items()}
    out = nc.dram_tensor("out", [1, LAT, D], F32, kind="ExternalOutput").ap()
    hybrid_backbone(nc, a, out)
    result = run_bass_kernel_spmd(nc, [arrays], core_ids=[0])
    return result.results[0]["out"]
```
